# Optimizing a Trainium2 kernel written in Bass

```python
import math
import jax, jax.numpy as jnp
from jax import lax
import numpy as np

D_MODEL = 1024
BATCH = 1
SEQ = 512
DEPTH = 1
DEC_BATCH = 1
DEC_SEQ = 64
PAST_LEN = 512

CHUNK = 64
Q_BLOCK = 128
RMS_EPS = 1e-6
SUBLN_EPS = 1e-5
ROPE_THETA = 10000.0
DA_HEADS = 8
DA_DK = 64
DA_DV = 2 * DA_DK
DA_QK_WIDTH = DA_HEADS * 2 * DA_DK
DA_V_WIDTH = DA_HEADS * DA_DV
RG_WIDTH = D_MODEL
RG_BLOCKS = 16
RG_BW = RG_WIDTH // RG_BLOCKS
RG_C = 8.0
CONV_W = 4
N_BRANCH = 2
IN_COLS = 2 * DA_QK_WIDTH + DA_V_WIDTH + 2 * RG_WIDTH + N_BRANCH * D_MODEL
SPLIT_AT = (DA_QK_WIDTH, 2 * DA_QK_WIDTH, 2 * DA_QK_WIDTH + DA_V_WIDTH,
            2 * DA_QK_WIDTH + DA_V_WIDTH + RG_WIDTH, 2 * DA_QK_WIDTH + DA_V_WIDTH + 2 * RG_WIDTH)
MEM_LEN = 256
CA_HEADS = 4
CA_DH = D_MODEL // CA_HEADS
PK_HEADS = 8
PK_DQ = 256
PK_DHALF = PK_DQ // 2
PK_NKEYS = 128
PK_EXPERTS = PK_NKEYS * PK_NKEYS
PK_TOPK = 16
PEER_BLOCK = 256

kernel_name = "hybrid_diffattn_rglru_peer_stream_step"

def rmsnorm(x, g, eps=RMS_EPS):
    xf = x.astype(jnp.float32)
    y = xf * lax.rsqrt(jnp.mean(xf * xf, axis=-1, keepdims=True) + eps)
    return (y * g.astype(jnp.float32)).astype(x.dtype)

def rope(x, pos):
    d = x.shape[-1]
    half = d // 2
    inv = jnp.exp(-math.log(ROPE_THETA) * jnp.arange(half, dtype=jnp.float32) * (2.0 / d))
    ang = pos.astype(jnp.float32)[:, None] * inv[None, :]
    cos = jnp.cos(ang)[None, :, None, :]
    sin = jnp.sin(ang)[None, :, None, :]
    xf = x.astype(jnp.float32)
    x1, x2 = xf[..., :half], xf[..., half:]
    return jnp.concatenate([x1 * cos - x2 * sin, x2 * cos + x1 * sin], axis=-1).astype(x.dtype)

def diff_attention(q, k, v, q_pos, k_pos, lam, g_subln, lam_init):
    b, lq = q.shape[0], q.shape[1]
    vf = v.astype(jnp.float32)
    kchunk = k_pos // CHUNK

    def block(qb, qpos):
        nq = qb.shape[1]
        s = jnp.einsum('bqhd,bkhd->bhqk', qb, k).astype(jnp.float32) * (DA_DK ** -0.5)
        mask = kchunk[None, :] <= (qpos // CHUNK)[:, None]
        s = jnp.where(mask[None, None], s, -jnp.inf)
        p = jax.nn.softmax(s, axis=-1).reshape(b, DA_HEADS, 2, nq, s.shape[-1])
        a = p[:, :, 0] - lam * p[:, :, 1]
        o = jnp.einsum('bhqk,bkhd->bqhd', a, vf)
        o = o * lax.rsqrt(jnp.mean(o * o, axis=-1, keepdims=True) + SUBLN_EPS)
        o = o * g_subln.astype(jnp.float32) * (1.0 - lam_init)
        return o.reshape(b, nq, DA_V_WIDTH).astype(v.dtype)

    if lq > Q_BLOCK and lq % Q_BLOCK == 0:
        nb = lq // Q_BLOCK
        qb = q.reshape(b, nb, Q_BLOCK, 2 * DA_HEADS, DA_DK).transpose(1, 0, 2, 3, 4)
        pb = q_pos.reshape(nb, Q_BLOCK)
        out = lax.map(lambda qp: block(qp[0], qp[1]), (qb, pb))
        return out.transpose(1, 0, 2, 3).reshape(b, lq, DA_V_WIDTH)
    return block(q, q_pos)

def _lin_combine(e1, e2):
    a1, b1 = e1
    a2, b2 = e2
    return a1 * a2, a2 * b1 + b2

def rglru_branch(xr, conv_buf, h0, conv_w, conv_b, wa, ba, wx, bx, lam):
    b, l, w = xr.shape
    xp = jnp.concatenate([conv_buf.astype(xr.dtype), xr], axis=1)
    c = conv_b[None, None, :] + conv_w[0][None, None, :] * xp[:, 0:l]
    for j in range(1, CONV_W):
        c = c + conv_w[j][None, None, :] * xp[:, j:j + l]
    new_buf = xp[:, l:]
    cb = c.reshape(b, l, RG_BLOCKS, RG_BW)
    r = jax.nn.sigmoid((jnp.einsum('blnc,ncd->blnd', cb, wa).reshape(b, l, w) + ba).astype(jnp.float32))
    i = jax.nn.sigmoid((jnp.einsum('blnc,ncd->blnd', cb, wx).reshape(b, l, w) + bx).astype(jnp.float32))
    log_a = -RG_C * r * jax.nn.softplus(-lam.astype(jnp.float32))
    a = jnp.exp(log_a)
    u = jnp.sqrt(-jnp.expm1(2.0 * log_a)) * i * c.astype(jnp.float32)
    a_cum, u_cum = lax.associative_scan(_lin_combine, (a, u), axis=1)
    h = a_cum * h0.astype(jnp.float32)[:, None, :] + u_cum
    return h.astype(xr.dtype), h[:, -1].astype(xr.dtype), new_buf

def memory_kv(mem, g_mem, w_ck, w_cv):
    b, m, _ = mem.shape
    mn = rmsnorm(mem, g_mem)
    return (mn @ w_ck).reshape(b, m, CA_HEADS, CA_DH), (mn @ w_cv).reshape(b, m, CA_HEADS, CA_DH)

def cross_attention(xn, mem_k, mem_v, w_cq, w_co):
    b, l, d = xn.shape
    q = (xn @ w_cq).reshape(b, l, CA_HEADS, CA_DH)
    s = jnp.einsum('blhd,bmhd->bhlm', q, mem_k).astype(jnp.float32) * (CA_DH ** -0.5)
    p = jax.nn.softmax(s, axis=-1)
    o = jnp.einsum('bhlm,bmhd->blhd', p, mem_v.astype(jnp.float32)).reshape(b, l, d).astype(xn.dtype)
    return o @ w_co

def peer(xn, w_pq, keys1, keys2, u_tab, v_tab):
    b, l, d = xn.shape
    t = b * l
    pad = (-t) % PEER_BLOCK
    xb = jnp.pad(xn.reshape(t, d), ((0, pad), (0, 0))).reshape(-1, PEER_BLOCK, d)
    k1 = keys1.astype(jnp.float32)
    k2 = keys2.astype(jnp.float32)

    def block(xt):
        q = (xt @ w_pq).astype(jnp.float32).reshape(PEER_BLOCK, PK_HEADS, 2, PK_DHALF)
        s1 = jnp.einsum('thd,hnd->thn', q[:, :, 0], k1)
        s2 = jnp.einsum('thd,hnd->thn', q[:, :, 1], k2)
        t1, i1 = lax.top_k(s1, PK_TOPK)
        t2, i2 = lax.top_k(s2, PK_TOPK)
        cand = (t1[..., :, None] + t2[..., None, :]).reshape(PEER_BLOCK, PK_HEADS, PK_TOPK * PK_TOPK)
        ts, ci = lax.top_k(cand, PK_TOPK)
        e = (jnp.take_along_axis(i1, ci // PK_TOPK, axis=-1) * PK_NKEYS
             + jnp.take_along_axis(i2, ci % PK_TOPK, axis=-1))
        g = jax.nn.softmax(ts, axis=-1)
        ue = u_tab[e]
        ve = v_tab[e]
        act = jax.nn.gelu(jnp.einsum('td,thkd->thk', xt, ue).astype(jnp.float32), approximate=False)
        return jnp.einsum('thk,thkd->td', (g * act).astype(ve.dtype), ve)

    out = lax.map(block, xb).reshape(-1, d)[:t]
    return out.reshape(b, l, d).astype(xn.dtype)

def layer(x, pos, k_past, v_past, conv_buf, h0, mem_k, mem_v, params, lam_init):
    (g_mix, w_in, lam_q1, lam_k1, lam_q2, lam_k2, g_subln, conv_w, conv_b, rg_wa, rg_ba,
     rg_wx, rg_bx, rg_lambda, w_out, g_cross, w_cq, w_co, g_ffn, w_pq, pk_keys1, pk_keys2,
     peer_u, peer_v) = params
    b, l, d = x.shape
    n = rmsnorm(x, g_mix)
    z = n @ w_in
    q, k, v, rx, rg, gates = jnp.split(z, SPLIT_AT, axis=-1)
    q = rope(q.reshape(b, l, 2 * DA_HEADS, DA_DK), pos)
    k = rope(k.reshape(b, l, 2 * DA_HEADS, DA_DK), pos)
    v = v.reshape(b, l, DA_HEADS, DA_DV)
    k_all = jnp.concatenate([k_past.astype(k.dtype), k], axis=1)
    v_all = jnp.concatenate([v_past.astype(v.dtype), v], axis=1)
    k_pos = jnp.concatenate([jnp.arange(k_past.shape[1], dtype=jnp.int32), pos])
    lam = (jnp.exp(jnp.sum(lam_q1.astype(jnp.float32) * lam_k1.astype(jnp.float32)))
           - jnp.exp(jnp.sum(lam_q2.astype(jnp.float32) * lam_k2.astype(jnp.float32))) + lam_init)
    y_att = diff_attention(q, k_all, v_all, pos, k_pos, lam, g_subln, lam_init)
    h, h_last, new_buf = rglru_branch(rx, conv_buf, h0, conv_w, conv_b, rg_wa, rg_ba, rg_wx, rg_bx, rg_lambda)
    y_rec = jax.nn.gelu(rg, approximate=False) * h
    gs = jax.nn.sigmoid(gates.astype(jnp.float32)).reshape(b, l, N_BRANCH, d)
    merged = (gs[:, :, 0] * y_att.astype(jnp.float32) + gs[:, :, 1] * y_rec.astype(jnp.float32)).astype(x.dtype)
    x = x + merged @ w_out
    x = x + cross_attention(rmsnorm(x, g_cross), mem_k, mem_v, w_cq, w_co)
    x = x + peer(rmsnorm(x, g_ffn), w_pq, pk_keys1, pk_keys2, peer_u, peer_v)
    return x, k, v, new_buf, h_last

def setup_inputs(seed: int = 0) -> dict:
    key = jax.random.key(seed)
    ks = iter(jax.random.split(key, 48))
    f32 = jnp.float32

    def nrm(shape, scale):
        return jax.random.normal(next(ks), shape, f32) * scale

    def gain(shape):
        return 1.0 + 0.05 * jax.random.normal(next(ks), shape, f32)

    aq = jax.random.uniform(next(ks), (DEPTH, RG_WIDTH), f32, minval=0.9, maxval=0.999)
    a_base = aq ** (1.0 / RG_C)
    rg_lambda = jnp.log(a_base) - jnp.log1p(-a_base)
    return {
        'x_prompt': nrm((BATCH, SEQ, D_MODEL), 1.0),
        'x_sample': nrm((DEC_BATCH, DEC_SEQ, D_MODEL), 1.0),
        'cache_attn_k': nrm((DEPTH, DEC_BATCH, PAST_LEN, 2 * DA_HEADS, DA_DK), 1.0),
        'cache_attn_v': nrm((DEPTH, DEC_BATCH, PAST_LEN, DA_HEADS, DA_DV), 1.0),
        'cache_mem_k': nrm((DEPTH, DEC_BATCH, MEM_LEN, CA_HEADS, CA_DH), 1.0),
        'cache_mem_v': nrm((DEPTH, DEC_BATCH, MEM_LEN, CA_HEADS, CA_DH), 1.0),
        'state_conv': nrm((DEPTH, DEC_BATCH, CONV_W - 1, RG_WIDTH), 1.0),
        'state_rglru': nrm((DEPTH, DEC_BATCH, RG_WIDTH), 0.5),
        'mem_prompt': nrm((BATCH, MEM_LEN, D_MODEL), 1.0),
        'g_mix': gain((DEPTH, D_MODEL)),
        'w_in': nrm((DEPTH, D_MODEL, IN_COLS), D_MODEL ** -0.5),
        'lam_q1': nrm((DEPTH, DA_DK), 0.1),
        'lam_k1': nrm((DEPTH, DA_DK), 0.1),
        'lam_q2': nrm((DEPTH, DA_DK), 0.1),
        'lam_k2': nrm((DEPTH, DA_DK), 0.1),
        'g_subln': gain((DEPTH, DA_DV)),
        'conv_w': nrm((DEPTH, CONV_W, RG_WIDTH), CONV_W ** -0.5),
        'conv_b': nrm((DEPTH, RG_WIDTH), 0.02),
        'rg_wa': nrm((DEPTH, RG_BLOCKS, RG_BW, RG_BW), RG_BW ** -0.5),
        'rg_ba': nrm((DEPTH, RG_WIDTH), 0.02),
        'rg_wx': nrm((DEPTH, RG_BLOCKS, RG_BW, RG_BW), RG_BW ** -0.5),
        'rg_bx': nrm((DEPTH, RG_WIDTH), 0.02),
        'rg_lambda': rg_lambda,
        'w_out': nrm((DEPTH, D_MODEL, D_MODEL), D_MODEL ** -0.5),
        'g_cross': gain((DEPTH, D_MODEL)),
        'g_mem': gain((DEPTH, D_MODEL)),
        'w_cq': nrm((DEPTH, D_MODEL, D_MODEL), D_MODEL ** -0.5),
        'w_ck': nrm((DEPTH, D_MODEL, D_MODEL), D_MODEL ** -0.5),
        'w_cv': nrm((DEPTH, D_MODEL, D_MODEL), D_MODEL ** -0.5),
        'w_co': nrm((DEPTH, D_MODEL, D_MODEL), D_MODEL ** -0.5),
        'g_ffn': gain((DEPTH, D_MODEL)),
        'w_pq': nrm((DEPTH, D_MODEL, PK_HEADS * PK_DQ), D_MODEL ** -0.5),
        'pk_keys1': nrm((DEPTH, PK_HEADS, PK_NKEYS, PK_DHALF), PK_DHALF ** -0.5),
        'pk_keys2': nrm((DEPTH, PK_HEADS, PK_NKEYS, PK_DHALF), PK_DHALF ** -0.5),
        'peer_u': nrm((DEPTH, PK_EXPERTS, D_MODEL), D_MODEL ** -0.5),
        'peer_v': nrm((DEPTH, PK_EXPERTS, D_MODEL), PK_HEADS ** -0.5),
        'g_final': gain((D_MODEL,)),
    }

def reference(x_prompt, x_sample, cache_attn_k, cache_attn_v, cache_mem_k, cache_mem_v, state_conv,
              state_rglru, mem_prompt, g_mix, w_in, lam_q1, lam_k1, lam_q2, lam_k2, g_subln, conv_w,
              conv_b, rg_wa, rg_ba, rg_wx, rg_bx, rg_lambda, w_out, g_cross, g_mem, w_cq, w_ck, w_cv,
              w_co, g_ffn, w_pq, pk_keys1, pk_keys2, peer_u, peer_v, g_final):
    b, l = x_prompt.shape[0], x_prompt.shape[1]
    db, dl = x_sample.shape[0], x_sample.shape[1]
    past = cache_attn_k.shape[2]
    pos_p = jnp.arange(l, dtype=jnp.int32)
    pos_s = past + jnp.arange(dl, dtype=jnp.int32)
    xp, xs = x_prompt, x_sample
    kp_l, vp_l, mk_l, mv_l, cp_l, hp_l = [], [], [], [], [], []
    ks_l, vs_l, cs_l, hs_l = [], [], [], []
    for li in range(DEPTH):
        lam_init = 0.8 - 0.6 * math.exp(-0.3 * li)
        params = (g_mix[li], w_in[li], lam_q1[li], lam_k1[li], lam_q2[li], lam_k2[li], g_subln[li],
                  conv_w[li], conv_b[li], rg_wa[li], rg_ba[li], rg_wx[li], rg_bx[li], rg_lambda[li],
                  w_out[li], g_cross[li], w_cq[li], w_co[li], g_ffn[li], w_pq[li], pk_keys1[li],
                  pk_keys2[li], peer_u[li], peer_v[li])
        mk_p, mv_p = memory_kv(mem_prompt, g_mem[li], w_ck[li], w_cv[li])
        xp, kp, vp, cp, hp = layer(
            xp, pos_p,
            jnp.zeros((b, 0, 2 * DA_HEADS, DA_DK), xp.dtype), jnp.zeros((b, 0, DA_HEADS, DA_DV), xp.dtype),
            jnp.zeros((b, CONV_W - 1, RG_WIDTH), xp.dtype), jnp.zeros((b, RG_WIDTH), xp.dtype),
            mk_p, mv_p, params, lam_init)
        xs, ks_, vs_, cs, hs = layer(
            xs, pos_s, cache_attn_k[li], cache_attn_v[li], state_conv[li], state_rglru[li],
            cache_mem_k[li], cache_mem_v[li], params, lam_init)
        kp_l.append(kp); vp_l.append(vp); mk_l.append(mk_p); mv_l.append(mv_p)
        cp_l.append(cp); hp_l.append(hp)
        ks_l.append(ks_); vs_l.append(vs_); cs_l.append(cs); hs_l.append(hs)
    y_prompt = rmsnorm(xp, g_final)
    y_sample = rmsnorm(xs, g_final)
    return (y_prompt, y_sample,
            jnp.stack(kp_l), jnp.stack(vp_l), jnp.stack(mk_l), jnp.stack(mv_l),
            jnp.stack(cp_l), jnp.stack(hp_l),
            jnp.stack(ks_l), jnp.stack(vs_l), jnp.stack(cs_l), jnp.stack(hs_l))


_drawn_inputs = setup_inputs


def setup_inputs(seed=0):
    import zlib

    import numpy as np

    out = dict(_drawn_inputs(seed))
    spreads = {}
    factors = {'lam_q2': 5.129, 'rg_ba': 8.0, 'rg_bx': 8.0, 'g_cross': 4.383}
    for name, (base, spread) in spreads.items():
        noise = np.random.default_rng([zlib.crc32(name.encode()), seed]).standard_normal(out[name].shape)
        drawn = base * np.exp(spread * noise) if base else spread * noise
        out[name] = __import__('jax').numpy.asarray(drawn.astype(out[name].dtype))
    for name, factor in factors.items():
        out[name] = (out[name] * factor).astype(out[name].dtype)
    return out
```

```python
import math

import concourse.bass as bass
import numpy as np
from concourse import mybir

F32 = mybir.dt.float32
F32R = mybir.dt.float32r
U32 = mybir.dt.uint32
ALU = mybir.AluOpType
ACT = mybir.ActivationFunctionType
AX = mybir.AxisListType.X

P = 128
D = 1024
KT = D // P
NP_TOK, NS_TOK = 512, 64
NT = NP_TOK + NS_TOK
HALF = NT // 2
ROWS = [128, 128, 128, 128, 64]
T0 = [0, 128, 256, 384, 512]
TILES = len(ROWS)
HEADS, DK, DV = 8, 64, 128
LAM_INIT = 0.8 - 0.6 * math.exp(-0.3 * 0)
PAST = 512
MEM = 256
MT = MEM // P
CA_HEADS, CA_DH = 4, 256
PK_HEADS, NKEYS, TOPK = 8, 128, 16
RG_C = 8.0
CONVW = 4
RMS_EPS, SUBLN_EPS = 1e-6, 1e-5
BANK = 512
BANKS = 8
CHUNK = 512
PIECE = 4 * CHUNK
SEG = NP_TOK + CONVW - 1
XPW = SEG + CONVW - 1 + NS_TOK
CW = XPW - (CONVW - 1)
CA_ = 290
PAR_CW, PAR_CB, PAR_BA, PAR_BX, PAR_SC, PAR_H0, PAR_N = 256, 260, 261, 262, 264, 267, 272
N_CK, N_CV, N_RG, N_K, N_V, N_Q, N_OUT, N_CQ, N_CO, N_PQ = 2, 2, 8, 2, 2, 2, 2, 2, 2, 4
PRE_CHUNKS = N_CK + N_CV + N_RG + N_K + N_V + N_Q + N_OUT + N_CQ + N_CO + N_PQ
EG = 4
GROUPS = NKEYS // EG
CHUNKS = PRE_CHUNKS + 2 * GROUPS
TB = 32
TBN = NT // TB
NEG = -3.0e38


class Steps:

    def __init__(self, eng, sem):
        self.eng, self.sem, self.n, self.i, self.per = eng, sem, 0, None, 0

    def done(self, ins):
        self.n += 1
        ins.then_inc(self.sem, 1)
        self.eng.wait_ge(self.sem, self.n if self.i is None else self.i * self.per + self.n)

    def enter(self, i, per):
        self.i, self.per, self.start = i, per, self.n

    def leave(self, times):
        assert self.n - self.start == self.per, (self.n - self.start, self.per)
        self.n, self.i = self.start + times * self.per, None


class Turns:

    def __init__(self):
        self.n, self.i, self.per = 0, None, 0

    def take(self):
        bank, value = self.n % BANKS, self.n // BANKS + 1
        self.n += 1
        return bank, value if self.i is None else self.i * (self.per // BANKS) + value

    def enter(self, i, per):
        self.i, self.per, self.start = i, per, self.n

    def leave(self, times):
        assert self.n - self.start == self.per and self.per % BANKS == 0
        self.n, self.i = self.start + times * self.per, None


class Count:

    def __init__(self, n=0):
        self.n, self.i, self.per = n, None, 0

    def up(self, k=1):
        self.n += k
        return self.value()

    def value(self, more=0):
        v = self.n + more
        return v if self.i is None else self.i * self.per + v

    def enter(self, i, per):
        self.i, self.per, self.start = i, per, self.n

    def leave(self, times):
        assert self.n - self.start == self.per, (self.n - self.start, self.per)
        self.n, self.i = self.start + times * self.per, None


def encoder_layer(nc: bass.Bass, block, a: dict, o: dict):
    base = (nc.sbuf_base + 31) // 32 * 32
    cursor = [base]

    def put(name, shape, dt=F32, at=None):
        size = int(np.prod(shape[1:])) * 4
        where = cursor[0] if at is None else at
        t = nc.alloc_sbuf_tensor_at(name, shape, dt, offset=where)
        if at is None:
            cursor[0] += (size + 31) // 32 * 32
        return t

    actH = put("actH", [P, KT, NT], F32R)
    actL = put("actL", [P, KT, NT], F32R)
    wH = put("wH", [P, 4, 4, CHUNK], F32R)
    wL = put("wL", [P, 4, 4, CHUNK], F32R)
    raw = put("raw", [P, 2, PIECE])
    ident = put("ident", [P, P])
    gain = put("gain", [P, D])
    small = put("small", [P, 256])
    mask = put("mask", [1, P + DK])
    arena = cursor[0]

    class Region:
        def __init__(self, start=arena):
            self.at = start

        def put(self, name, shape, dt=F32):
            size = (int(np.prod(shape[1:])) * 4 + 31) // 32 * 32
            t = nc.alloc_sbuf_tensor_at(name, shape, dt, offset=self.at)
            self.at += size
            return t

    sm = {}
    at = 0
    for name, n in (("ssq", 8), ("rstd", 8), ("nmax", 8), ("z", 8), ("lamv", 2), ("lamt", 8), ("gsub", 1),
                    ("ncall", 8), ("pcall", 8), ("sp", 40), ("oss", 8), ("orstd", 8), ("mz", 8), ("pk", 24)):
        sm[name] = small[:, at:at + n]
        at += n
    assert at <= 256

    r = Region()
    xres = r.put("xres", [P, TILES, D])
    after_xres = r.at
    xn = r.put("xn", [P, 2, D])
    sq = r.put("sq", [P, D])
    memx = r.put("memx", [P, MT, D])
    mk_sb = r.put("mk_sb", [P, KT, MEM])
    mv_sb = r.put("mv_sb", [P, MT, D])
    r = Region()
    rxp = r.put("rxp", [P, 2, XPW + 2])
    par = r.put("par", [P, 2, PAR_N])
    conv = r.put("conv", [P, 2, CW + 1])
    gel = r.put("gel", [P, 2, NT])
    sgr = r.put("sgr", [P, 2, NT])
    sga = r.put("sga", [P, 2, NT])
    gate_r = r.put("gate_r", [P, CW + 1])
    gate_i = r.put("gate_i", [P, CW + 1])
    lru_a = r.put("lru_a", [P, CW + 1])
    lru_t = r.put("lru_t", [P, CW + 1])
    lru_m = r.put("lru_m", [P, CW + 1])
    lru_h = r.put("lru_h", [P, NT])
    yrec = r.put("yrec", [P, 2, NT])
    cstate = r.put("cstate", [P, KT, 6])
    hstate = r.put("hstate", [P, KT, 2])
    lamp = r.put("lamp", [P, 4 * DK + KT])
    r = Region()
    kT = r.put("kT", [P, HEADS, NT])
    qT = r.put("qT", [P, HEADS, NT])
    vtok = r.put("vtok", [P, TILES, D])
    att = r.at
    ropec = r.put("ropec", [P, TILES, 32])
    ropes = r.put("ropes", [P, TILES, 32])
    ropen = r.put("ropen", [P, TILES, 32])
    rot1 = r.put("rot1", [P, CHUNK])
    rot2 = r.put("rot2", [P, CHUNK])
    rot = r.put("rot", [P, 2, CHUNK])
    r = Region(att)
    sat = r.put("sat", [P, KT, P])
    rt = r.put("rt", [P, KT, P])
    osb = r.put("osb", [P, D])
    prob_at = r.at
    osq = nc.alloc_sbuf_tensor_at("osq", [P, D], F32, offset=prob_at)
    prob = r.put("prob", [P, 2, 2, NP_TOK])
    aT = r.put("aT", [P, 2, CHUNK])
    attn_end = r.at
    probs = nc.alloc_sbuf_tensor_at("probs", [P, 2, NT], F32, offset=prob_at)
    ckv0 = r.put("ckv0", [P, 2, PAST])
    r = Region(after_xres)
    qcT = r.put("qcT", [P, KT, NT])
    mkT = r.put("mkT", [P, 2, KT, MEM])
    mvt = r.put("mvt", [P, 2, MT, D])
    cp = r.put("cp", [P, 2, D])
    cpT = r.put("cpT", [P, D])
    r = Region()
    pqT = r.put("pqT", [P, 2 * PK_HEADS, NT])
    keys = r.put("keys", [P, 2 * PK_HEADS, NKEYS])
    ssb = r.put("ssb", [P, 2 * PK_HEADS, NKEYS])
    work = r.put("work", [P, 2048])
    cand = r.put("cand", [P, 2048])
    top = r.put("top", [P, 2 * PK_HEADS, TOPK])
    topi = r.put("topi", [P, 2 * PK_HEADS, TOPK], U32)
    topf = r.put("topf", [P, 2 * PK_HEADS, TOPK])
    best = r.put("best", [P, PK_HEADS, TOPK])
    besti = r.put("besti", [P, PK_HEADS, TOPK], U32)
    bestr = r.put("bestr", [P, 2, PK_HEADS, TOPK], U32)
    bestf = r.put("bestf", [P, 2, PK_HEADS, TOPK])
    pick = cand
    iota16 = r.put("iota16", [P, TOPK])
    chosen = r.put("chosen", [P, 3, PK_HEADS * TOPK])
    assert r.at <= nc.sbuf_usable_end, r.at
    chosenT = nc.alloc_sbuf_tensor_at("chosenT", [P, 3, NT], F32, offset=nc.sbuf_usable_end // 32 * 32 - 3 * NT * 4)
    assert r.at <= nc.sbuf_usable_end // 32 * 32 - 3 * NT * 4
    r = Region()
    iota = r.put("iota", [P, NKEYS])
    hot1 = r.put("hot1", [P, 2, 4, NKEYS])
    hot2 = r.put("hot2", [P, 2, 4, NKEYS])
    cst = r.put("cst", [P, 2, NKEYS, TB])
    r = Region()
    acc = r.put("acc", [P, KT, NT])
    cg = r.put("cg", [P, 2, TBN, EG, TB])
    ge = r.put("ge", [P, 2, NT])
    gf = r.put("gf", [P, 2, NT])
    gH = r.put("gH", [P, 2, EG, NT], F32R)
    gL = r.put("gL", [P, 2, EG, NT], F32R)
    assert r.at <= nc.sbuf_usable_end, r.at
    r = Region(arena + KT * NT * 4)
    x2b = r.put("x2b", [P, TILES, D])
    yout = r.put("yout", [P, 2, D])

    ps = nc.alloc_psum_tensor("ps", [P, BANKS * BANK], F32)

    def bank(b, n=BANK, rows=P):
        return ps[0:rows, b * BANK:b * BANK + n]

    sa_d = nc.dram_tensor("sa_scratch", (KT, P, NT), F32).ap()
    r_d = nc.dram_tensor("r_scratch", (KT, P, NT), F32).ap()
    x2_d = nc.dram_tensor("x2_scratch", (NT, D), F32).ap()
    c_d = nc.dram_tensor("c_scratch", (TBN, P, NKEYS, TB), F32).ap()

    S = nc.alloc_semaphore
    raw_in = [S(f"raw_in{j}") for j in range(2)]
    high_done = S("high_done")
    w_ready = S("w_ready")
    w_free = S("w_free")
    filled = [S(f"filled{b}") for b in range(BANKS)]
    emptied = [S(f"emptied{b}") for b in range(BANKS)]
    ve_step = S("ve_step")
    names = """const_in gain_in gain_used memx_in x_in ssq_clear ssq_ready var_ready std_ready xn_ready acth_done
        out_done lamp_in sp_neg sp_exp sp_one sp_ln lam_sums lam_exp lam_ready conv_done gate_ready m_ready
        root_ready yrec_ready rot_ready rope_in sc_ready nm_ready p_ready a_ready t_ready aT_ready pv_done
        osb_ready ovar_ready ostd_ready on_ready yt_ready merged mh_done ml_done sat_in ckv_in mask_in mem_in
        cs_ready cm_ready ce_ready cn_ready ct_ready cpT_ready co_ready ch_done cl_done res_ready x2_store
        keys_in iota16_in score_ready ssb_ready ssb_used gexp_in gexp_out chosen_ready chT_ready chT_copied
        iota_in hot_ready c_filled c_copied c_used u_done ge_ready gf_ready gh_done gl_done v_done acc_added
        x2_in yt2_ready y_ready taken_up""".split()
    (const_in, gain_in, gain_used, memx_in, x_in, ssq_clear, ssq_ready, var_ready, std_ready, xn_ready, acth_done,
     out_done, lamp_in, sp_neg, sp_exp, sp_one, sp_ln, lam_sums, lam_exp, lam_ready, conv_done, gate_ready, m_ready,
     root_ready, yrec_ready, rot_ready, rope_in, sc_ready, nm_ready, p_ready, a_ready, t_ready, aT_ready, pv_done,
     osb_ready, ovar_ready, ostd_ready, on_ready, yt_ready, merged, mh_done, ml_done, sat_in, ckv_in, mask_in, mem_in,
     cs_ready, cm_ready, ce_ready, cn_ready, ct_ready, cpT_ready, co_ready, ch_done, cl_done, res_ready, x2_store,
     keys_in, iota16_in, score_ready, ssb_ready, ssb_used, gexp_in, gexp_out, chosen_ready, chT_ready, chT_copied,
     iota_in, hot_ready, c_filled, c_copied, c_used, u_done, ge_ready, gf_ready, gh_done, gl_done, v_done, acc_added,
     x2_in, yt2_ready, y_ready, taken_up) = [S(name) for name in names]
    par_in = [S(f"par_in{j}") for j in range(2)]
    sa_store = [S(f"sa_store{j}") for j in range(2)]
    r_store = [S(f"r_store{j}") for j in range(2)]
    k_store = [S(f"k_store{j}") for j in range(2)]
    c_store = [S(f"c_store{j}") for j in range(2)]
    c_in = [S(f"c_in{j}") for j in range(2)]
    y_store = [S(f"y_store{j}") for j in range(2)]

    UNITS = [(i, h) for i in range(TILES) for h in range(HEADS)]
    KQV = [("k", 0), ("k", 1), ("v", 0), ("v", 1), ("q", 0), ("q", 1)]
    TUNITS = [(kind, c, i) for kind, c in KQV for i in range(TILES)]

    def halves(b):
        return ps[:, b * BANK:(b + 2) * BANK].rearrange("p (c n) -> p c n", n=BANK)[:, :, 0:HALF]

    @block.sync
    def _(sp):
        def piece(n, j, used=True):
            if used:
                sp.wait_ge(w_ready, n * 2 - 2)
            sp.dma_start(raw[:, j, :], a["wts"][n]).then_inc(raw_in[j], 16)

        def load_c(g, s, used):
            if used is not None:
                sp.wait_ge(c_used, used)
            sp.dma_start(cg[:, s], c_d[:, :, bass.ts(g, EG), :].rearrange("b p e t -> p b e t")).then_inc(c_in[s], 16)

        piece(0, 0, used=False)
        piece(1, 1, used=False)
        with sp.Fori(0, PRE_CHUNKS + 1) as i:
            for j in range(2):
                piece(i * 2 + (2 + j), j)
        for j in range(2):
            sp.wait_ge(c_store[j], 16 * TBN // 2)
        load_c(0, 0, None)
        load_c(1, 1, None)
        n0 = 2 * (PRE_CHUNKS + 2)
        with sp.Fori(0, GROUPS // 2 - 1) as i:
            for s in range(2):
                for j in range(2):
                    piece(i * 8 + (n0 + 4 * s + j), j)
                load_c(i * 2 + (2 + s), s, i * 2 + (1 + s))
                for j in range(2):
                    piece(i * 8 + (n0 + 4 * s + 2 + j), j)
        for q in range(4):
            piece(2 * CHUNKS - 4 + q, q % 2)

    @block.gpsimd
    def _(pool):
        with pool.Fori(0, CHUNKS // 2) as i:
            for s in range(4):
                w = raw[:, s % 2, :]
                hi = wH[:, s].rearrange("p k n -> p (k n)")
                lo = wL[:, s].rearrange("p k n -> p (k n)")
                pool.wait_ge(raw_in[s % 2], i * 32 + 16 * (s // 2 + 1))
                pool.wait_ge(w_free, i * 4 + (s // 2 * 2 + 2))
                pool.sem_inc(taken_up, 1)
                cuts = (slice(0, PIECE // 2), slice(PIECE // 2, PIECE))
                for cut in cuts:
                    pool.tensor_scalar(hi[:, cut], w[:, cut], 1.0, 1.0, ALU.mult, ALU.mult).then_inc(high_done, 1)
                for c, cut in enumerate(cuts):
                    pool.wait_ge(high_done, i * 8 + (2 * s + c + 1))
                    pool.tensor_tensor(lo[:, cut], w[:, cut], hi[:, cut].bitcast(F32), ALU.subtract)\
                        .then_inc(w_ready, 1)

    @block.tensor
    def _(pe):
        turns = Turns()
        pieces = Count()
        release = [0]

        def begin(ins):
            if release[0]:
                ins.then_inc(w_free, 2)
                release[0] = 0

        pe.sem_inc(w_free, 4)
        for b in range(BANKS):
            pe.sem_inc(emptied[b], 1)
        pe.wait_ge(const_in, 16)

        def fill(out, terms, sem=None):
            for t, (lhs, rhs) in enumerate(terms):
                mm = pe.matmul(out, lhs, rhs, start=t == 0, stop=t == len(terms) - 1)
                if t == 0 and len(terms) > 1:
                    begin(mm)
            if sem is not None:
                mm.then_inc(sem, 1)
            return mm

        def weight(slot, k, cut):
            return wH[:, slot + k // 4, k % 4, cut], wL[:, slot + k // 4, k % 4, cut]

        def chunk(slot, groups):
            for g, (cols, terms) in enumerate(groups):
                b, value = turns.take()
                pe.wait_ge(emptied[b], value)
                for k in range(KT):
                    if g == 0 and k % 4 == 0:
                        pieces.up(2)
                        pe.wait_ge(w_ready, pieces.value())
                    for t, (lhs, rhs) in enumerate(terms(k)):
                        mm = pe.matmul(cols(b), lhs, rhs, start=k == 0 and t == 0, stop=k == KT - 1 and t == 2)
                        if k == 0 and t == 0:
                            begin(mm)
                mm.then_inc(filled[b], 1)
            release[0] = 1

        def feature_chunk(slot, n_tok, n_parts):
            def make(blk, part):
                w = slice(blk * P, blk * P + P)
                t = slice(part * n_tok, (part + 1) * n_tok)

                def terms(k):
                    h, l = weight(slot, k, w)
                    return (h, actH[:, k, t]), (h, actL[:, k, t]), (l, actH[:, k, t])
                return (lambda b: bank(b, n_tok)), terms
            chunk(slot, [make(blk, part) for blk in range(4) for part in range(n_parts)])

        def token_group(slot, i, rows, t0):
            t = slice(t0, t0 + rows)

            def terms(k):
                h, l = weight(slot, k, slice(0, CHUNK))
                return (actH[:, k, t], h), (actH[:, k, t], l), (actL[:, k, t], h)
            return (lambda b: bank(b, CHUNK, rows)), terms

        def norm(n_tiles, first, rows):
            for i in range(n_tiles):
                pe.wait_ge(xn_ready, first + i + 1)
                for half in range(2):
                    b, value = turns.take()
                    pe.wait_ge(emptied[b], value)
                    for k in range(4):
                        src = xn[0:rows[i], (first + i) % 2, (half * 4 + k) * P:(half * 4 + k + 1) * P]
                        mm = pe.transpose(ps[:, b * BANK + k * rows[i]:b * BANK + (k + 1) * rows[i]], src,
                                          ident[0:rows[i], 0:rows[i]])
                        if half == 0 and k == 0:
                            begin(mm)
                    mm.then_inc(filled[b], 1)
            last[0] = (b, value)

        last = [None]

        def evacuated():
            b, value = last[0]
            pe.wait_ge(emptied[b], value + 1)

        norm(MT, 0, ROWS)
        evacuated()
        for c in range(N_CK):
            feature_chunk(2 * c, MEM, 1)
        for c in range(N_CV):
            chunk(2 * c, [token_group(2 * c, i, P, i * P) for i in range(MT)])
        norm(TILES, MT, ROWS)
        evacuated()

        def gates(s, value):
            pe.wait_ge(conv_done, value)
            for w in range(2):
                for cut in (slice(0, CA_), slice(CA_, CW)):
                    b, turn = turns.take()
                    pe.wait_ge(emptied[b], turn)
                    fill(ps[:, b * BANK:b * BANK + cut.stop - cut.start],
                         [(par[:, s, w * P:(w + 1) * P], conv[:, s, cut])], filled[b])

        feature_chunk(0, HALF, 2)
        feature_chunk(2, HALF, 2)
        gates(0, 1)
        with pe.Fori(0, N_RG // 2 - 1) as i:
            turns.enter(i, 24)
            pieces.enter(i, 8)
            feature_chunk(0, HALF, 2)
            gates(1, i * 2 + 2)
            feature_chunk(2, HALF, 2)
            gates(0, i * 2 + 3)
            turns.leave(N_RG // 2 - 1)
            pieces.leave(N_RG // 2 - 1)
        def turn_rotated(u):
            kind, c, i = TUNITS[u]
            if kind == "v":
                return
            n = sum(1 for k, _, _ in TUNITS[:u + 1] if k != "v")
            pe.wait_ge(rot_ready, n)
            b, value = turns.take()
            pe.wait_ge(emptied[b], value)
            for k in range(4):
                mm = pe.transpose(ps[:, b * BANK + k * ROWS[i]:b * BANK + (k + 1) * ROWS[i]],
                                  rot[0:ROWS[i], (n - 1) % 2, k * P:(k + 1) * P], ident[0:ROWS[i], 0:ROWS[i]])
                if k == 0:
                    begin(mm)
            mm.then_inc(filled[b], 1)

        u = 0
        for n, (kind, c) in enumerate(KQV):
            slot = 2 * (n % 2)
            for i in range(TILES):
                cols, terms = token_group(slot, i, ROWS[i], T0[i])
                b, value = turns.take()
                pe.wait_ge(emptied[b], value)
                for k in range(KT):
                    if i == 0 and k % 4 == 0:
                        pieces.up(2)
                        pe.wait_ge(w_ready, pieces.value())
                    for t, (lhs, rhs) in enumerate(terms(k)):
                        mm = pe.matmul(cols(b), lhs, rhs, start=k == 0 and t == 0, stop=k == KT - 1 and t == 2)
                        if k == 0 and t == 0:
                            begin(mm)
                mm.then_inc(filled[b], 1)
                if i == TILES - 1:
                    release[0] = 1
                if n == 0 and i == 0:
                    gates(1, N_RG)
                if u >= 1:
                    turn_rotated(u - 1)
                u += 1
        turn_rotated(u - 1)
        for b in range(BANKS):
            pe.wait_ge(emptied[b], (turns.n - 1 - b) // BANKS + 2)

        pe.wait_ge(mask_in, 16)

        def scores(u):
            i, h = UNITS[u]
            rows = ROWS[i]
            t = slice(T0[i], T0[i] + rows)
            if u >= 1 and (i == TILES - 1 or u >= 2):
                pe.wait_ge(p_ready, u if i == TILES - 1 else u - 1)
            if i == TILES - 1:
                pe.wait_ge(ckv_in, 32 * (h + 1))
            for s in range(2):
                half = slice(s * DK, (s + 1) * DK)
                if i < TILES - 1:
                    b, n = 2 * (u % 2) + s, P * (i + 1)
                    mm = pe.matmul(bank(b, n), qT[half, h, t], kT[half, h, 0:n], start=True, stop=False)
                    if s == 0:
                        begin(mm)
                    mm = pe.matmul(ps[:, b * BANK + n - DK:b * BANK + n], mask[0:1, 0:P], mask[0:1, P:P + DK],
                                   start=False, stop=True)
                else:
                    b = 2 * s
                    pe.matmul(bank(b, PAST, rows), qT[half, h, t], ckv0[half, 0, :], start=True, stop=True)
                    mm = pe.matmul(bank(b + 1, rows, rows), qT[half, h, t], kT[half, h, t], start=True, stop=True)
            mm.then_inc(sc_ready, 1)

        def turn_probs(u):
            i, h = UNITS[u]
            rows = ROWS[i]
            pe.wait_ge(a_ready, u + 1)
            if u >= 2:
                pe.wait_ge(aT_ready, u - 1)
            if h < 2 and i > 0:
                pe.wait_ge(ml_done, i)
            b = 4 + u % 2
            if i < TILES - 1:
                for k in range(i + 1):
                    mm = pe.transpose(ps[:, b * BANK + k * P:b * BANK + (k + 1) * P],
                                      prob[:, u % 2, 0, k * P:(k + 1) * P], ident[:, :])
            else:
                for k in range(PAST // P):
                    pe.transpose(ps[:, b * BANK + k * rows:b * BANK + (k + 1) * rows],
                                 probs[0:rows, 0, k * P:(k + 1) * P], ident[0:rows, 0:rows])
                k = PAST // P
                mm = pe.transpose(ps[0:rows, b * BANK + k * rows:b * BANK + (k + 1) * rows],
                                  probs[0:rows, 0, PAST:NT], ident[0:rows, 0:rows])
            mm.then_inc(t_ready, 1)

        def weighted(u):
            i, h = UNITS[u]
            rows = ROWS[i]
            pe.wait_ge(aT_ready, u + 1)
            if h == 0 and i > 0:
                pe.wait_ge(osb_ready, i)
            out = ps[0:rows, 6 * BANK + h * DV:6 * BANK + (h + 1) * DV]
            cols = slice(h * DV, (h + 1) * DV)
            if i < TILES - 1:
                terms = [(aT[:, u % 2, k * P:(k + 1) * P], vtok[:, k, cols]) for k in range(i + 1)]
            else:
                terms = [(aT[:, u % 2, k * rows:(k + 1) * rows], ckv0[:, 1, k * P:(k + 1) * P]) for k in range(PAST // P)]
                k = PAST // P
                terms.append((aT[0:rows, u % 2, k * rows:(k + 1) * rows], vtok[0:rows, TILES - 1, cols]))
            for t, (lhs, rhs) in enumerate(terms):
                mm = pe.matmul(out, lhs, rhs, start=t == 0, stop=t == len(terms) - 1)
            mm.then_inc(pv_done, 1)

        def turn_outputs(i):
            rows = ROWS[i]
            pe.wait_ge(on_ready, i + 1)
            pe.wait_ge(aT_ready, HEADS * (i + 1))
            for h in range(HEADS):
                b = 4 + h // 4
                mm = pe.transpose(ps[:, b * BANK + (h % 4) * rows:b * BANK + (h % 4 + 1) * rows],
                                  osb[0:rows, h * DV:(h + 1) * DV], ident[0:rows, 0:rows])
            mm.then_inc(yt_ready, 1)

        for i in range(TILES):
            for h in range(HEADS):
                u = i * HEADS + h
                if i < TILES - 1:
                    if h == 0:
                        scores(u)
                    if h + 1 < HEADS:
                        scores(u + 1)
                    turn_probs(u)
                    if h > 0:
                        weighted(u - 1)
                else:
                    scores(u)
                    turn_probs(u)
                    weighted(u)
            if i < TILES - 1:
                weighted(i * HEADS + HEADS - 1)
            turn_outputs(i)
        pe.wait_ge(ml_done, TILES)

        def token_chunks(n_chunks):
            for c in range(n_chunks):
                chunk(2 * c, [token_group(2 * c, i, ROWS[i], T0[i]) for i in range(TILES)])

        token_chunks(N_OUT)
        norm(TILES, MT + TILES, ROWS)
        evacuated()
        for c in range(N_CQ):
            feature_chunk(2 * c, HALF, 2)
        for b in range(BANKS):
            pe.wait_ge(emptied[b], (turns.n - 1 - b) // BANKS + 2)
        pe.wait_ge(mem_in, 64)

        def cross_scores(i):
            rows, src = ROWS[i], i // (TILES - 1)
            if i >= 2:
                pe.wait_ge(ce_ready, i - 1)
            for h in range(CA_HEADS):
                out = ps[0:rows, 2 * (i % 2) * BANK + h * MEM:2 * (i % 2) * BANK + (h + 1) * MEM]
                mm = fill(out, [(qcT[:, 2 * h + k, T0[i]:T0[i] + rows], mkT[:, src, 2 * h + k, :]) for k in range(2)])
            mm.then_inc(cs_ready, 1)

        def cross_rest(i):
            rows, src = ROWS[i], i // (TILES - 1)
            pe.wait_ge(cn_ready, i + 1)
            if i >= 1:
                pe.wait_ge(cpT_ready, i)
            for m in range(2 * CA_HEADS):
                b = 4 + m // 4
                mm = pe.transpose(ps[:, b * BANK + (m % 4) * rows:b * BANK + (m % 4 + 1) * rows],
                                  cp[0:rows, i % 2, m * P:(m + 1) * P], ident[0:rows, 0:rows])
            mm.then_inc(ct_ready, 1)
            pe.wait_ge(cpT_ready, i + 1)
            if i >= 1:
                pe.wait_ge(cl_done, 2 * i)
            for blk in range(KT):
                h = blk // 2
                out = ps[:, (6 + blk // 4) * BANK + (blk % 4) * rows:(6 + blk // 4) * BANK + (blk % 4 + 1) * rows]
                mm = fill(out, [(mvt[:, src, m, blk * P:(blk + 1) * P], cpT[:, (2 * h + m) * rows:(2 * h + m + 1) * rows])
                                for m in range(MT)])
            mm.then_inc(co_ready, 1)

        cross_scores(0)
        for i in range(TILES):
            if i + 1 < TILES:
                cross_scores(i + 1)
            cross_rest(i)
        pe.wait_ge(cl_done, 2 * TILES)
        token_chunks(N_CO)
        norm(TILES, MT + 2 * TILES, ROWS)
        evacuated()
        for c in range(N_PQ):
            feature_chunk(2 * (c % 2), HALF, 2)
        for b in range(BANKS):
            pe.wait_ge(emptied[b], (turns.n - 1 - b) // BANKS + 2)

        pe.wait_ge(keys_in, 16)

        def key_scores(i):
            rows = ROWS[i]
            if i >= 1:
                pe.wait_ge(ssb_ready, i)
            for s in range(2 * PK_HEADS):
                mm = fill(ps[0:rows, s * P:(s + 1) * P], [(pqT[:, s, T0[i]:T0[i] + rows], keys[:, s, :])])
            mm.then_inc(score_ready, 1)

        key_scores(0)
        for i in range(TILES):
            if i + 1 < TILES:
                key_scores(i + 1)
            pe.wait_ge(chosen_ready, i + 1)
            if i >= 1:
                pe.wait_ge(chT_copied, i)
            for s in range(3):
                mm = pe.transpose(ps[:, 4 * BANK + s * P:4 * BANK + s * P + ROWS[i]], chosen[0:ROWS[i], s, :],
                                  ident[0:ROWS[i], 0:ROWS[i]])
            mm.then_inc(chT_ready, 1)

        pe.sem_inc(c_filled, 2)
        with pe.Fori(0, TBN // 2) as i:
            for q in range(2 * TB // 4):
                b = q % BANKS
                pe.wait_ge(hot_ready, i * (TB // 2) + (q + 1))
                pe.wait_ge(c_copied, i * (TB // 2) + (q + 1))
                for t in range(4):
                    mm = pe.matmul(ps[:, b * BANK + t * P:b * BANK + (t + 1) * P], hot1[:, q % 2, t, :],
                                   hot2[:, q % 2, t, :], start=True, stop=True)
                mm.then_inc(c_filled, 1)
        pe.wait_ge(c_copied, NT // 4 + BANKS)

        def up(g_count, slot, tiles):
            for e in range(EG):
                b = 2 * (e % 2)
                pe.wait_ge(ge_ready, tiles(e))
                for part in range(2):
                    t = slice(part * HALF, (part + 1) * HALF)
                    for k in range(KT):
                        if e == 0 and part == 0 and k % 4 == 0:
                            pieces.up(2)
                            pe.wait_ge(w_ready, pieces.value())
                        h, l = weight(slot, k, slice(e * P, (e + 1) * P))
                        for w, (lhs, rhs) in enumerate(((h, actH[:, k, t]), (h, actL[:, k, t]), (l, actH[:, k, t]))):
                            mm = pe.matmul(bank(b + part, HALF), lhs, rhs, start=k == 0 and w == 0,
                                           stop=k == KT - 1 and w == 2)
                            if k == 0 and w == 0 and part == 0 and e == 0:
                                begin(mm)
                mm.then_inc(u_done, 1)
            release[0] = 1

        def down(slot, s, gl, added):
            pe.wait_ge(gl_done, gl)
            for d in range(KT):
                b = 4 + 2 * (d % 2)
                pe.wait_ge(acc_added, added(d))
                for part in range(2):
                    t = slice(part * HALF, (part + 1) * HALF)
                    for e in range(EG):
                        if d == 0 and part == 0 and e % 2 == 0:
                            pieces.up(2)
                            pe.wait_ge(w_ready, pieces.value())
                        at = (e % 2) * D + d * P
                        h = wH[:, slot + e // 2].rearrange("p k n -> p (k n)")[:, at:at + P]
                        l = wL[:, slot + e // 2].rearrange("p k n -> p (k n)")[:, at:at + P]
                        for w, (lhs, rhs) in enumerate(((h, gH[:, s, e, t]), (h, gL[:, s, e, t]), (l, gH[:, s, e, t]))):
                            mm = pe.matmul(bank(b + part, HALF), lhs, rhs, start=e == 0 and w == 0,
                                           stop=e == EG - 1 and w == 2)
                            if d == 0 and part == 0 and e == 0 and w == 0:
                                begin(mm)
                mm.then_inc(v_done, 1)
            release[0] = 1

        up(0, 0, lambda e: e + 1)
        with pe.Fori(0, GROUPS // 2 - 1) as i:
            pieces.enter(i, 16)
            for s in range(2):
                up(0, 2, lambda e: i * (2 * EG) + (EG * (s + 1) + e + 1))
                down(0, s, i * (2 * EG) + EG * (s + 1), lambda d: i * (2 * KT) + (KT * s + d + 1))
            pieces.leave(GROUPS // 2 - 1)
        up(0, 2, lambda e: EG * (GROUPS - 1) + e + 1)
        down(0, 0, EG * (GROUPS - 1), lambda d: KT * (GROUPS - 2) + d + 1)
        down(2, 1, EG * GROUPS, lambda d: KT * (GROUPS - 1) + d + 1)

        pe.wait_ge(acc_added, KT * GROUPS + 2)
        for i in range(TILES):
            if i >= 2:
                pe.wait_ge(res_ready, i - 1)
            for k in range(KT):
                b = 2 * (i % 2) + k // 4
                mm = pe.transpose(ps[0:ROWS[i], b * BANK + (k % 4) * P:b * BANK + (k % 4 + 1) * P],
                                  acc[:, k, T0[i]:T0[i] + ROWS[i]], ident[:, :])
            mm.then_inc(yt2_ready, 1)


    @block.scalar
    def _(act):
        turns = Turns()

        def wait_filled():
            b, value = turns.take()
            act.wait_ge(filled[b], value)
            return b, value

        def skip(n):
            for _ in range(n):
                turns.take()

        def load_x():
            act.dma_start(xres[:, 0:4, :], a["x"][0:NP_TOK].rearrange("(i p) d -> p i d", p=P)).then_inc(x_in, 16)
            act.dma_start(xres[0:NS_TOK, 4, :], a["x"][NP_TOK:NT]).then_inc(x_in, 16)

        act.dma_start(ident[:, :], a["ident"]).then_inc(const_in, 16)
        act.dma_start(memx[:, :, :], a["mem"].rearrange("(i p) d -> p i d", p=P)).then_inc(memx_in, 16)
        act.dma_start(gain[:, :], a["gains"][0]).then_inc(gain_in, 16)
        load_x()

        sums = [0]

        def squares(n_tiles, src, n, ready=None):
            act.wait_ge(ssq_clear, n + 1)
            for i in range(n_tiles):
                if ready is not None:
                    act.wait_ge(*ready[i])
                if sums[0]:
                    act.wait_ge(ssq_ready, sums[0])
                rows = ROWS[i]
                act.activation(sq[0:rows, :], src[0:rows, i, :], ACT.Square, accum_out=sm["ssq"][0:rows, i:i + 1])\
                   .then_inc(ssq_ready, 1)
                sums[0] += 1
            act.wait_ge(var_ready, n + 1)
            act.activation(sm["rstd"][:, 0:n_tiles], sm["rstd"][:, 0:n_tiles], ACT.Sqrt).then_inc(std_ready, 1)

        def high_parts(n_tiles):
            for i in range(n_tiles):
                for half in range(2):
                    b, _ = wait_filled()
                    act.activation(actH[:, half * 4:half * 4 + 4, T0[i]:T0[i] + ROWS[i]],
                                   bank(b, 4 * ROWS[i]).rearrange("p (k t) -> p k t", k=4), ACT.Copy)\
                       .then_inc(acth_done, 1)

        def next_gain(n, tiles):
            act.wait_ge(xn_ready, tiles)
            act.dma_start(gain[:, :], a["gains"][n]).then_inc(gain_in, 16)

        act.wait_ge(memx_in, 16)
        squares(MT, memx, 0)
        high_parts(MT)
        next_gain(1, MT)
        act.wait_ge(x_in, 32)
        squares(TILES, xres, 1)
        for q in range(N_CK * 4):
            b, value = wait_filled()
            act.activation(mk_sb[:, q, :], bank(b, MEM), ACT.Copy).then_inc(emptied[b], 1)
            act.wait_ge(emptied[b], value + 1)
        act.dma_start(o["mkT"].rearrange("(k p) m -> p k m", p=P), mk_sb[:, :, :]).then_inc(out_done, 16)
        for c in range(N_CV):
            for i in range(MT):
                b, value = wait_filled()
                act.activation(mv_sb[:, i, c * CHUNK:(c + 1) * CHUNK], bank(b), ACT.Copy).then_inc(emptied[b], 1)
                act.wait_ge(emptied[b], value + 1)
        act.dma_start(o["mv"].rearrange("(i p) d -> p i d", p=P), mv_sb[:, :, :]).then_inc(out_done, 16)
        high_parts(TILES)
        act.wait_ge(out_done, 32)
        act.wait_ge(xn_ready, MT + TILES)

        for s in range(2):
            act.dma_start(par[:, s, :], a["par"][s]).then_inc(par_in[s], 16)
        act.dma_start(lamp[:, :], a["lamp"]).then_inc(lamp_in, 16)
        act.dma_start(sm["gsub"], a["gsub"]).then_inc(lamp_in, 16)

        def projections(j, s, first=False, j_old=None, stored=None):
            if not first:
                act.wait_ge(conv_done, j_old + 1)
            for part in range(2):
                b, _ = wait_filled()
                if part == 0:
                    act.activation(rxp[:, s, 3:3 + HALF], bank(b, HALF), ACT.Copy).then_inc(emptied[b], 1)
                else:
                    act.activation(rxp[:, s, 3 + HALF:3 + NP_TOK], bank(b, NP_TOK - HALF), ACT.Copy)
                    act.activation(rxp[:, s, SEG + 3:XPW], ps[:, b * BANK + NP_TOK - HALF:b * BANK + HALF],
                                   ACT.Copy).then_inc(emptied[b], 1)
            if not first:
                act.wait_ge(yrec_ready, j_old + 1)
                act.dma_start(par[:, s, :], a["par"][j]).then_inc(par_in[s], 16)
            for dst, func in ((gel, ACT.Gelu), (sgr, ACT.Sigmoid), (sga, ACT.Sigmoid)):
                if dst is sga and not first:
                    act.wait_ge(sa_store[s], stored)
                for part in range(2):
                    b, value = wait_filled()
                    act.activation(dst[:, s, part * HALF:(part + 1) * HALF], bank(b, HALF), func).then_inc(emptied[b], 1)
                    if dst is sga:
                        act.wait_ge(emptied[b], value + 1)
            act.dma_start(sa_d[j], sga[:, s, :]).then_inc(sa_store[s], 16)

        def gate_block(j, s, first=False):
            for w, (dst, col) in enumerate(((gate_r, PAR_BA), (gate_i, PAR_BX))):
                for cut in (slice(0, CA_), slice(CA_, CW)):
                    b, value = wait_filled()
                    if w == 0 and cut.start == 0 and not first:
                        act.wait_ge(yrec_ready, j)
                    act.activation(dst[:, cut], ps[:, b * BANK:b * BANK + cut.stop - cut.start], ACT.Sigmoid,
                                   bias=par[:, s, col:col + 1]).then_inc(emptied[b], 1)
                    act.wait_ge(emptied[b], value + 1)
            if first:
                act.wait_ge(lam_ready, 1)
            act.activation(lru_a[:, 0:CW], gate_r[:, 0:CW], ACT.Exp, scale=sm["ncall"][:, bass.ds(j, 1)])\
               .then_inc(gate_ready, 1)
            act.activation(lru_t[:, 0:CW], gate_r[:, 0:CW], ACT.Tanh, scale=sm["pcall"][:, bass.ds(j, 1)])\
               .then_inc(gate_ready, 1)
            act.wait_ge(m_ready, j + 1)
            act.activation(lru_m[:, 0:CW], lru_m[:, 0:CW], ACT.Sqrt).then_inc(root_ready, 1)
            act.wait_ge(yrec_ready, j + 1)
            act.dma_start(r_d[j], yrec[:, s, :]).then_inc(r_store[s], 16)

        projections(0, 0, first=True)
        sp = sm["sp"]
        act.wait_ge(sp_neg, 1)
        act.activation(sp[:, 16:24], sp[:, 8:16], ACT.Exp, scale=-1.0).then_inc(sp_exp, 1)
        act.wait_ge(sp_one, 1)
        act.activation(sp[:, 32:40], sp[:, 24:32], ACT.Ln).then_inc(sp_ln, 1)
        act.wait_ge(lam_sums, 1)
        act.activation(sm["lamt"][:, 2:4], sm["lamt"][:, 0:2], ACT.Exp).then_inc(lam_exp, 1)
        projections(1, 1, first=True)
        gate_block(0, 0, first=True)
        with act.Fori(0, N_RG // 2 - 1) as i:
            turns.enter(i, 24)
            projections(i * 2 + 2, 0, j_old=i * 2, stored=i * 16 + 16)
            gate_block(i * 2 + 1, 1)
            projections(i * 2 + 3, 1, j_old=i * 2 + 1, stored=i * 16 + 16)
            gate_block(i * 2 + 2, 0)
            turns.leave(N_RG // 2 - 1)

        def turned(u):
            kind, c, i = TUNITS[u]
            if kind == "v":
                return
            n = sum(1 for k, _, _ in TUNITS[:u + 1] if k != "v")
            if kind == "k":
                act.wait_ge(rot_ready, n)
                act.dma_start(o["k"][T0[i]:T0[i] + ROWS[i], c * CHUNK:(c + 1) * CHUNK],
                              rot[0:ROWS[i], (n - 1) % 2, :]).then_inc(k_store[(n - 1) % 2], 16)
            b, _ = wait_filled()
            dst = kT if kind == "k" else qT
            act.activation(dst[:, 4 * c:4 * c + 4, T0[i]:T0[i] + ROWS[i]],
                           bank(b, 4 * ROWS[i]).rearrange("p (h t) -> p h t", h=4), ACT.Copy,
                           scale=1.0 if kind == "k" else DK ** -0.5).then_inc(emptied[b], 1)

        for u, (kind, c, i) in enumerate(TUNITS):
            if u == 0:
                skip(1)
                gate_block(N_RG - 1, 1)
                act.dma_start(o["cstate"], cstate[:, :, :]).then_inc(out_done, 16)
                act.dma_start(o["hstate"], hstate[:, :, :]).then_inc(out_done, 16)
                for s in range(2):
                    act.wait_ge(sa_store[s], 16 * N_RG // 2)
                    act.wait_ge(r_store[s], 16 * N_RG // 2)
                act.wait_ge(out_done, 64)
                for name, t in (("ropec", ropec), ("ropes", ropes), ("ropen", ropen)):
                    act.dma_start(t[:, :, :], a[name]).then_inc(rope_in, 16)
                act.dma_start(mask[0:1, :], a["mask"]).then_inc(mask_in, 16)
                continue
            if kind == "v":
                b, value = wait_filled()
                act.activation(vtok[0:ROWS[i], i, c * CHUNK:(c + 1) * CHUNK], bank(b, CHUNK, ROWS[i]),
                               ACT.Copy).then_inc(emptied[b], 1)
                if (c, i) == (1, TILES - 1):
                    act.wait_ge(emptied[b], value + 1)
                    act.dma_start(o["v"][0:NP_TOK].rearrange("(i p) d -> p i d", p=P), vtok[:, 0:4, :])\
                       .then_inc(out_done, 16)
                    act.dma_start(o["v"][NP_TOK:NT], vtok[0:NS_TOK, 4, :]).then_inc(out_done, 16)
            else:
                skip(1)
            turned(u - 1)
        turned(len(TUNITS) - 1)
        for s in range(2):
            act.wait_ge(k_store[s], 16 * TILES)

        def load_merge(i):
            t = slice(T0[i], T0[i] + ROWS[i])
            act.dma_start(sat[:, :, 0:ROWS[i]], sa_d[:, :, t].rearrange("k p t -> p k t")).then_inc(sat_in, 16)
            act.dma_start(rt[:, :, 0:ROWS[i]], r_d[:, :, t].rearrange("k p t -> p k t")).then_inc(sat_in, 16)

        def load_cache(h):
            act.dma_start(ckv0[:, 0, :], a["ckT"][h]).then_inc(ckv_in, 16)
            act.dma_start(ckv0[:, 1, :].rearrange("p (k d) -> p k d", k=4),
                          a["cv"][:, :, h * DV:(h + 1) * DV]).then_inc(ckv_in, 16)

        def exps(u):
            i, h = UNITS[u]
            rows = ROWS[i]
            act.wait_ge(nm_ready, u + 1)
            if u >= 2:
                act.wait_ge(t_ready, u - 1 if i < TILES - 1 else u)
            for s in range(2):
                if i < TILES - 1:
                    n = P * (i + 1)
                    dst, src = prob[:, u % 2, s, 0:n], bank(2 * (u % 2) + s, n)
                else:
                    dst, src = probs[0:rows, s, :], ps[0:rows, 2 * s * BANK:2 * s * BANK + NT]
                col = 2 * (u % 2) + s
                ins = act.activation(dst, src, ACT.Exp, bias=sm["nmax"][0:rows, col:col + 1],
                                     accum_out=sm["z"][0:rows, col:col + 1])
            ins.then_inc(p_ready, 1)

        def copy_turned(u):
            i, h = UNITS[u]
            rows = ROWS[i]
            b = 4 + u % 2
            act.wait_ge(t_ready, u + 1)
            if u >= 2:
                act.wait_ge(pv_done, u - 1)
            if i < TILES - 1:
                n = P * (i + 1)
                act.activation(aT[:, u % 2, 0:n], bank(b, n), ACT.Copy).then_inc(aT_ready, 1)
            else:
                n = (PAST // P) * rows
                act.activation(aT[:, u % 2, 0:n], bank(b, n), ACT.Copy)
                act.activation(aT[0:rows, u % 2, n:n + rows], ps[0:rows, b * BANK + n:b * BANK + n + rows],
                               ACT.Copy).then_inc(aT_ready, 1)

        for i in range(TILES):
            rows = ROWS[i]
            load_merge(i)
            if i == TILES - 1:
                load_cache(0)
            for h in range(HEADS):
                u = i * HEADS + h
                exps(u)
                if i == TILES - 1:
                    copy_turned(u)
                    if h + 1 < HEADS:
                        act.wait_ge(pv_done, u + 1)
                        load_cache(h + 1)
                elif h > 0:
                    copy_turned(u - 1)
            if i < TILES - 1:
                copy_turned(i * HEADS + HEADS - 1)
            act.wait_ge(pv_done, HEADS * (i + 1))
            act.activation(osb[0:rows, :], ps[0:rows, 6 * BANK:8 * BANK], ACT.Copy).then_inc(osb_ready, 1)
            act.wait_ge(ovar_ready, i + 1)
            act.activation(sm["orstd"][0:rows, :], sm["orstd"][0:rows, :], ACT.Sqrt).then_inc(ostd_ready, 1)
            act.wait_ge(merged, i + 1)
            act.activation(actH[:, :, T0[i]:T0[i] + rows], sat[:, :, 0:rows], ACT.Copy).then_inc(mh_done, 1)
            act.wait_ge(ml_done, i + 1)

        act.wait_ge(out_done, 96)
        load_x()
        next_gain(2, MT + TILES)

        def sums_of(n_groups):
            groups = [turns.take() for _ in range(n_groups * TILES)]
            return [(emptied[b], value + 1) for b, value in groups[-TILES:]]

        ready = sums_of(N_OUT)
        squares(TILES, xres, 2, ready)
        high_parts(TILES)
        next_gain(3, MT + 2 * TILES)
        act.dma_start(mkT[:, 0, :, :], o["mkT"].rearrange("(k p) m -> p k m", p=P)).then_inc(mem_in, 16)
        act.dma_start(mkT[:, 1, :, :], a["cmkT"].rearrange("(k p) m -> p k m", p=P)).then_inc(mem_in, 16)
        act.dma_start(mvt[:, 0, :, :], o["mv"].rearrange("(i p) d -> p i d", p=P)).then_inc(mem_in, 16)
        act.dma_start(mvt[:, 1, :, :], a["cmv"].rearrange("(i p) d -> p i d", p=P)).then_inc(mem_in, 16)
        for q in range(N_CQ * 4):
            for part in range(2):
                b, _ = wait_filled()
                act.activation(qcT[:, q, part * HALF:(part + 1) * HALF], bank(b, HALF), ACT.Copy,
                               scale=CA_DH ** -0.5).then_inc(emptied[b], 1)

        def cross_exps(i):
            rows = ROWS[i]
            act.wait_ge(cm_ready, i + 1)
            if i >= 2:
                act.wait_ge(ct_ready, i - 1)
            for h in range(CA_HEADS):
                c = 4 * (i % 2) + h
                at = 2 * (i % 2) * BANK + h * MEM
                ins = act.activation(cp[0:rows, i % 2, h * MEM:(h + 1) * MEM], ps[0:rows, at:at + MEM],
                                     ACT.Exp, bias=sm["nmax"][0:rows, c:c + 1], accum_out=sm["mz"][0:rows, c:c + 1])
            ins.then_inc(ce_ready, 1)

        cross_exps(0)
        for i in range(TILES):
            rows = ROWS[i]
            if i + 1 < TILES:
                cross_exps(i + 1)
            act.wait_ge(ct_ready, i + 1)
            if i >= 1:
                act.wait_ge(co_ready, i)
            for m in range(2):
                ins = act.activation(cpT[:, m * 4 * rows:(m + 1) * 4 * rows], bank(4 + m, 4 * rows), ACT.Copy)
            ins.then_inc(cpT_ready, 1)
            act.wait_ge(co_ready, i + 1)
            for m in range(2):
                act.activation(actH[:, 4 * m:4 * m + 4, T0[i]:T0[i] + rows],
                               bank(6 + m, 4 * rows).rearrange("p (k t) -> p k t", k=4), ACT.Copy).then_inc(ch_done, 1)

        ready = sums_of(N_CO)
        squares(TILES, xres, 3, ready)
        act.dma_start(x2_d[0:NP_TOK].rearrange("(i p) d -> p i d", p=P), xres[:, 0:4, :]).then_inc(x2_store, 16)
        act.dma_start(x2_d[NP_TOK:NT], xres[0:NS_TOK, 4, :]).then_inc(x2_store, 16)
        high_parts(TILES)
        next_gain(4, MT + 3 * TILES)
        act.dma_start(keys[:, :, :], a["keysT"]).then_inc(keys_in, 16)
        act.wait_ge(x2_store, 32)
        for q in range(N_PQ * 4):
            for part in range(2):
                b, _ = wait_filled()
                act.activation(pqT[:, q, part * HALF:(part + 1) * HALF], bank(b, HALF), ACT.Copy)\
                   .then_inc(emptied[b], 1)
        act.dma_start(iota16[:, :], a["iota"][:, 0:TOPK]).then_inc(iota16_in, 16)

        for i in range(TILES):
            rows = ROWS[i]
            act.wait_ge(score_ready, i + 1)
            if i >= 1:
                act.wait_ge(ssb_used, i)
            act.activation(ssb[0:rows, :, :].rearrange("p h n -> p (h n)"), ps[0:rows, 0:4 * BANK], ACT.Copy)\
               .then_inc(ssb_ready, 1)
            act.wait_ge(gexp_in, i + 1)
            act.activation(chosen[0:rows, 2, :], chosen[0:rows, 2, :], ACT.Exp).then_inc(gexp_out, 1)
            act.wait_ge(chT_ready, i + 1)
            act.activation(chosenT[:, :, T0[i]:T0[i] + rows],
                           ps[:, 4 * BANK:4 * BANK + 3 * P].rearrange("p (s t) -> p s t", s=3)[:, :, 0:rows],
                           ACT.Copy).then_inc(chT_copied, 1)
        act.dma_start(iota[:, :], a["iota"]).then_inc(iota_in, 16)

        act.sem_inc(c_copied, BANKS)

        def c_block(block_no, s, base, stored):
            if stored is not None:
                act.wait_ge(c_store[s], stored)
            for q in range(TB // 4):
                act.wait_ge(c_filled, base + (q + 3))
                act.activation(cst[:, s, :, 4 * q:4 * q + 4], bank((s * (TB // 4) + q) % BANKS).rearrange(
                    "p (t e) -> p e t", t=4), ACT.Copy).then_inc(c_copied, 1)
            act.wait_ge(c_copied, base + (BANKS + TB // 4))
            act.dma_start(c_d[block_no], cst[:, s, :, :]).then_inc(c_store[s], 16)

        for s in range(2):
            c_block(s, s, s * (TB // 4), None)
        with act.Fori(0, TBN // 2 - 1) as i:
            for s in range(2):
                c_block(i * 2 + (2 + s), s, i * (TB // 2) + (s + 2) * (TB // 4), i * 16 + 16)
        for s in range(2):
            act.wait_ge(c_store[s], 16 * TBN // 2)

        act.sem_inc(ge_ready, 2)
        act.sem_inc(gh_done, 2)

        def gelu_and_high(e, s, n, used):
            act.wait_ge(u_done, n + 1)
            act.wait_ge(gf_ready, n + 1)
            act.activation(ge[:, e % 2, :].rearrange("p (c n) -> p c n", c=2), halves(2 * (e % 2)), ACT.Gelu)\
               .then_inc(ge_ready, 1)
            act.wait_ge(gf_ready, n + 3)
            if used is not None:
                act.wait_ge(v_done, used)
            act.activation(gH[:, s, e, :], gf[:, e % 2, :], ACT.Copy).then_inc(gh_done, 1)

        for n in range(2 * EG):
            gelu_and_high(n % EG, n // EG, n, None)
        with act.Fori(0, GROUPS // 2 - 1) as i:
            for s in range(2):
                for e in range(EG):
                    gelu_and_high(e, s, i * (2 * EG) + (EG * (s + 2) + e), i * (2 * KT) + KT * (s + 1))

        act.wait_ge(v_done, KT * GROUPS)
        act.wait_ge(gl_done, EG * GROUPS)
        act.dma_start(x2b[:, 0:4, :], x2_d[0:NP_TOK].rearrange("(i p) d -> p i d", p=P)).then_inc(x2_in, 16)
        act.dma_start(x2b[0:NS_TOK, 4, :], x2_d[NP_TOK:NT]).then_inc(x2_in, 16)
        for i in range(TILES):
            rows = ROWS[i]
            act.wait_ge(res_ready, i + 1)
            if i >= 2:
                act.wait_ge(y_store[i % 2], 16 * (i // 2))
            act.activation(yout[0:rows, i % 2, :], x2b[0:rows, i, :], ACT.Square,
                           accum_out=sm["ssq"][0:rows, i:i + 1]).then_inc(ssq_ready, 1)
            act.wait_ge(var_ready, 4 + i + 1)
            act.activation(sm["rstd"][0:rows, i:i + 1], sm["rstd"][0:rows, i:i + 1], ACT.Sqrt).then_inc(std_ready, 1)
            act.wait_ge(y_ready, i + 1)
            act.dma_start(o["y"][T0[i]:T0[i] + rows, :], yout[0:rows, i % 2, :]).then_inc(y_store[i % 2], 16)
        for s in range(2):
            act.wait_ge(y_store[s], 16 * ((TILES + 1 - s) // 2))

    @block.vector
    def _(ve):
        turns = Turns()
        step = Steps(ve, ve_step)

        def wait_filled():
            b, value = turns.take()
            ve.wait_ge(filled[b], value)
            return b, value

        def skip(n):
            for _ in range(n):
                turns.take()

        xn_groups = []
        sums = [0]

        def normalise(n_tiles, src, n):
            first = len(xn_groups)
            rstd = sm["rstd"][:, 0:n_tiles]
            step.done(ve.memset(sm["ssq"], 0.0))
            ve.sem_inc(ssq_clear, 1)
            sums[0] += n_tiles
            ve.wait_ge(ssq_ready, sums[0])
            ve.tensor_scalar(rstd, sm["ssq"][:, 0:n_tiles], 1.0 / D, RMS_EPS, ALU.mult, ALU.add).then_inc(var_ready, 1)
            ve.wait_ge(std_ready, n + 1)
            step.done(ve.reciprocal(rstd, rstd))
            ve.wait_ge(gain_in, 16 * (n + 1))
            for i in range(n_tiles):
                if first + i >= 2:
                    b, value = xn_groups[first + i - 2]
                    ve.wait_ge(filled[b], value)
                rows = ROWS[i]
                ve.scalar_tensor_tensor(xn[0:rows, (first + i) % 2, :], src[0:rows, i, :], sm["rstd"][0:rows, i:i + 1],
                                        gain[0:rows, :], ALU.mult, ALU.mult).then_inc(xn_ready, 1)
                if n == 1 and i == 0:
                    skip(N_CK * 4 + N_CV * MT)
                take = [turns.take(), turns.take()]
                xn_groups.append(take[1])
                todo.append((first + i, i, take))
                if i >= 1:
                    low_parts(*todo.pop(0))
            low_parts(*todo.pop(0))

        todo = []

        def low_parts(tile, i, take):
            for half, (b, value) in enumerate(take):
                ve.wait_ge(acth_done, 2 * tile + half + 1)
                cut = (slice(None), slice(half * 4, half * 4 + 4), slice(T0[i], T0[i] + ROWS[i]))
                ve.tensor_tensor(actL[cut], bank(b, 4 * ROWS[i]).rearrange("p (k t) -> p k t", k=4),
                                 actH[cut].bitcast(F32), ALU.subtract).then_inc(emptied[b], 1)

        normalise(MT, memx, 0)
        normalise(TILES, xres, 1)

        sp, lamt, lamv = sm["sp"], sm["lamt"], sm["lamv"]
        neg, mag, exp_, one, log = (sp[:, 8 * k:8 * k + 8] for k in range(5))
        ve.wait_ge(lamp_in, 32)
        step.done(ve.tensor_scalar(neg, lamp[:, 4 * DK:4 * DK + KT], -1.0, None, ALU.mult))
        ve.tensor_tensor(mag, neg, lamp[:, 4 * DK:4 * DK + KT], ALU.max).then_inc(sp_neg, 1)
        ve.wait_ge(sp_exp, 1)
        ve.tensor_scalar(one, exp_, 1.0, None, ALU.add).then_inc(sp_one, 1)
        for k in range(2):
            step.done(ve.tensor_tensor(lamp[:, 2 * k * DK:(2 * k + 1) * DK], lamp[:, 2 * k * DK:(2 * k + 1) * DK],
                                       lamp[:, (2 * k + 1) * DK:(2 * k + 2) * DK], ALU.mult))
        step.done(ve.tensor_reduce(lamt[:, 0:1], lamp[:, 0:DK], AX, ALU.add))
        ve.tensor_reduce(lamt[:, 1:2], lamp[:, 2 * DK:3 * DK], AX, ALU.add).then_inc(lam_sums, 1)
        ve.wait_ge(sp_ln, 1)
        step.done(ve.tensor_scalar(mag, one, -1.0, None, ALU.add))
        step.done(ve.tensor_scalar(one, mag, 0.0, None, ALU.is_equal))
        step.done(ve.tensor_scalar(mag, mag, 1e-30, None, ALU.max))
        step.done(ve.reciprocal(mag, mag))
        step.done(ve.tensor_tensor(mag, mag, log, ALU.mult))
        step.done(ve.tensor_tensor(mag, mag, exp_, ALU.mult))
        step.done(ve.tensor_tensor(exp_, exp_, one, ALU.mult))
        step.done(ve.tensor_tensor(mag, mag, exp_, ALU.add))
        step.done(ve.tensor_scalar(neg, neg, 0.0, None, ALU.max))
        step.done(ve.tensor_tensor(neg, neg, mag, ALU.add))
        step.done(ve.tensor_scalar(sm["pcall"], neg, RG_C, None, ALU.mult))
        ve.wait_ge(lam_exp, 1)
        step.done(ve.tensor_tensor(lamt[:, 4:5], lamt[:, 2:3], lamt[:, 3:4], ALU.subtract))
        step.done(ve.tensor_scalar(lamv[:, 1:2], lamt[:, 4:5], LAM_INIT, -1.0, ALU.add, ALU.mult))
        step.done(ve.memset(lamv[:, 0:1], 1.0))
        step.done(ve.tensor_scalar(sm["gsub"], sm["gsub"], 1.0 - LAM_INIT, None, ALU.mult))
        for s in range(2):
            step.done(ve.memset(rxp[:, s, 0:CONVW - 1], 0.0))
        ve.tensor_scalar(sm["ncall"], neg, -RG_C, None, ALU.mult).then_inc(lam_ready, 1)

        def convolve(j, s, arrived, j_old=None):
            groups = [turns.take(), turns.take()]
            ve.wait_ge(par_in[s], arrived)
            if j_old is not None:
                ve.wait_ge(yrec_ready, j_old + 1)
            step.done(ve.tensor_copy(rxp[:, s, SEG:SEG + 3], par[:, s, PAR_SC:PAR_SC + 3]))
            for b, value in groups:
                ve.wait_ge(emptied[b], value + 1)
            step.done(ve.tensor_copy(cstate[:, bass.ds(j, 1), 0:3], rxp[:, s:s + 1, NP_TOK:NP_TOK + 3]))
            step.done(ve.tensor_copy(cstate[:, bass.ds(j, 1), 3:6], rxp[:, s:s + 1, SEG + NS_TOK:SEG + NS_TOK + 3]))
            step.done(ve.tensor_scalar(conv[:, s, 0:CW], rxp[:, s, 0:CW], par[:, s, PAR_CW:PAR_CW + 1],
                                       par[:, s, PAR_CB:PAR_CB + 1], ALU.mult, ALU.add))
            for w in range(1, CONVW):
                ins = ve.scalar_tensor_tensor(conv[:, s, 0:CW], rxp[:, s, w:w + CW], par[:, s, PAR_CW + w:PAR_CW + w + 1],
                                              conv[:, s, 0:CW], ALU.mult, ALU.add)
                if w < CONVW - 1:
                    step.done(ins)
            ins.then_inc(conv_done, 1)
            skip(6)

        def recur(j, s, stored=None):
            skip(4)
            ve.wait_ge(gate_ready, j * 2 + 2)
            step.done(ve.tensor_scalar(lru_m[:, 0:CW], lru_t[:, 0:CW], 1.0, None, ALU.add))
            step.done(ve.reciprocal(lru_m[:, 0:CW], lru_m[:, 0:CW]))
            ve.scalar_tensor_tensor(lru_m[:, 0:CW], lru_t[:, 0:CW], 2.0, lru_m[:, 0:CW], ALU.mult, ALU.mult)\
              .then_inc(m_ready, 1)
            step.done(ve.tensor_tensor(gate_i[:, 0:CW], gate_i[:, 0:CW], conv[:, s, 0:CW], ALU.mult))
            ve.wait_ge(root_ready, j + 1)
            step.done(ve.tensor_tensor(gate_i[:, 0:CW], gate_i[:, 0:CW], lru_m[:, 0:CW], ALU.mult))
            step.done(ve.tensor_tensor_scan(lru_h[:, 0:NP_TOK], lru_a[:, 0:NP_TOK], gate_i[:, 0:NP_TOK], 0.0,
                                            ALU.mult, ALU.add))
            step.done(ve.tensor_tensor_scan(lru_h[:, NP_TOK:NT], lru_a[:, SEG:CW], gate_i[:, SEG:CW],
                                            par[:, s, PAR_H0:PAR_H0 + 1], ALU.mult, ALU.add))
            step.done(ve.tensor_copy(hstate[:, bass.ds(j, 1), 0:1], lru_h[:, NP_TOK - 1:NP_TOK].unsqueeze(1)))
            step.done(ve.tensor_copy(hstate[:, bass.ds(j, 1), 1:2], lru_h[:, NT - 1:NT].unsqueeze(1)))
            step.done(ve.tensor_tensor(lru_h[:, :], lru_h[:, :], gel[:, s, :], ALU.mult))
            if stored is not None:
                ve.wait_ge(r_store[s], stored)
            ve.tensor_tensor(yrec[:, s, :], lru_h[:, :], sgr[:, s, :], ALU.mult).then_inc(yrec_ready, 1)
            ve.wait_ge(yrec_ready, j + 1)

        convolve(0, 0, 16)
        convolve(1, 1, 16)
        recur(0, 0)
        with ve.Fori(0, N_RG // 2 - 1) as i:
            turns.enter(i, 24)
            step.enter(i, 2 * (3 + CONVW - 1 + 1 + 8))
            convolve(i * 2 + 2, 0, i * 16 + 32, i * 2)
            recur(i * 2 + 1, 1, None)
            convolve(i * 2 + 3, 1, i * 16 + 32, i * 2 + 1)
            recur(i * 2 + 2, 0, i * 16 + 16)
            turns.leave(N_RG // 2 - 1)
            step.leave(N_RG // 2 - 1)

        rots = []
        turned_groups = {}

        def turned(u):
            if TUNITS[u][0] != "v":
                turned_groups[u] = turns.take()

        for u, (kind, c, i) in enumerate(TUNITS):
            b, value = turns.take()
            if u == 0:
                recur(N_RG - 1, 1, None)
                ve.wait_ge(rope_in, 48)
            if kind != "v":
                rows, r = ROWS[i], len(rots) % 2
                ve.wait_ge(filled[b], value)
                src = bank(b, CHUNK, rows).rearrange("p (h s n) -> p h s n", s=2, n=32)
                r1 = rot1[0:rows, :].rearrange("p (h s n) -> p h s n", s=2, n=32)
                r2 = rot2[0:rows, :].rearrange("p (h s n) -> p h s n", s=2, n=32)
                heads = [rows, CHUNK // DK, 32]
                if rots:
                    ve.wait_ge(rot_ready, len(rots))
                ve.tensor_tensor(rot1[0:rows, :].rearrange("p (h n) -> p h n", n=32),
                                 bank(b, CHUNK, rows).rearrange("p (h n) -> p h n", n=32),
                                 ropec[0:rows, i:i + 1, :].broadcast_to([rows, CHUNK // 32, 32]), ALU.mult)
                ve.tensor_tensor(r2[:, :, 0, :], src[:, :, 1, :], ropen[0:rows, i:i + 1, :].broadcast_to(heads), ALU.mult)
                ve.tensor_tensor(r2[:, :, 1, :], src[:, :, 0, :], ropes[0:rows, i:i + 1, :].broadcast_to(heads), ALU.mult)\
                  .then_inc(emptied[b], 1)
                ve.wait_ge(emptied[b], value + 1)
                if len(rots) >= 2:
                    before = rots[-2]
                    tb, tv = turned_groups[before]
                    ve.wait_ge(filled[tb], tv)
                    if TUNITS[before][0] == "k":
                        ve.wait_ge(k_store[r], 16 * ((len(rots) - 2) // 2 + 1))
                ve.tensor_tensor(rot[0:rows, r, :], rot1[0:rows, :], rot2[0:rows, :], ALU.add).then_inc(rot_ready, 1)
                rots.append(u)
            if u >= 1:
                turned(u - 1)
        turned(len(TUNITS) - 1)

        def maxima(u):
            i, h = UNITS[u]
            rows = ROWS[i]
            ve.wait_ge(sc_ready, u + 1)
            if u >= 2:
                ve.wait_ge(p_ready, u - 1)
            if i < TILES - 1:
                n = P * (i + 1)
                src = ps[:, 2 * (u % 2) * BANK:(2 * (u % 2) + 2) * BANK].rearrange("p (s n) -> p s n", s=2)[:, :, 0:n]
            else:
                src = ps[0:rows, 0:4 * BANK].rearrange("p (s n) -> p s n", s=2)[:, :, 0:NT]
            ve.tensor_reduce(sm["nmax"][0:rows, 2 * (u % 2):2 * (u % 2) + 2], src, AX, ALU.max, negate=True)\
              .then_inc(nm_ready, 1)

        def combine(u):
            i, h = UNITS[u]
            rows = ROWS[i]
            if i < TILES - 1:
                p1, p2 = (prob[:, u % 2, s, 0:P * (i + 1)] for s in range(2))
            else:
                p1, p2 = (probs[0:rows, s, :] for s in range(2))
            rz = sm["pk"][0:rows, 0:2]
            ve.wait_ge(p_ready, u + 1)
            if u >= 1:
                ve.wait_ge(a_ready, u)
            step.done(ve.reciprocal(rz, sm["z"][0:rows, 2 * (u % 2):2 * (u % 2) + 2]))
            step.done(ve.tensor_tensor(rz, rz, lamv[0:rows, :], ALU.mult))
            step.done(ve.tensor_scalar(p2, p2, rz[:, 1:2], None, ALU.mult))
            ve.scalar_tensor_tensor(p1, p1, rz[:, 0:1], p2, ALU.mult, ALU.add).then_inc(a_ready, 1)

        for i in range(TILES):
            rows = ROWS[i]
            for h in range(HEADS):
                u = i * HEADS + h
                maxima(u)
                if i == TILES - 1:
                    combine(u)
                elif h > 0:
                    combine(u - 1)
            if i < TILES - 1:
                combine(i * HEADS + HEADS - 1)
            ve.wait_ge(osb_ready, i + 1)
            step.done(ve.tensor_tensor(osq[0:rows, :], osb[0:rows, :], osb[0:rows, :], ALU.mult))
            step.done(ve.tensor_reduce(sm["oss"][0:rows, :], osq[0:rows, :].rearrange("p (h d) -> p h d", h=HEADS),
                                       AX, ALU.add))
            ve.tensor_scalar(sm["orstd"][0:rows, :], sm["oss"][0:rows, :], 1.0 / DV, SUBLN_EPS, ALU.mult, ALU.add)\
              .then_inc(ovar_ready, 1)
            ve.wait_ge(ostd_ready, i + 1)
            step.done(ve.reciprocal(sm["orstd"][0:rows, :], sm["orstd"][0:rows, :]))
            heads = osb[0:rows, :].rearrange("p (h d) -> p h d", h=HEADS)
            ve.tensor_tensor(heads, heads, sm["orstd"][0:rows, :].unsqueeze(2).broadcast_to([rows, HEADS, DV]),
                             ALU.mult).then_inc(on_ready, 1)
            ve.wait_ge(yt_ready, i + 1)
            ve.wait_ge(sat_in, 32 * (i + 1))
            for m in range(2):
                part = sat[:, 4 * m:4 * m + 4, 0:rows]
                step.done(ve.scalar_tensor_tensor(part, bank(4 + m, 4 * rows).rearrange("p (k t) -> p k t", k=4),
                                                  sm["gsub"], part, ALU.mult, ALU.mult))
            ve.tensor_tensor(sat[:, :, 0:rows], sat[:, :, 0:rows], rt[:, :, 0:rows], ALU.add).then_inc(merged, 1)
            ve.wait_ge(mh_done, i + 1)
            t = slice(T0[i], T0[i] + rows)
            ve.tensor_tensor(actL[:, :, t], sat[:, :, 0:rows], actH[:, :, t].bitcast(F32), ALU.subtract)\
              .then_inc(ml_done, 1)

        def add_products():
            for c in range(2):
                for i in range(TILES):
                    b, _ = wait_filled()
                    part = xres[0:ROWS[i], i, c * CHUNK:(c + 1) * CHUNK]
                    ve.tensor_tensor(part, part, bank(b, CHUNK, ROWS[i]), ALU.add).then_inc(emptied[b], 1)

        ve.wait_ge(x_in, 64)
        add_products()
        normalise(TILES, xres, 2)
        skip(N_CQ * 8)

        def cross_maxima(i):
            ve.wait_ge(cs_ready, i + 1)
            if i >= 2:
                ve.wait_ge(ce_ready, i - 1)
            rows, at = ROWS[i], 2 * (i % 2) * BANK
            ve.tensor_reduce(sm["nmax"][0:rows, 4 * (i % 2):4 * (i % 2) + 4],
                             ps[0:rows, at:at + 2 * BANK].rearrange("p (h n) -> p h n", h=CA_HEADS), AX, ALU.max,
                             negate=True).then_inc(cm_ready, 1)

        cross_maxima(0)
        for i in range(TILES):
            rows = ROWS[i]
            if i + 1 < TILES:
                cross_maxima(i + 1)
            ve.wait_ge(ce_ready, i + 1)
            if i >= 1:
                ve.wait_ge(cn_ready, i)
            rz = sm["pk"][0:rows, 0:4]
            step.done(ve.reciprocal(rz, sm["mz"][0:rows, 4 * (i % 2):4 * (i % 2) + 4]))
            heads = cp[0:rows, i % 2, :].rearrange("p (h n) -> p h n", h=CA_HEADS)
            ve.tensor_tensor(heads, heads, rz.unsqueeze(2).broadcast_to([rows, CA_HEADS, MEM]), ALU.mult)\
              .then_inc(cn_ready, 1)
            for m in range(2):
                ve.wait_ge(ch_done, 2 * i + m + 1)
                cut = (slice(None), slice(4 * m, 4 * m + 4), slice(T0[i], T0[i] + rows))
                ve.tensor_tensor(actL[cut], bank(6 + m, 4 * rows).rearrange("p (k t) -> p k t", k=4),
                                 actH[cut].bitcast(F32), ALU.subtract).then_inc(cl_done, 1)
        add_products()
        normalise(TILES, xres, 3)
        skip(N_PQ * 8)

        S2 = 2 * PK_HEADS
        halves_of = work[:, :].rearrange("p (s n) -> p s n", s=S2)
        sums_of = cand[:, :].rearrange("p (h n) -> p h n", h=PK_HEADS)
        rest_of = work[:, :].rearrange("p (h n) -> p h n", h=PK_HEADS)

        def best_of(n, values, rest, best_values, best_places, rows, used=None):
            for s in range(n):
                ins = ve.max(best_values[0:rows, s, 0:8], values[0:rows, s, :])
            step.done(ins)
            for s in range(n):
                ve.match_replace(rest[0:rows, s, :], best_values[0:rows, s, 0:8], values[0:rows, s, :], NEG)
                ins = ve.max_index(best_places[0:rows, s, 0:8], best_values[0:rows, s, 0:8], values[0:rows, s, :])
            step.done(ins)
            for s in range(n):
                ins = ve.max(best_values[0:rows, s, 8:16], rest[0:rows, s, :])
            step.done(ins)
            for s in range(n):
                ins = ve.max_index(best_places[0:rows, s, 8:16], best_values[0:rows, s, 8:16], rest[0:rows, s, :])
            step.done(ins)

        ve.wait_ge(iota16_in, 16)
        for i in range(TILES):
            rows = ROWS[i]
            ve.wait_ge(ssb_ready, i + 1)
            best_of(S2, ssb, halves_of, top, topi, rows)
            ve.sem_inc(ssb_used, 1)
            step.done(ve.tensor_copy(topf[0:rows, :, :], topi[0:rows, :, :]))
            square = [rows, TOPK, TOPK]
            for h in range(PK_HEADS):
                ins = ve.tensor_tensor(sums_of[0:rows, h, :].rearrange("p (x y) -> p x y", y=TOPK),
                                       top[0:rows, 2 * h, :].unsqueeze(2).broadcast_to(square),
                                       top[0:rows, 2 * h + 1, :].unsqueeze(1).broadcast_to(square), ALU.add)
            step.done(ins)
            best_of(PK_HEADS, sums_of, rest_of, best, besti, rows)
            step.done(ve.tensor_scalar(bestr[0:rows, 0], besti[0:rows], 4, None, ALU.logical_shift_right))
            step.done(ve.tensor_scalar(bestr[0:rows, 1], besti[0:rows], TOPK - 1, None, ALU.bitwise_and))
            step.done(ve.tensor_copy(bestf[0:rows].rearrange("p r h t -> p (r h t)"),
                                     bestr[0:rows].rearrange("p r h t -> p (r h t)")))
            if i >= 1:
                ve.wait_ge(chT_ready, i)
            g = chosen[0:rows, 2, :].rearrange("p (h t) -> p h t", t=TOPK)
            ve.tensor_tensor(g, best[0:rows], best[0:rows, :, 0:1].broadcast_to([rows, PK_HEADS, TOPK]), ALU.subtract)\
              .then_inc(gexp_in, 1)
            for half in range(2):
                for h in range(PK_HEADS):
                    k = h % 4
                    hit = pick[0:rows, k * TOPK * TOPK:(k + 1) * TOPK * TOPK].rearrange("p (t j) -> p t j", j=TOPK)
                    step.done(ve.tensor_tensor(hit, bestf[0:rows, half, h, :].unsqueeze(2).broadcast_to(square),
                                               iota16[0:rows, :].unsqueeze(1).broadcast_to(square), ALU.is_equal))
                    step.done(ve.tensor_tensor(hit, hit, topf[0:rows, 2 * h + half, :].unsqueeze(1)
                                               .broadcast_to(square), ALU.mult))
                    step.done(ve.tensor_reduce(chosen[0:rows, half, h * TOPK:(h + 1) * TOPK], hit, AX, ALU.add))
            ve.wait_ge(gexp_out, i + 1)
            total = sm["pk"][0:rows, 8:16]
            step.done(ve.tensor_reduce(total, g, AX, ALU.add))
            step.done(ve.reciprocal(total, total))
            ve.tensor_tensor(g, g, total.unsqueeze(2).broadcast_to([rows, PK_HEADS, TOPK]), ALU.mult)\
              .then_inc(chosen_ready, 1)

        ve.wait_ge(iota_in, 16)
        ve.wait_ge(chT_copied, TILES)
        with ve.Fori(0, NT // 8) as i:
            for s in range(2):
                ve.wait_ge(c_filled, i * 2 + (s + 1))
                for t in range(4):
                    tok = bass.ds(i * 8 + (4 * s + t), 1)
                    ve.tensor_scalar(hot1[:, s, t, :], iota[:, :], chosenT[:, 0, tok], None, ALU.is_equal)
                    ins = ve.tensor_scalar(hot2[:, s, t, :], iota[:, :], chosenT[:, 1, tok], chosenT[:, 2, tok],
                                           ALU.is_equal, ALU.mult)
                ins.then_inc(hot_ready, 1)

        for s in range(2):
            ve.wait_ge(c_store[s], 16 * TBN // 2)
        step.done(ve.memset(acc[:, :, :], 0.0))
        ve.sem_inc(gf_ready, 2)
        ve.sem_inc(acc_added, 2)

        def weigh(e, s, n, c_arrived):
            ve.wait_ge(ge_ready, n + 3)
            ve.wait_ge(gh_done, n + 1)
            if e == 0:
                ve.wait_ge(c_in[s], c_arrived)
            ve.tensor_tensor(gf[:, e % 2, :].rearrange("p (b t) -> p b t", t=TB),
                             ge[:, e % 2, :].rearrange("p (b t) -> p b t", t=TB), cg[:, s, :, e, :], ALU.mult)\
              .then_inc(gf_ready, 1)
            ve.wait_ge(gh_done, n + 3)
            ve.tensor_tensor(gL[:, s, e, :], gf[:, e % 2, :], gH[:, s, e, :].bitcast(F32), ALU.subtract)\
              .then_inc(gl_done, 1)
            ve.wait_ge(gl_done, n + 1)

        def add_down(d, m):
            ve.wait_ge(v_done, m + 1)
            part = acc[:, d, :].rearrange("p (c n) -> p c n", c=2)
            ve.tensor_tensor(part, part, halves(4 + 2 * (d % 2)), ALU.add).then_inc(acc_added, 1)

        for e in range(EG):
            weigh(e, 0, e, 16)
        ve.sem_inc(c_used, 1)
        with ve.Fori(0, GROUPS // 2 - 1) as i:
            for s in range(2):
                for e in range(EG):
                    weigh(e, 1 - s, i * (2 * EG) + (EG * (s + 1) + e), i * 16 + (16 if s == 0 else 32))
                ve.sem_inc(c_used, 1)
                for d in range(KT):
                    add_down(d, i * (2 * KT) + (KT * s + d))
        for e in range(EG):
            weigh(e, 1, EG * (GROUPS - 1) + e, 16 * (GROUPS // 2))
        for m in range(KT * (GROUPS - 2), KT * GROUPS):
            add_down(m % KT, m)

        ve.wait_ge(gain_in, 16 * 5)
        ve.wait_ge(x2_in, 32)
        for i in range(TILES):
            rows = ROWS[i]
            at = 2 * (i % 2) * BANK
            ve.wait_ge(yt2_ready, i + 1)
            ve.tensor_tensor(x2b[0:rows, i, :], x2b[0:rows, i, :], ps[0:rows, at:at + 2 * BANK], ALU.add)\
              .then_inc(res_ready, 1)
            ve.wait_ge(ssq_ready, sums[0] + i + 1)
            rstd = sm["rstd"][0:rows, i:i + 1]
            ve.tensor_scalar(rstd, sm["ssq"][0:rows, i:i + 1], 1.0 / D, RMS_EPS, ALU.mult, ALU.add)\
              .then_inc(var_ready, 1)
            ve.wait_ge(std_ready, 4 + i + 1)
            step.done(ve.reciprocal(rstd, rstd))
            ve.scalar_tensor_tensor(yout[0:rows, i % 2, :], x2b[0:rows, i, :], rstd, gain[0:rows, :],
                                    ALU.mult, ALU.mult).then_inc(y_ready, 1)


INPUTS = ["wts", "ident", "x", "mem", "gains", "par", "lamp", "gsub", "ropec", "ropes", "ropen", "mask", "ckT", "cv",
          "cmkT", "cmv", "keysT", "iota"]
OUTPUTS = {"y": (NT, D), "k": (NT, D), "v": (NT, D), "mkT": (D, MEM), "mv": (MEM, D), "cstate": (P, KT, 6),
           "hstate": (P, KT, 2)}


def layout(p):
    p = {name: np.asarray(value) for name, value in p.items()}
    f32 = np.float32

    def pieces(w):
        n = w.shape[1] // CHUNK
        return w.reshape(2, 4, P, n, CHUNK).transpose(3, 0, 2, 1, 4).reshape(2 * n, P, PIECE)

    w_in = p["w_in"][0]
    q, k, v, rx, rg, ga, gr = (w_in[:, c * D:(c + 1) * D] for c in range(7))
    recurrent = np.concatenate([w[:, j * P:(j + 1) * P] for j in range(N_RG) for w in (rx, rg, gr, ga)], axis=1)
    u = p["peer_u"][0].reshape(NKEYS, NKEYS, D)
    u = u.reshape(NKEYS, GROUPS, EG, 2, 4, P).transpose(1, 3, 5, 4, 2, 0).reshape(GROUPS, 2, P, PIECE)
    vt = p["peer_v"][0].reshape(NKEYS, GROUPS, 2, 2, D).transpose(1, 2, 0, 3, 4).reshape(GROUPS, 2, P, PIECE)
    experts = [u[0]]
    for g in range(1, GROUPS):
        experts += [u[g], vt[g - 1]]
    experts.append(vt[GROUPS - 1])
    wts = np.concatenate([pieces(p["w_ck"][0]), pieces(p["w_cv"][0]), pieces(recurrent), pieces(k), pieces(v),
                          pieces(q), pieces(p["w_out"][0]), pieces(p["w_cq"][0]), pieces(p["w_co"][0]),
                          pieces(p["w_pq"][0])] + experts)

    def columns(x):
        return np.moveaxis(x.reshape(x.shape[:-1] + (KT, P)), (-2, -1), (0, 1))

    par = np.zeros((KT, P, PAR_N), f32)
    for at, w in ((0, p["rg_wa"][0]), (P, p["rg_wx"][0])):
        for b in range(2):
            par[:, b * 64:b * 64 + 64, at + b * 64:at + b * 64 + 64] = w[b::2]
    par[:, :, PAR_CW:PAR_CW + CONVW] = columns(p["conv_w"][0])
    for at, name in ((PAR_CB, "conv_b"), (PAR_BA, "rg_ba"), (PAR_BX, "rg_bx")):
        par[:, :, at] = columns(p[name][0])
    par[:, :, PAR_SC:PAR_SC + 3] = columns(p["state_conv"][0, 0])
    par[:, :, PAR_H0] = columns(p["state_rglru"][0, 0])

    lams = np.concatenate([p[n][0] for n in ("lam_q1", "lam_k1", "lam_q2", "lam_k2")])
    lamp = np.concatenate([np.broadcast_to(lams, (P, 4 * DK)), p["rg_lambda"][0].reshape(KT, P).T], axis=1)
    gains = np.stack([p["g_mem"][0], p["g_mix"][0], p["g_cross"][0], p["g_ffn"][0], p["g_final"]])

    inv = np.exp(f32(-math.log(10000.0)) * np.arange(32, dtype=f32) * f32(2.0 / DK)).astype(f32)
    pos = np.arange(TILES * P, dtype=f32)
    ang = (pos[:, None] * inv[None, :]).astype(f32).astype(np.float64)
    rope = {n: np.ascontiguousarray(t.astype(f32).reshape(TILES, P, 32).transpose(1, 0, 2))
            for n, t in (("ropec", np.cos(ang)), ("ropes", np.sin(ang)), ("ropen", -np.sin(ang)))}
    mask = np.zeros((1, P + DK), f32)
    mask[0, 0:DK] = 1.0
    mask[0, P:] = -1e30
    keys = np.stack([p["pk_keys1"][0], p["pk_keys2"][0]], axis=1).reshape(2 * PK_HEADS, NKEYS, P)
    arrays = {
        "wts": wts, "ident": np.eye(P, dtype=f32),
        "x": np.concatenate([p["x_prompt"][0], p["x_sample"][0]]), "mem": p["mem_prompt"][0],
        "gains": np.broadcast_to(gains[:, None, :], (5, P, D)), "par": par, "lamp": lamp,
        "gsub": p["g_subln"][0][:, None], **rope, "mask": mask,
        "ckT": p["cache_attn_k"][0, 0].reshape(PAST, HEADS, P).transpose(1, 2, 0),
        "cv": p["cache_attn_v"][0, 0].reshape(PAST // P, P, D).transpose(1, 0, 2),
        "cmkT": p["cache_mem_k"][0, 0].reshape(MEM, D).T, "cmv": p["cache_mem_v"][0, 0].reshape(MEM, D),
        "keysT": keys.transpose(2, 0, 1), "iota": np.broadcast_to(np.arange(P, dtype=f32), (P, P)),
    }
    return {name: np.ascontiguousarray(arrays[name]) for name in INPUTS}


def kernel(**inputs):
    import concourse.bacc as _bacc
    from concourse.bass_utils import run_bass_kernel_spmd as _run

    arrays = layout(inputs)
    nc = _bacc.Bacc("TRN2", target_bir_lowering=False, num_devices=1)
    a = {name: nc.dram_tensor(name, x.shape, F32, kind="ExternalInput").ap() for name, x in arrays.items()}
    o = {name: nc.dram_tensor(f"out_{name}", shape, F32, kind="ExternalOutput").ap() for name, shape in OUTPUTS.items()}
    with nc.Block() as block:
        encoder_layer(nc, block, a, o)
    r = _run(nc, [arrays], core_ids=[0]).results[0]
    y, k, v, mkT, mv, cs, hs = (np.asarray(r[f"out_{name}"]) for name in OUTPUTS)
    cs = cs.transpose(2, 1, 0).reshape(6, D)
    hs = hs.transpose(2, 1, 0).reshape(2, D)
    n = NP_TOK
    return (y[None, :n], y[None, n:],
            k[:n].reshape(1, 1, n, 2 * HEADS, DK), v[:n].reshape(1, 1, n, HEADS, DV),
            mkT.T.reshape(1, 1, MEM, CA_HEADS, CA_DH), mv.reshape(1, 1, MEM, CA_HEADS, CA_DH),
            cs[None, None, 0:3], hs[None, 0:1],
            k[n:].reshape(1, 1, NS_TOK, 2 * HEADS, DK), v[n:].reshape(1, 1, NS_TOK, HEADS, DV),
            cs[None, None, 3:6], hs[None, 1:2])
```

```python
import math

import concourse.bass as bass
import numpy as np
from concourse import mybir

F32 = mybir.dt.float32
F32R = mybir.dt.float32r
U32 = mybir.dt.uint32
ALU = mybir.AluOpType
ACT = mybir.ActivationFunctionType
AX = mybir.AxisListType.X

P = 128
D = 1024
KT = D // P
NP_TOK, NS_TOK = 512, 64
NT = NP_TOK + NS_TOK
HALF = NT // 2
ROWS = [128, 128, 128, 128, 64]
T0 = [0, 128, 256, 384, 512]
TILES = len(ROWS)
HEADS, DK, DV = 8, 64, 128
LAM_INIT = 0.8 - 0.6 * math.exp(-0.3 * 0)
PAST = 512
MEM = 256
MT = MEM // P
CA_HEADS, CA_DH = 4, 256
PK_HEADS, NKEYS, TOPK = 8, 128, 16
RG_C = 8.0
CONVW = 4
RMS_EPS, SUBLN_EPS = 1e-6, 1e-5
BANK = 512
BANKS = 8
CHUNK = 512
PIECE = 4 * CHUNK
SEG = NP_TOK + CONVW - 1
XPW = SEG + CONVW - 1 + NS_TOK
CW = XPW - (CONVW - 1)
CA_ = 290
PAR_CW, PAR_CB, PAR_BA, PAR_BX, PAR_SC, PAR_H0, PAR_N = 256, 260, 261, 262, 264, 267, 272
N_CK, N_CV, N_RG, N_K, N_V, N_Q, N_OUT, N_CQ, N_CO, N_PQ = 2, 2, 8, 2, 2, 2, 2, 2, 2, 4
PRE_CHUNKS = N_CK + N_CV + N_RG + N_K + N_V + N_Q + N_OUT + N_CQ + N_CO + N_PQ
EG = 4
GROUPS = NKEYS // EG
CHUNKS = PRE_CHUNKS + 2 * GROUPS
TB = 32
TBN = NT // TB
RANK_GROUPS = 12
C_GROUPS = TBN // 2
EARLY = RANK_GROUPS + C_GROUPS + 1
LATE_PAIRS = (GROUPS - EARLY) // 2 - 1
assert EARLY % 2 == 0 and RANK_GROUPS % 2 == 0 and C_GROUPS % 2 == 1
NEG = -3.0e38


class Steps:

    def __init__(self, eng, sem):
        self.eng, self.sem, self.n, self.i, self.per = eng, sem, 0, None, 0

    def done(self, ins):
        self.n += 1
        ins.then_inc(self.sem, 1)
        self.eng.wait_ge(self.sem, self.n if self.i is None else self.i * self.per + self.n)

    def enter(self, i, per):
        self.i, self.per, self.start = i, per, self.n

    def leave(self, times):
        assert self.n - self.start == self.per, (self.n - self.start, self.per)
        self.n, self.i = self.start + times * self.per, None


class Turns:

    def __init__(self):
        self.n, self.i, self.per = 0, None, 0

    def take(self):
        bank, value = self.n % BANKS, self.n // BANKS + 1
        self.n += 1
        return bank, value if self.i is None else self.i * (self.per // BANKS) + value

    def enter(self, i, per):
        self.i, self.per, self.start = i, per, self.n

    def leave(self, times):
        assert self.n - self.start == self.per and self.per % BANKS == 0
        self.n, self.i = self.start + times * self.per, None


class Count:

    def __init__(self, n=0):
        self.n, self.i, self.per = n, None, 0

    def up(self, k=1):
        self.n += k
        return self.value()

    def value(self, more=0):
        v = self.n + more
        return v if self.i is None else self.i * self.per + v

    def enter(self, i, per):
        self.i, self.per, self.start = i, per, self.n

    def leave(self, times):
        assert self.n - self.start == self.per, (self.n - self.start, self.per)
        self.n, self.i = self.start + times * self.per, None


def encoder_layer(nc: bass.Bass, block, a: dict, o: dict):
    base = (nc.sbuf_base + 31) // 32 * 32
    cursor = [base]

    def put(name, shape, dt=F32, at=None):
        size = int(np.prod(shape[1:])) * 4
        where = cursor[0] if at is None else at
        t = nc.alloc_sbuf_tensor_at(name, shape, dt, offset=where)
        if at is None:
            cursor[0] += (size + 31) // 32 * 32
        return t

    actH = put("actH", [P, KT, NT], F32R)
    actL = put("actL", [P, KT, NT], F32R)
    wH = put("wH", [P, 4, 4, CHUNK], F32R)
    wL = put("wL", [P, 4, 4, CHUNK], F32R)
    raw = put("raw", [P, 2, PIECE])
    ident = put("ident", [P, P])
    gain = put("gain", [P, D])
    small = put("small", [P, 256])
    mask = put("mask", [1, P + DK])
    arena = cursor[0]

    class Region:
        def __init__(self, start=arena):
            self.at = start

        def put(self, name, shape, dt=F32):
            size = (int(np.prod(shape[1:])) * 4 + 31) // 32 * 32
            t = nc.alloc_sbuf_tensor_at(name, shape, dt, offset=self.at)
            self.at += size
            return t

    sm = {}
    at = 0
    for name, n in (("ssq", 8), ("rstd", 8), ("nmax", 8), ("z", 8), ("lamv", 2), ("lamt", 8), ("gsub", 1),
                    ("ncall", 8), ("pcall", 8), ("sp", 40), ("oss", 8), ("orstd", 8), ("mz", 8), ("pk", 24)):
        sm[name] = small[:, at:at + n]
        at += n
    assert at <= 256

    r = Region()
    xres = r.put("xres", [P, TILES, D])
    after_xres = r.at
    xn = r.put("xn", [P, 2, D])
    sq = r.put("sq", [P, D])
    memx = r.put("memx", [P, MT, D])
    mk_sb = r.put("mk_sb", [P, KT, MEM])
    mv_sb = r.put("mv_sb", [P, MT, D])
    r = Region()
    rxp = r.put("rxp", [P, 2, XPW + 2])
    par = r.put("par", [P, 2, PAR_N])
    conv = r.put("conv", [P, 2, CW + 1])
    gel = r.put("gel", [P, 2, NT])
    sgr = r.put("sgr", [P, 2, NT])
    sga = r.put("sga", [P, 2, NT])
    gate_r = r.put("gate_r", [P, CW + 1])
    gate_i = r.put("gate_i", [P, CW + 1])
    lru_a = r.put("lru_a", [P, CW + 1])
    lru_t = r.put("lru_t", [P, CW + 1])
    lru_m = r.put("lru_m", [P, CW + 1])
    lru_h = r.put("lru_h", [P, NT])
    yrec = r.put("yrec", [P, 2, NT])
    cstate = r.put("cstate", [P, KT, 6])
    hstate = r.put("hstate", [P, KT, 2])
    lamp = r.put("lamp", [P, 4 * DK + KT])
    r = Region()
    kT = r.put("kT", [P, HEADS, NT])
    qT = r.put("qT", [P, HEADS, NT])
    vtok = r.put("vtok", [P, TILES, D])
    att = r.at
    ropec = r.put("ropec", [P, TILES, 32])
    ropes = r.put("ropes", [P, TILES, 32])
    ropen = r.put("ropen", [P, TILES, 32])
    rot1 = r.put("rot1", [P, CHUNK])
    rot2 = r.put("rot2", [P, CHUNK])
    rot = r.put("rot", [P, 2, CHUNK])
    r = Region(att)
    sat = r.put("sat", [P, KT, P])
    rt = r.put("rt", [P, KT, P])
    osb = r.put("osb", [P, D])
    prob_at = r.at
    osq = nc.alloc_sbuf_tensor_at("osq", [P, D], F32, offset=prob_at)
    prob = r.put("prob", [P, 2, 2, NP_TOK])
    aT = r.put("aT", [P, 2, CHUNK])
    attn_end = r.at
    probs = nc.alloc_sbuf_tensor_at("probs", [P, 2, NT], F32, offset=prob_at)
    ckv0 = r.put("ckv0", [P, 2, PAST])
    r = Region(after_xres)
    qcT = r.put("qcT", [P, KT, NT])
    mkT = r.put("mkT", [P, 2, KT, MEM])
    mvt = r.put("mvt", [P, 2, MT, D])
    cp = r.put("cp", [P, 2, D])
    cpT = r.put("cpT", [P, D])
    r = Region()
    pqT = r.put("pqT", [P, 2 * PK_HEADS, NT])
    keys = r.put("keys", [P, 2 * PK_HEADS, NKEYS])
    after_keys = r.at
    ssb = r.put("ssb", [P, TILES, 2 * PK_HEADS, NKEYS])
    iota16 = r.put("iota16", [P, TOPK])
    assert r.at <= nc.sbuf_usable_end, r.at
    r = Region()
    ge = r.put("ge", [P, EG, NT])
    after_ge = r.at
    work = r.put("work", [P, 2048])
    after_work = r.at
    cand = r.put("cand", [P, 2048])
    pick = cand
    top = r.put("top", [P, 2 * PK_HEADS, TOPK])
    topi = r.put("topi", [P, 2 * PK_HEADS, TOPK], U32)
    topf = r.put("topf", [P, 2 * PK_HEADS, TOPK])
    best = r.put("best", [P, PK_HEADS, TOPK])
    besti = r.put("besti", [P, PK_HEADS, TOPK], U32)
    bestr = r.put("bestr", [P, 2, PK_HEADS, TOPK], U32)
    bestf = r.put("bestf", [P, 2, PK_HEADS, TOPK])
    chosen = r.put("chosen", [P, TILES, 3, PK_HEADS * TOPK])
    assert r.at <= after_keys
    chosenT = nc.alloc_sbuf_tensor_at("chosenT", [P, 3, NT], F32, offset=after_ge)
    assert after_ge + 3 * NT * 4 <= after_work
    r = Region(after_work)
    iota = r.put("iota", [P, NKEYS])
    hot1 = r.put("hot1", [P, 2, 8, NKEYS])
    hot2 = r.put("hot2", [P, 2, 8, NKEYS])
    cst = r.put("cst", [P, 2, NKEYS, TB])
    assert r.at <= nc.sbuf_usable_end, r.at
    r = Region(after_ge)
    acc = r.put("acc", [P, KT, NT])
    cg = r.put("cg", [P, 2, TBN, EG, TB])
    gf = r.put("gf", [P, 2, NT])
    gH = r.put("gH", [P, 2, EG, NT], F32R)
    gL = r.put("gL", [P, 2, EG, NT], F32R)
    assert r.at <= nc.sbuf_usable_end, r.at
    r = Region(after_ge + KT * NT * 4)
    x2b = r.put("x2b", [P, TILES, D])
    yout = r.put("yout", [P, 2, D])

    ps = nc.alloc_psum_tensor("ps", [P, BANKS * BANK], F32)

    def bank(b, n=BANK, rows=P):
        return ps[0:rows, b * BANK:b * BANK + n]

    sa_d = nc.dram_tensor("sa_scratch", (KT, P, NT), F32).ap()
    r_d = nc.dram_tensor("r_scratch", (KT, P, NT), F32).ap()
    x2_d = nc.dram_tensor("x2_scratch", (NT, D), F32).ap()
    ge_d = nc.dram_tensor("ge_scratch", (EARLY * EG, P, NT), F32).ap()
    c_d = nc.dram_tensor("c_scratch", (TBN, P, NKEYS, TB), F32).ap()

    S = nc.alloc_semaphore
    raw_in = [S(f"raw_in{j}") for j in range(2)]
    high_done = S("high_done")
    w_ready = S("w_ready")
    w_free = S("w_free")
    filled = [S(f"filled{b}") for b in range(BANKS)]
    emptied = [S(f"emptied{b}") for b in range(BANKS)]
    ve_step = S("ve_step")
    names = """const_in gain_in gain_used memx_in x_in ssq_clear ssq_ready var_ready std_ready xn_ready acth_done
        out_done lamp_in sp_neg sp_exp sp_one sp_ln lam_sums lam_exp lam_ready conv_done gate_ready m_ready
        root_ready yrec_ready rot_ready rope_in sc_ready nm_ready p_ready a_ready t_ready aT_ready pv_done
        osb_ready ovar_ready ostd_ready on_ready yt_ready merged mh_done ml_done sat_in ckv_in mask_in mem_in
        cs_ready cm_ready ce_ready cn_ready ct_ready cpT_ready co_ready ch_done cl_done res_ready x2_store
        keys_in iota16_in score_ready ssb_ready  gexp_in gexp_out chosen_ready chT_ready chT_copied
        hot_ready c_filled c_copied u_done ge_ready gf_ready gh_done gl_done v_done acc_added
        x2_in yt2_ready y_ready taken_up""".split()
    (const_in, gain_in, gain_used, memx_in, x_in, ssq_clear, ssq_ready, var_ready, std_ready, xn_ready, acth_done,
     out_done, lamp_in, sp_neg, sp_exp, sp_one, sp_ln, lam_sums, lam_exp, lam_ready, conv_done, gate_ready, m_ready,
     root_ready, yrec_ready, rot_ready, rope_in, sc_ready, nm_ready, p_ready, a_ready, t_ready, aT_ready, pv_done,
     osb_ready, ovar_ready, ostd_ready, on_ready, yt_ready, merged, mh_done, ml_done, sat_in, ckv_in, mask_in, mem_in,
     cs_ready, cm_ready, ce_ready, cn_ready, ct_ready, cpT_ready, co_ready, ch_done, cl_done, res_ready, x2_store,
     keys_in, iota16_in, score_ready, ssb_ready, gexp_in, gexp_out, chosen_ready, chT_ready, chT_copied,
     hot_ready, c_filled, c_copied, u_done, ge_ready, gf_ready, gh_done, gl_done, v_done, acc_added,
     x2_in, yt2_ready, y_ready, taken_up) = [S(name) for name in names]
    par_in = [S(f"par_in{j}") for j in range(2)]
    sa_store = [S(f"sa_store{j}") for j in range(2)]
    r_store = [S(f"r_store{j}") for j in range(2)]
    k_store = [S(f"k_store{j}") for j in range(2)]
    c_store = [S(f"c_store{j}") for j in range(2)]
    c_in = [S(f"c_in{j}") for j in range(2)]
    ge_store = [S(f"ge_store{j}") for j in range(EG)]
    ge_in = [S(f"ge_in{j}") for j in range(EG)]
    y_store = [S(f"y_store{j}") for j in range(2)]

    UNITS = [(i, h) for i in range(TILES) for h in range(HEADS)]
    KQV = [("k", 0), ("k", 1), ("v", 0), ("v", 1), ("q", 0), ("q", 1)]
    TUNITS = [(kind, c, i) for kind, c in KQV for i in range(TILES)]

    def halves(b):
        return ps[:, b * BANK:(b + 2) * BANK].rearrange("p (c n) -> p c n", n=BANK)[:, :, 0:HALF]

    @block.sync
    def _(sp):
        for j in range(2):
            sp.dma_start(raw[:, j, :], a["wts"][j]).then_inc(raw_in[j], 16)
        with sp.Fori(0, CHUNKS - 1) as i:
            for j in range(2):
                sp.wait_ge(w_ready, i * 4 + (2 * j + 2))
                sp.dma_start(raw[:, j, :], a["wts"][i * 2 + (2 + j)]).then_inc(raw_in[j], 16)

    @block.gpsimd
    def _(pool):
        with pool.Fori(0, CHUNKS // 2) as i:
            for s in range(4):
                w = raw[:, s % 2, :]
                hi = wH[:, s].rearrange("p k n -> p (k n)")
                lo = wL[:, s].rearrange("p k n -> p (k n)")
                pool.wait_ge(raw_in[s % 2], i * 32 + 16 * (s // 2 + 1))
                pool.wait_ge(w_free, i * 4 + (s // 2 * 2 + 2))
                pool.sem_inc(taken_up, 1)
                cuts = (slice(0, PIECE // 2), slice(PIECE // 2, PIECE))
                for cut in cuts:
                    pool.tensor_scalar(hi[:, cut], w[:, cut], 1.0, 1.0, ALU.mult, ALU.mult).then_inc(high_done, 1)
                for c, cut in enumerate(cuts):
                    pool.wait_ge(high_done, i * 8 + (2 * s + c + 1))
                    pool.tensor_tensor(lo[:, cut], w[:, cut], hi[:, cut].bitcast(F32), ALU.subtract)\
                        .then_inc(w_ready, 1)

    @block.tensor
    def _(pe):
        turns = Turns()
        pieces = Count()
        release = [0]

        def begin(ins):
            if release[0]:
                ins.then_inc(w_free, 2)
                release[0] = 0

        pe.sem_inc(w_free, 4)
        for b in range(BANKS):
            pe.sem_inc(emptied[b], 1)
        pe.wait_ge(const_in, 16)

        def fill(out, terms, sem=None):
            for t, (lhs, rhs) in enumerate(terms):
                mm = pe.matmul(out, lhs, rhs, start=t == 0, stop=t == len(terms) - 1)
                if t == 0 and len(terms) > 1:
                    begin(mm)
            if sem is not None:
                mm.then_inc(sem, 1)
            return mm

        def weight(slot, k, cut):
            return wH[:, slot + k // 4, k % 4, cut], wL[:, slot + k // 4, k % 4, cut]

        def chunk(slot, groups):
            for g, (cols, terms) in enumerate(groups):
                b, value = turns.take()
                pe.wait_ge(emptied[b], value)
                for k in range(KT):
                    if g == 0 and k % 4 == 0:
                        pieces.up(2)
                        pe.wait_ge(w_ready, pieces.value())
                    for t, (lhs, rhs) in enumerate(terms(k)):
                        mm = pe.matmul(cols(b), lhs, rhs, start=k == 0 and t == 0, stop=k == KT - 1 and t == 2)
                        if k == 0 and t == 0:
                            begin(mm)
                mm.then_inc(filled[b], 1)
            release[0] = 1

        def feature_chunk(slot, n_tok, n_parts):
            def make(blk, part):
                w = slice(blk * P, blk * P + P)
                t = slice(part * n_tok, (part + 1) * n_tok)

                def terms(k):
                    h, l = weight(slot, k, w)
                    return (h, actH[:, k, t]), (h, actL[:, k, t]), (l, actH[:, k, t])
                return (lambda b: bank(b, n_tok)), terms
            chunk(slot, [make(blk, part) for blk in range(4) for part in range(n_parts)])

        def token_group(slot, i, rows, t0):
            t = slice(t0, t0 + rows)

            def terms(k):
                h, l = weight(slot, k, slice(0, CHUNK))
                return (actH[:, k, t], h), (actH[:, k, t], l), (actL[:, k, t], h)
            return (lambda b: bank(b, CHUNK, rows)), terms

        def norm(n_tiles, first, rows):
            for i in range(n_tiles):
                pe.wait_ge(xn_ready, first + i + 1)
                for half in range(2):
                    b, value = turns.take()
                    pe.wait_ge(emptied[b], value)
                    for k in range(4):
                        src = xn[0:rows[i], (first + i) % 2, (half * 4 + k) * P:(half * 4 + k + 1) * P]
                        mm = pe.transpose(ps[:, b * BANK + k * rows[i]:b * BANK + (k + 1) * rows[i]], src,
                                          ident[0:rows[i], 0:rows[i]])
                        if half == 0 and k == 0:
                            begin(mm)
                    mm.then_inc(filled[b], 1)
            last[0] = (b, value)

        last = [None]

        def evacuated():
            b, value = last[0]
            pe.wait_ge(emptied[b], value + 1)

        norm(MT, 0, ROWS)
        evacuated()
        for c in range(N_CK):
            feature_chunk(2 * c, MEM, 1)
        for c in range(N_CV):
            chunk(2 * c, [token_group(2 * c, i, P, i * P) for i in range(MT)])
        norm(TILES, MT, ROWS)
        evacuated()

        def gates(s, value):
            pe.wait_ge(conv_done, value)
            for w in range(2):
                for cut in (slice(0, CA_), slice(CA_, CW)):
                    b, turn = turns.take()
                    pe.wait_ge(emptied[b], turn)
                    fill(ps[:, b * BANK:b * BANK + cut.stop - cut.start],
                         [(par[:, s, w * P:(w + 1) * P], conv[:, s, cut])], filled[b])

        feature_chunk(0, HALF, 2)
        feature_chunk(2, HALF, 2)
        gates(0, 1)
        with pe.Fori(0, N_RG // 2 - 1) as i:
            turns.enter(i, 24)
            pieces.enter(i, 8)
            feature_chunk(0, HALF, 2)
            gates(1, i * 2 + 2)
            feature_chunk(2, HALF, 2)
            gates(0, i * 2 + 3)
            turns.leave(N_RG // 2 - 1)
            pieces.leave(N_RG // 2 - 1)
        def turn_rotated(u):
            kind, c, i = TUNITS[u]
            if kind == "v":
                return
            n = sum(1 for k, _, _ in TUNITS[:u + 1] if k != "v")
            pe.wait_ge(rot_ready, n)
            b, value = turns.take()
            pe.wait_ge(emptied[b], value)
            for k in range(4):
                mm = pe.transpose(ps[:, b * BANK + k * ROWS[i]:b * BANK + (k + 1) * ROWS[i]],
                                  rot[0:ROWS[i], (n - 1) % 2, k * P:(k + 1) * P], ident[0:ROWS[i], 0:ROWS[i]])
                if k == 0:
                    begin(mm)
            mm.then_inc(filled[b], 1)

        u = 0
        for n, (kind, c) in enumerate(KQV):
            slot = 2 * (n % 2)
            for i in range(TILES):
                cols, terms = token_group(slot, i, ROWS[i], T0[i])
                b, value = turns.take()
                pe.wait_ge(emptied[b], value)
                for k in range(KT):
                    if i == 0 and k % 4 == 0:
                        pieces.up(2)
                        pe.wait_ge(w_ready, pieces.value())
                    for t, (lhs, rhs) in enumerate(terms(k)):
                        mm = pe.matmul(cols(b), lhs, rhs, start=k == 0 and t == 0, stop=k == KT - 1 and t == 2)
                        if k == 0 and t == 0:
                            begin(mm)
                mm.then_inc(filled[b], 1)
                if i == TILES - 1:
                    release[0] = 1
                if n == 0 and i == 0:
                    gates(1, N_RG)
                if u >= 1:
                    turn_rotated(u - 1)
                u += 1
        turn_rotated(u - 1)
        for b in range(BANKS):
            pe.wait_ge(emptied[b], (turns.n - 1 - b) // BANKS + 2)

        pe.wait_ge(mask_in, 16)

        def scores(u):
            i, h = UNITS[u]
            rows = ROWS[i]
            t = slice(T0[i], T0[i] + rows)
            if u >= 1 and (i == TILES - 1 or u >= 2):
                pe.wait_ge(p_ready, u if i == TILES - 1 else u - 1)
            if i == TILES - 1:
                pe.wait_ge(ckv_in, 32 * (h + 1))
            for s in range(2):
                half = slice(s * DK, (s + 1) * DK)
                if i < TILES - 1:
                    b, n = 2 * (u % 2) + s, P * (i + 1)
                    mm = pe.matmul(bank(b, n), qT[half, h, t], kT[half, h, 0:n], start=True, stop=False)
                    if s == 0:
                        begin(mm)
                    mm = pe.matmul(ps[:, b * BANK + n - DK:b * BANK + n], mask[0:1, 0:P], mask[0:1, P:P + DK],
                                   start=False, stop=True)
                else:
                    b = 2 * s
                    pe.matmul(bank(b, PAST, rows), qT[half, h, t], ckv0[half, 0, :], start=True, stop=True)
                    mm = pe.matmul(bank(b + 1, rows, rows), qT[half, h, t], kT[half, h, t], start=True, stop=True)
            mm.then_inc(sc_ready, 1)

        def turn_probs(u):
            i, h = UNITS[u]
            rows = ROWS[i]
            pe.wait_ge(a_ready, u + 1)
            if u >= 2:
                pe.wait_ge(aT_ready, u - 1)
            if h < 2 and i > 0:
                pe.wait_ge(ml_done, i)
            b = 4 + u % 2
            if i < TILES - 1:
                for k in range(i + 1):
                    mm = pe.transpose(ps[:, b * BANK + k * P:b * BANK + (k + 1) * P],
                                      prob[:, u % 2, 0, k * P:(k + 1) * P], ident[:, :])
            else:
                for k in range(PAST // P):
                    pe.transpose(ps[:, b * BANK + k * rows:b * BANK + (k + 1) * rows],
                                 probs[0:rows, 0, k * P:(k + 1) * P], ident[0:rows, 0:rows])
                k = PAST // P
                mm = pe.transpose(ps[0:rows, b * BANK + k * rows:b * BANK + (k + 1) * rows],
                                  probs[0:rows, 0, PAST:NT], ident[0:rows, 0:rows])
            mm.then_inc(t_ready, 1)

        def weighted(u):
            i, h = UNITS[u]
            rows = ROWS[i]
            pe.wait_ge(aT_ready, u + 1)
            if h == 0 and i > 0:
                pe.wait_ge(osb_ready, i)
            out = ps[0:rows, 6 * BANK + h * DV:6 * BANK + (h + 1) * DV]
            cols = slice(h * DV, (h + 1) * DV)
            if i < TILES - 1:
                terms = [(aT[:, u % 2, k * P:(k + 1) * P], vtok[:, k, cols]) for k in range(i + 1)]
            else:
                terms = [(aT[:, u % 2, k * rows:(k + 1) * rows], ckv0[:, 1, k * P:(k + 1) * P]) for k in range(PAST // P)]
                k = PAST // P
                terms.append((aT[0:rows, u % 2, k * rows:(k + 1) * rows], vtok[0:rows, TILES - 1, cols]))
            for t, (lhs, rhs) in enumerate(terms):
                mm = pe.matmul(out, lhs, rhs, start=t == 0, stop=t == len(terms) - 1)
            mm.then_inc(pv_done, 1)

        def turn_outputs(i):
            rows = ROWS[i]
            pe.wait_ge(on_ready, i + 1)
            pe.wait_ge(aT_ready, HEADS * (i + 1))
            for h in range(HEADS):
                b = 4 + h // 4
                mm = pe.transpose(ps[:, b * BANK + (h % 4) * rows:b * BANK + (h % 4 + 1) * rows],
                                  osb[0:rows, h * DV:(h + 1) * DV], ident[0:rows, 0:rows])
            mm.then_inc(yt_ready, 1)

        for i in range(TILES):
            for h in range(HEADS):
                u = i * HEADS + h
                if i < TILES - 1:
                    if h == 0:
                        scores(u)
                    if h + 1 < HEADS:
                        scores(u + 1)
                    turn_probs(u)
                    if h > 0:
                        weighted(u - 1)
                else:
                    scores(u)
                    turn_probs(u)
                    weighted(u)
            if i < TILES - 1:
                weighted(i * HEADS + HEADS - 1)
            turn_outputs(i)
        pe.wait_ge(ml_done, TILES)

        def token_chunks(n_chunks):
            for c in range(n_chunks):
                chunk(2 * c, [token_group(2 * c, i, ROWS[i], T0[i]) for i in range(TILES)])

        token_chunks(N_OUT)
        norm(TILES, MT + TILES, ROWS)
        evacuated()
        for c in range(N_CQ):
            feature_chunk(2 * c, HALF, 2)
        for b in range(BANKS):
            pe.wait_ge(emptied[b], (turns.n - 1 - b) // BANKS + 2)
        pe.wait_ge(mem_in, 64)

        def cross_scores(i):
            rows, src = ROWS[i], i // (TILES - 1)
            if i >= 2:
                pe.wait_ge(ce_ready, i - 1)
            for h in range(CA_HEADS):
                out = ps[0:rows, 2 * (i % 2) * BANK + h * MEM:2 * (i % 2) * BANK + (h + 1) * MEM]
                mm = fill(out, [(qcT[:, 2 * h + k, T0[i]:T0[i] + rows], mkT[:, src, 2 * h + k, :]) for k in range(2)])
            mm.then_inc(cs_ready, 1)

        def cross_rest(i):
            rows, src = ROWS[i], i // (TILES - 1)
            pe.wait_ge(cn_ready, i + 1)
            if i >= 1:
                pe.wait_ge(cpT_ready, i)
            for m in range(2 * CA_HEADS):
                b = 4 + m // 4
                mm = pe.transpose(ps[:, b * BANK + (m % 4) * rows:b * BANK + (m % 4 + 1) * rows],
                                  cp[0:rows, i % 2, m * P:(m + 1) * P], ident[0:rows, 0:rows])
            mm.then_inc(ct_ready, 1)
            pe.wait_ge(cpT_ready, i + 1)
            if i >= 1:
                pe.wait_ge(cl_done, 2 * i)
            for blk in range(KT):
                h = blk // 2
                out = ps[:, (6 + blk // 4) * BANK + (blk % 4) * rows:(6 + blk // 4) * BANK + (blk % 4 + 1) * rows]
                mm = fill(out, [(mvt[:, src, m, blk * P:(blk + 1) * P], cpT[:, (2 * h + m) * rows:(2 * h + m + 1) * rows])
                                for m in range(MT)])
            mm.then_inc(co_ready, 1)

        cross_scores(0)
        for i in range(TILES):
            if i + 1 < TILES:
                cross_scores(i + 1)
            cross_rest(i)
        pe.wait_ge(cl_done, 2 * TILES)
        token_chunks(N_CO)
        norm(TILES, MT + 2 * TILES, ROWS)
        evacuated()
        for c in range(N_PQ):
            feature_chunk(2 * (c % 2), HALF, 2)
        for b in range(BANKS):
            pe.wait_ge(emptied[b], (turns.n - 1 - b) // BANKS + 2)

        pe.wait_ge(keys_in, 16)
        for i in range(TILES):
            rows = ROWS[i]
            if i >= 2:
                pe.wait_ge(ssb_ready, i - 1)
            for s in range(2 * PK_HEADS):
                at = 4 * (i % 2) * BANK + s * P
                mm = fill(ps[0:rows, at:at + P], [(pqT[:, s, T0[i]:T0[i] + rows], keys[:, s, :])])
            mm.then_inc(score_ready, 1)
        pe.wait_ge(ssb_ready, TILES)

        def up(slot, gelus, between=None):
            for e in range(EG):
                b = 2 * (e % 2)
                pe.wait_ge(ge_ready, gelus(e))
                for part in range(2):
                    t = slice(part * HALF, (part + 1) * HALF)
                    for k in range(KT):
                        if e == 0 and part == 0 and k % 4 == 0:
                            pieces.up(2)
                            pe.wait_ge(w_ready, pieces.value())
                        h, l = weight(slot, k, slice(e * P, (e + 1) * P))
                        for w, (lhs, rhs) in enumerate(((h, actH[:, k, t]), (h, actL[:, k, t]), (l, actH[:, k, t]))):
                            mm = pe.matmul(bank(b + part, HALF), lhs, rhs, start=k == 0 and w == 0,
                                           stop=k == KT - 1 and w == 2)
                            if k == 0 and w == 0 and part == 0 and e == 0:
                                begin(mm)
                    if part == 1:
                        mm.then_inc(u_done, 1)
                    if between is not None:
                        between(2 * e + part)
            release[0] = 1

        with pe.Fori(0, RANK_GROUPS // 2) as i:
            pieces.enter(i, 8)
            for s in range(2):
                up(2 * s, lambda e: i * (2 * EG) + (EG * s + e + 1))
            pieces.leave(RANK_GROUPS // 2)
        pe.wait_ge(chosen_ready, 1)
        for i in range(TILES):
            if i >= 4:
                pe.wait_ge(chT_copied, i - 3)
            for s in range(3):
                at = (4 + i % 4) * BANK + s * P
                mm = pe.transpose(ps[:, at:at + ROWS[i]], chosen[0:ROWS[i], i, s, :], ident[0:ROWS[i], 0:ROWS[i]])
            mm.then_inc(chT_ready, 1)

        pe.wait_ge(chT_copied, TILES)
        pe.sem_inc(c_filled, 4)

        def c_tokens(i, n):
            pe.wait_ge(hot_ready, i * 8 + (n + 1))
            for half in range(2):
                q = 2 * n + half
                pe.wait_ge(c_copied, i * 16 + (q + 1))
                for t in range(4):
                    at = (4 + q % 4) * BANK + t * P
                    mm = pe.matmul(ps[:, at:at + P], hot1[:, n % 2, 4 * half + t, :], hot2[:, n % 2, 4 * half + t, :],
                                   start=True, stop=True)
                mm.then_inc(c_filled, 1)

        with pe.Fori(0, C_GROUPS // 2) as i:
            pieces.enter(i, 8)
            for s in range(2):
                up(2 * s, lambda e: i * (2 * EG) + (EG * (RANK_GROUPS + s) + e + 1),
                   lambda n: c_tokens(i * 2, 8 * s + n))
            pieces.leave(C_GROUPS // 2)
        up(0, lambda e: EG * (EARLY - 2) + e + 1, lambda n: c_tokens(0, 8 * (C_GROUPS - 1) + n))
        up(2, lambda e: EG * (EARLY - 1) + e + 1)
        pe.wait_ge(c_copied, NT // 4 + 4)

        def down(slot, s, split, added):
            pe.wait_ge(gl_done, split)
            for d in range(KT):
                b = 4 + 2 * (d % 2)
                pe.wait_ge(acc_added, added(d))
                for part in range(2):
                    t = slice(part * HALF, (part + 1) * HALF)
                    for e in range(EG):
                        if d == 0 and part == 0 and e % 2 == 0:
                            pieces.up(2)
                            pe.wait_ge(w_ready, pieces.value())
                        at = (e % 2) * D + d * P
                        h = wH[:, slot + e // 2].rearrange("p k n -> p (k n)")[:, at:at + P]
                        l = wL[:, slot + e // 2].rearrange("p k n -> p (k n)")[:, at:at + P]
                        for w, (lhs, rhs) in enumerate(((h, gH[:, s, e, t]), (h, gL[:, s, e, t]), (l, gH[:, s, e, t]))):
                            mm = pe.matmul(bank(b + part, HALF), lhs, rhs, start=e == 0 and w == 0,
                                           stop=e == EG - 1 and w == 2)
                            if d == 0 and part == 0 and e == 0 and w == 0:
                                begin(mm)
                mm.then_inc(v_done, 1)
            release[0] = 1

        with pe.Fori(0, EARLY // 2) as i:
            pieces.enter(i, 8)
            for s in range(2):
                down(2 * s, s, i * (2 * EG) + EG * (s + 1), lambda d: i * (2 * KT) + (KT * s + d + 1))
            pieces.leave(EARLY // 2)
        up(0, lambda e: EG * EARLY + e + 1)
        with pe.Fori(0, LATE_PAIRS) as i:
            pieces.enter(i, 16)
            for s in range(2):
                up(2, lambda e: i * (2 * EG) + (EG * (EARLY + s + 1) + e + 1))
                down(0, s, i * (2 * EG) + EG * (EARLY + s + 1), lambda d: i * (2 * KT) + (KT * (EARLY + s) + d + 1))
            pieces.leave(LATE_PAIRS)
        up(2, lambda e: EG * (GROUPS - 1) + e + 1)
        down(0, 0, EG * (GROUPS - 1), lambda d: KT * (GROUPS - 2) + d + 1)
        down(2, 1, EG * GROUPS, lambda d: KT * (GROUPS - 1) + d + 1)

        pe.wait_ge(acc_added, KT * GROUPS + 2)
        for i in range(TILES):
            if i >= 2:
                pe.wait_ge(res_ready, i - 1)
            for k in range(KT):
                b = 2 * (i % 2) + k // 4
                mm = pe.transpose(ps[0:ROWS[i], b * BANK + (k % 4) * P:b * BANK + (k % 4 + 1) * P],
                                  acc[:, k, T0[i]:T0[i] + ROWS[i]], ident[:, :])
            mm.then_inc(yt2_ready, 1)


    @block.scalar
    def _(act):
        turns = Turns()

        def wait_filled():
            b, value = turns.take()
            act.wait_ge(filled[b], value)
            return b, value

        def skip(n):
            for _ in range(n):
                turns.take()

        def load_x():
            act.dma_start(xres[:, 0:4, :], a["x"][0:NP_TOK].rearrange("(i p) d -> p i d", p=P)).then_inc(x_in, 16)
            act.dma_start(xres[0:NS_TOK, 4, :], a["x"][NP_TOK:NT]).then_inc(x_in, 16)

        act.dma_start(ident[:, :], a["ident"]).then_inc(const_in, 16)
        act.dma_start(memx[:, :, :], a["mem"].rearrange("(i p) d -> p i d", p=P)).then_inc(memx_in, 16)
        act.dma_start(gain[:, :], a["gains"][0]).then_inc(gain_in, 16)
        load_x()

        sums = [0]

        def squares(n_tiles, src, n, ready=None):
            act.wait_ge(ssq_clear, n + 1)
            for i in range(n_tiles):
                if ready is not None:
                    act.wait_ge(*ready[i])
                if sums[0]:
                    act.wait_ge(ssq_ready, sums[0])
                rows = ROWS[i]
                act.activation(sq[0:rows, :], src[0:rows, i, :], ACT.Square, accum_out=sm["ssq"][0:rows, i:i + 1])\
                   .then_inc(ssq_ready, 1)
                sums[0] += 1
            act.wait_ge(var_ready, n + 1)
            act.activation(sm["rstd"][:, 0:n_tiles], sm["rstd"][:, 0:n_tiles], ACT.Sqrt).then_inc(std_ready, 1)

        def high_parts(n_tiles):
            for i in range(n_tiles):
                for half in range(2):
                    b, _ = wait_filled()
                    act.activation(actH[:, half * 4:half * 4 + 4, T0[i]:T0[i] + ROWS[i]],
                                   bank(b, 4 * ROWS[i]).rearrange("p (k t) -> p k t", k=4), ACT.Copy)\
                       .then_inc(acth_done, 1)

        def next_gain(n, tiles):
            act.wait_ge(xn_ready, tiles)
            act.dma_start(gain[:, :], a["gains"][n]).then_inc(gain_in, 16)

        act.wait_ge(memx_in, 16)
        squares(MT, memx, 0)
        high_parts(MT)
        next_gain(1, MT)
        act.wait_ge(x_in, 32)
        squares(TILES, xres, 1)
        for q in range(N_CK * 4):
            b, value = wait_filled()
            act.activation(mk_sb[:, q, :], bank(b, MEM), ACT.Copy).then_inc(emptied[b], 1)
            act.wait_ge(emptied[b], value + 1)
        act.dma_start(o["mkT"].rearrange("(k p) m -> p k m", p=P), mk_sb[:, :, :]).then_inc(out_done, 16)
        for c in range(N_CV):
            for i in range(MT):
                b, value = wait_filled()
                act.activation(mv_sb[:, i, c * CHUNK:(c + 1) * CHUNK], bank(b), ACT.Copy).then_inc(emptied[b], 1)
                act.wait_ge(emptied[b], value + 1)
        act.dma_start(o["mv"].rearrange("(i p) d -> p i d", p=P), mv_sb[:, :, :]).then_inc(out_done, 16)
        high_parts(TILES)
        act.wait_ge(out_done, 32)
        act.wait_ge(xn_ready, MT + TILES)

        for s in range(2):
            act.dma_start(par[:, s, :], a["par"][s]).then_inc(par_in[s], 16)
        act.dma_start(lamp[:, :], a["lamp"]).then_inc(lamp_in, 16)
        act.dma_start(sm["gsub"], a["gsub"]).then_inc(lamp_in, 16)

        def projections(j, s, first=False, j_old=None, stored=None):
            if not first:
                act.wait_ge(conv_done, j_old + 1)
            for part in range(2):
                b, _ = wait_filled()
                if part == 0:
                    act.activation(rxp[:, s, 3:3 + HALF], bank(b, HALF), ACT.Copy).then_inc(emptied[b], 1)
                else:
                    act.activation(rxp[:, s, 3 + HALF:3 + NP_TOK], bank(b, NP_TOK - HALF), ACT.Copy)
                    act.activation(rxp[:, s, SEG + 3:XPW], ps[:, b * BANK + NP_TOK - HALF:b * BANK + HALF],
                                   ACT.Copy).then_inc(emptied[b], 1)
            if not first:
                act.wait_ge(yrec_ready, j_old + 1)
                act.dma_start(par[:, s, :], a["par"][j]).then_inc(par_in[s], 16)
            for dst, func in ((gel, ACT.Gelu), (sgr, ACT.Sigmoid), (sga, ACT.Sigmoid)):
                if dst is sga and not first:
                    act.wait_ge(sa_store[s], stored)
                for part in range(2):
                    b, value = wait_filled()
                    act.activation(dst[:, s, part * HALF:(part + 1) * HALF], bank(b, HALF), func).then_inc(emptied[b], 1)
                    if dst is sga:
                        act.wait_ge(emptied[b], value + 1)
            act.dma_start(sa_d[j], sga[:, s, :]).then_inc(sa_store[s], 16)

        def gate_block(j, s, first=False):
            for w, (dst, col) in enumerate(((gate_r, PAR_BA), (gate_i, PAR_BX))):
                for cut in (slice(0, CA_), slice(CA_, CW)):
                    b, value = wait_filled()
                    if w == 0 and cut.start == 0 and not first:
                        act.wait_ge(yrec_ready, j)
                    act.activation(dst[:, cut], ps[:, b * BANK:b * BANK + cut.stop - cut.start], ACT.Sigmoid,
                                   bias=par[:, s, col:col + 1]).then_inc(emptied[b], 1)
                    act.wait_ge(emptied[b], value + 1)
            if first:
                act.wait_ge(lam_ready, 1)
            act.activation(lru_a[:, 0:CW], gate_r[:, 0:CW], ACT.Exp, scale=sm["ncall"][:, bass.ds(j, 1)])\
               .then_inc(gate_ready, 1)
            act.activation(lru_t[:, 0:CW], gate_r[:, 0:CW], ACT.Tanh, scale=sm["pcall"][:, bass.ds(j, 1)])\
               .then_inc(gate_ready, 1)
            act.wait_ge(m_ready, j + 1)
            act.activation(lru_m[:, 0:CW], lru_m[:, 0:CW], ACT.Sqrt).then_inc(root_ready, 1)
            act.wait_ge(yrec_ready, j + 1)
            act.dma_start(r_d[j], yrec[:, s, :]).then_inc(r_store[s], 16)

        projections(0, 0, first=True)
        sp = sm["sp"]
        act.wait_ge(sp_neg, 1)
        act.activation(sp[:, 16:24], sp[:, 8:16], ACT.Exp, scale=-1.0).then_inc(sp_exp, 1)
        act.wait_ge(sp_one, 1)
        act.activation(sp[:, 32:40], sp[:, 24:32], ACT.Ln).then_inc(sp_ln, 1)
        act.wait_ge(lam_sums, 1)
        act.activation(sm["lamt"][:, 2:4], sm["lamt"][:, 0:2], ACT.Exp).then_inc(lam_exp, 1)
        projections(1, 1, first=True)
        gate_block(0, 0, first=True)
        with act.Fori(0, N_RG // 2 - 1) as i:
            turns.enter(i, 24)
            projections(i * 2 + 2, 0, j_old=i * 2, stored=i * 16 + 16)
            gate_block(i * 2 + 1, 1)
            projections(i * 2 + 3, 1, j_old=i * 2 + 1, stored=i * 16 + 16)
            gate_block(i * 2 + 2, 0)
            turns.leave(N_RG // 2 - 1)

        def turned(u):
            kind, c, i = TUNITS[u]
            if kind == "v":
                return
            n = sum(1 for k, _, _ in TUNITS[:u + 1] if k != "v")
            if kind == "k":
                act.wait_ge(rot_ready, n)
                act.dma_start(o["k"][T0[i]:T0[i] + ROWS[i], c * CHUNK:(c + 1) * CHUNK],
                              rot[0:ROWS[i], (n - 1) % 2, :]).then_inc(k_store[(n - 1) % 2], 16)
            b, _ = wait_filled()
            dst = kT if kind == "k" else qT
            act.activation(dst[:, 4 * c:4 * c + 4, T0[i]:T0[i] + ROWS[i]],
                           bank(b, 4 * ROWS[i]).rearrange("p (h t) -> p h t", h=4), ACT.Copy,
                           scale=1.0 if kind == "k" else DK ** -0.5).then_inc(emptied[b], 1)

        for u, (kind, c, i) in enumerate(TUNITS):
            if u == 0:
                skip(1)
                gate_block(N_RG - 1, 1)
                act.dma_start(o["cstate"], cstate[:, :, :]).then_inc(out_done, 16)
                act.dma_start(o["hstate"], hstate[:, :, :]).then_inc(out_done, 16)
                for s in range(2):
                    act.wait_ge(sa_store[s], 16 * N_RG // 2)
                    act.wait_ge(r_store[s], 16 * N_RG // 2)
                act.wait_ge(out_done, 64)
                for name, t in (("ropec", ropec), ("ropes", ropes), ("ropen", ropen)):
                    act.dma_start(t[:, :, :], a[name]).then_inc(rope_in, 16)
                act.dma_start(mask[0:1, :], a["mask"]).then_inc(mask_in, 16)
                continue
            if kind == "v":
                b, value = wait_filled()
                act.activation(vtok[0:ROWS[i], i, c * CHUNK:(c + 1) * CHUNK], bank(b, CHUNK, ROWS[i]),
                               ACT.Copy).then_inc(emptied[b], 1)
                if (c, i) == (1, TILES - 1):
                    act.wait_ge(emptied[b], value + 1)
                    act.dma_start(o["v"][0:NP_TOK].rearrange("(i p) d -> p i d", p=P), vtok[:, 0:4, :])\
                       .then_inc(out_done, 16)
                    act.dma_start(o["v"][NP_TOK:NT], vtok[0:NS_TOK, 4, :]).then_inc(out_done, 16)
            else:
                skip(1)
            turned(u - 1)
        turned(len(TUNITS) - 1)
        for s in range(2):
            act.wait_ge(k_store[s], 16 * TILES)

        def load_merge(i):
            t = slice(T0[i], T0[i] + ROWS[i])
            act.dma_start(sat[:, :, 0:ROWS[i]], sa_d[:, :, t].rearrange("k p t -> p k t")).then_inc(sat_in, 16)
            act.dma_start(rt[:, :, 0:ROWS[i]], r_d[:, :, t].rearrange("k p t -> p k t")).then_inc(sat_in, 16)

        def load_cache(h):
            act.dma_start(ckv0[:, 0, :], a["ckT"][h]).then_inc(ckv_in, 16)
            act.dma_start(ckv0[:, 1, :].rearrange("p (k d) -> p k d", k=4),
                          a["cv"][:, :, h * DV:(h + 1) * DV]).then_inc(ckv_in, 16)

        def exps(u):
            i, h = UNITS[u]
            rows = ROWS[i]
            act.wait_ge(nm_ready, u + 1)
            if u >= 2:
                act.wait_ge(t_ready, u - 1 if i < TILES - 1 else u)
            for s in range(2):
                if i < TILES - 1:
                    n = P * (i + 1)
                    dst, src = prob[:, u % 2, s, 0:n], bank(2 * (u % 2) + s, n)
                else:
                    dst, src = probs[0:rows, s, :], ps[0:rows, 2 * s * BANK:2 * s * BANK + NT]
                col = 2 * (u % 2) + s
                ins = act.activation(dst, src, ACT.Exp, bias=sm["nmax"][0:rows, col:col + 1],
                                     accum_out=sm["z"][0:rows, col:col + 1])
            ins.then_inc(p_ready, 1)

        def copy_turned(u):
            i, h = UNITS[u]
            rows = ROWS[i]
            b = 4 + u % 2
            act.wait_ge(t_ready, u + 1)
            if u >= 2:
                act.wait_ge(pv_done, u - 1)
            if i < TILES - 1:
                n = P * (i + 1)
                act.activation(aT[:, u % 2, 0:n], bank(b, n), ACT.Copy).then_inc(aT_ready, 1)
            else:
                n = (PAST // P) * rows
                act.activation(aT[:, u % 2, 0:n], bank(b, n), ACT.Copy)
                act.activation(aT[0:rows, u % 2, n:n + rows], ps[0:rows, b * BANK + n:b * BANK + n + rows],
                               ACT.Copy).then_inc(aT_ready, 1)

        for i in range(TILES):
            rows = ROWS[i]
            load_merge(i)
            if i == TILES - 1:
                load_cache(0)
            for h in range(HEADS):
                u = i * HEADS + h
                exps(u)
                if i == TILES - 1:
                    copy_turned(u)
                    if h + 1 < HEADS:
                        act.wait_ge(pv_done, u + 1)
                        load_cache(h + 1)
                elif h > 0:
                    copy_turned(u - 1)
            if i < TILES - 1:
                copy_turned(i * HEADS + HEADS - 1)
            act.wait_ge(pv_done, HEADS * (i + 1))
            act.activation(osb[0:rows, :], ps[0:rows, 6 * BANK:8 * BANK], ACT.Copy).then_inc(osb_ready, 1)
            act.wait_ge(ovar_ready, i + 1)
            act.activation(sm["orstd"][0:rows, :], sm["orstd"][0:rows, :], ACT.Sqrt).then_inc(ostd_ready, 1)
            act.wait_ge(merged, i + 1)
            act.activation(actH[:, :, T0[i]:T0[i] + rows], sat[:, :, 0:rows], ACT.Copy).then_inc(mh_done, 1)
            act.wait_ge(ml_done, i + 1)

        act.wait_ge(out_done, 96)
        load_x()
        next_gain(2, MT + TILES)

        def sums_of(n_groups):
            groups = [turns.take() for _ in range(n_groups * TILES)]
            return [(emptied[b], value + 1) for b, value in groups[-TILES:]]

        ready = sums_of(N_OUT)
        squares(TILES, xres, 2, ready)
        high_parts(TILES)
        next_gain(3, MT + 2 * TILES)
        act.dma_start(mkT[:, 0, :, :], o["mkT"].rearrange("(k p) m -> p k m", p=P)).then_inc(mem_in, 16)
        act.dma_start(mkT[:, 1, :, :], a["cmkT"].rearrange("(k p) m -> p k m", p=P)).then_inc(mem_in, 16)
        act.dma_start(mvt[:, 0, :, :], o["mv"].rearrange("(i p) d -> p i d", p=P)).then_inc(mem_in, 16)
        act.dma_start(mvt[:, 1, :, :], a["cmv"].rearrange("(i p) d -> p i d", p=P)).then_inc(mem_in, 16)
        for q in range(N_CQ * 4):
            for part in range(2):
                b, _ = wait_filled()
                act.activation(qcT[:, q, part * HALF:(part + 1) * HALF], bank(b, HALF), ACT.Copy,
                               scale=CA_DH ** -0.5).then_inc(emptied[b], 1)

        def cross_exps(i):
            rows = ROWS[i]
            act.wait_ge(cm_ready, i + 1)
            if i >= 2:
                act.wait_ge(ct_ready, i - 1)
            for h in range(CA_HEADS):
                c = 4 * (i % 2) + h
                at = 2 * (i % 2) * BANK + h * MEM
                ins = act.activation(cp[0:rows, i % 2, h * MEM:(h + 1) * MEM], ps[0:rows, at:at + MEM],
                                     ACT.Exp, bias=sm["nmax"][0:rows, c:c + 1], accum_out=sm["mz"][0:rows, c:c + 1])
            ins.then_inc(ce_ready, 1)

        cross_exps(0)
        for i in range(TILES):
            rows = ROWS[i]
            if i + 1 < TILES:
                cross_exps(i + 1)
            act.wait_ge(ct_ready, i + 1)
            if i >= 1:
                act.wait_ge(co_ready, i)
            for m in range(2):
                ins = act.activation(cpT[:, m * 4 * rows:(m + 1) * 4 * rows], bank(4 + m, 4 * rows), ACT.Copy)
            ins.then_inc(cpT_ready, 1)
            act.wait_ge(co_ready, i + 1)
            for m in range(2):
                act.activation(actH[:, 4 * m:4 * m + 4, T0[i]:T0[i] + rows],
                               bank(6 + m, 4 * rows).rearrange("p (k t) -> p k t", k=4), ACT.Copy).then_inc(ch_done, 1)

        ready = sums_of(N_CO)
        squares(TILES, xres, 3, ready)
        act.dma_start(x2_d[0:NP_TOK].rearrange("(i p) d -> p i d", p=P), xres[:, 0:4, :]).then_inc(x2_store, 16)
        act.dma_start(x2_d[NP_TOK:NT], xres[0:NS_TOK, 4, :]).then_inc(x2_store, 16)
        high_parts(TILES)
        next_gain(4, MT + 3 * TILES)
        act.dma_start(keys[:, :, :], a["keysT"]).then_inc(keys_in, 16)
        act.dma_start(iota16[:, :], a["iota"][:, 0:TOPK]).then_inc(iota16_in, 16)
        act.wait_ge(x2_store, 32)
        for q in range(N_PQ * 4):
            for part in range(2):
                b, _ = wait_filled()
                act.activation(pqT[:, q, part * HALF:(part + 1) * HALF], bank(b, HALF), ACT.Copy)\
                   .then_inc(emptied[b], 1)
        for i in range(TILES):
            rows = ROWS[i]
            act.wait_ge(score_ready, i + 1)
            act.activation(ssb[0:rows, i, :, :].rearrange("p h n -> p (h n)"),
                           ps[0:rows, 4 * (i % 2) * BANK:4 * (i % 2 + 1) * BANK], ACT.Copy).then_inc(ssb_ready, 1)

        act.sem_inc(ge_ready, 2)

        def gelu(e, n):
            act.wait_ge(u_done, n + 1)
            act.activation(ge[:, e, :].rearrange("p (c n) -> p c n", c=2), halves(2 * (e % 2)), ACT.Gelu)\
               .then_inc(ge_ready, 1)

        def gelu_early(e, n, stored):
            if stored is not None:
                act.wait_ge(ge_store[e], stored)
            gelu(e, n)
            act.wait_ge(ge_ready, n + 3)
            act.dma_start(ge_d[n], ge[:, e, :]).then_inc(ge_store[e], 16)

        for g in range(2):
            for e in range(EG):
                gelu_early(e, EG * g + e, 16 * g if g else None)
        with act.Fori(0, RANK_GROUPS - 2) as i:
            for e in range(EG):
                gelu_early(e, i * EG + (2 * EG + e), i * 16 + 32)
        act.wait_ge(gexp_in, TILES)
        for rows, tiles in ((P, slice(0, TILES - 1)), (NS_TOK, slice(TILES - 1, TILES))):
            g = chosen[0:rows, tiles, 2, :]
            act.activation(g, g, ACT.Exp).then_inc(gexp_out, 1)
        for i in range(TILES):
            rows, at = ROWS[i], (4 + i % 4) * BANK
            act.wait_ge(chT_ready, i + 1)
            act.activation(chosenT[:, :, T0[i]:T0[i] + rows],
                           ps[:, at:at + 3 * P].rearrange("p (s t) -> p s t", s=3)[:, :, 0:rows],
                           ACT.Copy).then_inc(chT_copied, 1)

        act.sem_inc(c_copied, 4)

        def c_group(i, n, stored):
            for k in range(8):
                s, at = k // 4, 8 * (k % 4)
                if k % 4 == 0 and stored is not None:
                    act.wait_ge(c_store[s], stored)
                for half in range(2):
                    q = 16 * n + 2 * k + half
                    act.wait_ge(c_filled, i * 16 + (q + 5))
                    act.activation(cst[:, s, :, at + 4 * half:at + 4 * half + 4],
                                   bank(4 + q % 4).rearrange("p (t e) -> p e t", t=4), ACT.Copy).then_inc(c_copied, 1)
                if k % 2 == 0:
                    gelu_early(k // 2, i * EG + (EG * (RANK_GROUPS + n) + k // 2), i * 16 + 16 * (RANK_GROUPS + n))
                if k % 4 == 3:
                    act.wait_ge(c_copied, i * 16 + (16 * n + 2 * k + 2 + 4))
                    act.dma_start(c_d[i * 2 + (2 * n + s)], cst[:, s, :, :]).then_inc(c_store[s], 16)

        c_group(0, 0, None)
        with act.Fori(0, C_GROUPS - 1) as i:
            c_group(i, 1, i * 16 + 16)
        for e in range(EG):
            gelu_early(e, EG * (EARLY - 1) + e, 16 * (EARLY - 1))

        for s in range(2):
            act.wait_ge(c_store[s], 16 * C_GROUPS)
        act.sem_inc(gh_done, 2)

        def load_c(g, s):
            act.dma_start(cg[:, s], c_d[:, :, bass.ts(g, EG), :].rearrange("b p e t -> p b e t")).then_inc(c_in[s], 16)

        def load_ge(e, n):
            act.dma_start(ge[:, e, :], ge_d[n]).then_inc(ge_in[e], 16)

        def high(e, s, n, used):
            act.wait_ge(gf_ready, n + 3)
            if used is not None:
                act.wait_ge(v_done, used)
            act.activation(gH[:, s, e, :], gf[:, e % 2, :], ACT.Copy).then_inc(gh_done, 1)

        load_c(0, 0)
        for e in range(EG):
            act.wait_ge(ge_store[e], 16 * EARLY)
            load_ge(e, e)
        load_c(1, 1)
        for g in range(2):
            for e in range(EG):
                high(e, g, EG * g + e, None)
                load_ge(e, EG * (g + 1) + e)
            load_c(g + 2, g)
        with act.Fori(0, EARLY // 2 - 2) as i:
            for s in range(2):
                for e in range(EG):
                    n = EG * (s + 2) + e
                    high(e, s, i * (2 * EG) + n, i * (2 * KT) + KT * (s + 1))
                    load_ge(e, i * (2 * EG) + (n + EG))
                load_c(i * 2 + (4 + s), s)
        for g in (EARLY - 2, EARLY - 1):
            for e in range(EG):
                high(e, g % 2, EG * g + e, KT * (g - 1))
                if g == EARLY - 2:
                    load_ge(e, EG * (g + 1) + e)
            load_c(g + 2, g % 2)

        def gelu_and_high(e, s, n, used):
            act.wait_ge(gf_ready, n - 1)
            gelu(e, n)
            high(e, s, n, used)

        for e in range(EG):
            gelu_and_high(e, 0, EG * EARLY + e, KT * (EARLY - 1))
        with act.Fori(0, LATE_PAIRS) as i:
            for s in range(2):
                load_c(i * 2 + (EARLY + 2 + s), s)
                for e in range(EG):
                    n = EG * (EARLY + 1 + s) + e
                    gelu_and_high(e, 1 - s, i * (2 * EG) + n, i * (2 * KT) + KT * (EARLY + s))
        for e in range(EG):
            gelu_and_high(e, 1, EG * (GROUPS - 1) + e, KT * (GROUPS - 2))

        act.wait_ge(v_done, KT * GROUPS)
        act.wait_ge(gl_done, EG * GROUPS)
        act.dma_start(x2b[:, 0:4, :], x2_d[0:NP_TOK].rearrange("(i p) d -> p i d", p=P)).then_inc(x2_in, 16)
        act.dma_start(x2b[0:NS_TOK, 4, :], x2_d[NP_TOK:NT]).then_inc(x2_in, 16)
        for i in range(TILES):
            rows = ROWS[i]
            act.wait_ge(res_ready, i + 1)
            if i >= 2:
                act.wait_ge(y_store[i % 2], 16 * (i // 2))
            act.activation(yout[0:rows, i % 2, :], x2b[0:rows, i, :], ACT.Square,
                           accum_out=sm["ssq"][0:rows, i:i + 1]).then_inc(ssq_ready, 1)
            act.wait_ge(var_ready, 4 + i + 1)
            act.activation(sm["rstd"][0:rows, i:i + 1], sm["rstd"][0:rows, i:i + 1], ACT.Sqrt).then_inc(std_ready, 1)
            act.wait_ge(y_ready, i + 1)
            act.dma_start(o["y"][T0[i]:T0[i] + rows, :], yout[0:rows, i % 2, :]).then_inc(y_store[i % 2], 16)
        for s in range(2):
            act.wait_ge(y_store[s], 16 * ((TILES + 1 - s) // 2))

    @block.vector
    def _(ve):
        turns = Turns()
        step = Steps(ve, ve_step)

        def wait_filled():
            b, value = turns.take()
            ve.wait_ge(filled[b], value)
            return b, value

        def skip(n):
            for _ in range(n):
                turns.take()

        xn_groups = []
        sums = [0]

        def normalise(n_tiles, src, n):
            first = len(xn_groups)
            rstd = sm["rstd"][:, 0:n_tiles]
            step.done(ve.memset(sm["ssq"], 0.0))
            ve.sem_inc(ssq_clear, 1)
            sums[0] += n_tiles
            ve.wait_ge(ssq_ready, sums[0])
            ve.tensor_scalar(rstd, sm["ssq"][:, 0:n_tiles], 1.0 / D, RMS_EPS, ALU.mult, ALU.add).then_inc(var_ready, 1)
            ve.wait_ge(std_ready, n + 1)
            step.done(ve.reciprocal(rstd, rstd))
            ve.wait_ge(gain_in, 16 * (n + 1))
            for i in range(n_tiles):
                if first + i >= 2:
                    b, value = xn_groups[first + i - 2]
                    ve.wait_ge(filled[b], value)
                rows = ROWS[i]
                ve.scalar_tensor_tensor(xn[0:rows, (first + i) % 2, :], src[0:rows, i, :], sm["rstd"][0:rows, i:i + 1],
                                        gain[0:rows, :], ALU.mult, ALU.mult).then_inc(xn_ready, 1)
                if n == 1 and i == 0:
                    skip(N_CK * 4 + N_CV * MT)
                take = [turns.take(), turns.take()]
                xn_groups.append(take[1])
                todo.append((first + i, i, take))
                if i >= 1:
                    low_parts(*todo.pop(0))
            low_parts(*todo.pop(0))

        todo = []

        def low_parts(tile, i, take):
            for half, (b, value) in enumerate(take):
                ve.wait_ge(acth_done, 2 * tile + half + 1)
                cut = (slice(None), slice(half * 4, half * 4 + 4), slice(T0[i], T0[i] + ROWS[i]))
                ve.tensor_tensor(actL[cut], bank(b, 4 * ROWS[i]).rearrange("p (k t) -> p k t", k=4),
                                 actH[cut].bitcast(F32), ALU.subtract).then_inc(emptied[b], 1)

        normalise(MT, memx, 0)
        normalise(TILES, xres, 1)

        sp, lamt, lamv = sm["sp"], sm["lamt"], sm["lamv"]
        neg, mag, exp_, one, log = (sp[:, 8 * k:8 * k + 8] for k in range(5))
        ve.wait_ge(lamp_in, 32)
        step.done(ve.tensor_scalar(neg, lamp[:, 4 * DK:4 * DK + KT], -1.0, None, ALU.mult))
        ve.tensor_tensor(mag, neg, lamp[:, 4 * DK:4 * DK + KT], ALU.max).then_inc(sp_neg, 1)
        ve.wait_ge(sp_exp, 1)
        ve.tensor_scalar(one, exp_, 1.0, None, ALU.add).then_inc(sp_one, 1)
        for k in range(2):
            step.done(ve.tensor_tensor(lamp[:, 2 * k * DK:(2 * k + 1) * DK], lamp[:, 2 * k * DK:(2 * k + 1) * DK],
                                       lamp[:, (2 * k + 1) * DK:(2 * k + 2) * DK], ALU.mult))
        step.done(ve.tensor_reduce(lamt[:, 0:1], lamp[:, 0:DK], AX, ALU.add))
        ve.tensor_reduce(lamt[:, 1:2], lamp[:, 2 * DK:3 * DK], AX, ALU.add).then_inc(lam_sums, 1)
        ve.wait_ge(sp_ln, 1)
        step.done(ve.tensor_scalar(mag, one, -1.0, None, ALU.add))
        step.done(ve.tensor_scalar(one, mag, 0.0, None, ALU.is_equal))
        step.done(ve.tensor_scalar(mag, mag, 1e-30, None, ALU.max))
        step.done(ve.reciprocal(mag, mag))
        step.done(ve.tensor_tensor(mag, mag, log, ALU.mult))
        step.done(ve.tensor_tensor(mag, mag, exp_, ALU.mult))
        step.done(ve.tensor_tensor(exp_, exp_, one, ALU.mult))
        step.done(ve.tensor_tensor(mag, mag, exp_, ALU.add))
        step.done(ve.tensor_scalar(neg, neg, 0.0, None, ALU.max))
        step.done(ve.tensor_tensor(neg, neg, mag, ALU.add))
        step.done(ve.tensor_scalar(sm["pcall"], neg, RG_C, None, ALU.mult))
        ve.wait_ge(lam_exp, 1)
        step.done(ve.tensor_tensor(lamt[:, 4:5], lamt[:, 2:3], lamt[:, 3:4], ALU.subtract))
        step.done(ve.tensor_scalar(lamv[:, 1:2], lamt[:, 4:5], LAM_INIT, -1.0, ALU.add, ALU.mult))
        step.done(ve.memset(lamv[:, 0:1], 1.0))
        step.done(ve.tensor_scalar(sm["gsub"], sm["gsub"], 1.0 - LAM_INIT, None, ALU.mult))
        for s in range(2):
            step.done(ve.memset(rxp[:, s, 0:CONVW - 1], 0.0))
        ve.tensor_scalar(sm["ncall"], neg, -RG_C, None, ALU.mult).then_inc(lam_ready, 1)

        def convolve(j, s, arrived, j_old=None):
            groups = [turns.take(), turns.take()]
            ve.wait_ge(par_in[s], arrived)
            if j_old is not None:
                ve.wait_ge(yrec_ready, j_old + 1)
            step.done(ve.tensor_copy(rxp[:, s, SEG:SEG + 3], par[:, s, PAR_SC:PAR_SC + 3]))
            for b, value in groups:
                ve.wait_ge(emptied[b], value + 1)
            step.done(ve.tensor_copy(cstate[:, bass.ds(j, 1), 0:3], rxp[:, s:s + 1, NP_TOK:NP_TOK + 3]))
            step.done(ve.tensor_copy(cstate[:, bass.ds(j, 1), 3:6], rxp[:, s:s + 1, SEG + NS_TOK:SEG + NS_TOK + 3]))
            step.done(ve.tensor_scalar(conv[:, s, 0:CW], rxp[:, s, 0:CW], par[:, s, PAR_CW:PAR_CW + 1],
                                       par[:, s, PAR_CB:PAR_CB + 1], ALU.mult, ALU.add))
            for w in range(1, CONVW):
                ins = ve.scalar_tensor_tensor(conv[:, s, 0:CW], rxp[:, s, w:w + CW], par[:, s, PAR_CW + w:PAR_CW + w + 1],
                                              conv[:, s, 0:CW], ALU.mult, ALU.add)
                if w < CONVW - 1:
                    step.done(ins)
            ins.then_inc(conv_done, 1)
            skip(6)

        def recur(j, s, stored=None):
            skip(4)
            ve.wait_ge(gate_ready, j * 2 + 2)
            step.done(ve.tensor_scalar(lru_m[:, 0:CW], lru_t[:, 0:CW], 1.0, None, ALU.add))
            step.done(ve.reciprocal(lru_m[:, 0:CW], lru_m[:, 0:CW]))
            ve.scalar_tensor_tensor(lru_m[:, 0:CW], lru_t[:, 0:CW], 2.0, lru_m[:, 0:CW], ALU.mult, ALU.mult)\
              .then_inc(m_ready, 1)
            step.done(ve.tensor_tensor(gate_i[:, 0:CW], gate_i[:, 0:CW], conv[:, s, 0:CW], ALU.mult))
            ve.wait_ge(root_ready, j + 1)
            step.done(ve.tensor_tensor(gate_i[:, 0:CW], gate_i[:, 0:CW], lru_m[:, 0:CW], ALU.mult))
            step.done(ve.tensor_tensor_scan(lru_h[:, 0:NP_TOK], lru_a[:, 0:NP_TOK], gate_i[:, 0:NP_TOK], 0.0,
                                            ALU.mult, ALU.add))
            step.done(ve.tensor_tensor_scan(lru_h[:, NP_TOK:NT], lru_a[:, SEG:CW], gate_i[:, SEG:CW],
                                            par[:, s, PAR_H0:PAR_H0 + 1], ALU.mult, ALU.add))
            step.done(ve.tensor_copy(hstate[:, bass.ds(j, 1), 0:1], lru_h[:, NP_TOK - 1:NP_TOK].unsqueeze(1)))
            step.done(ve.tensor_copy(hstate[:, bass.ds(j, 1), 1:2], lru_h[:, NT - 1:NT].unsqueeze(1)))
            step.done(ve.tensor_tensor(lru_h[:, :], lru_h[:, :], gel[:, s, :], ALU.mult))
            if stored is not None:
                ve.wait_ge(r_store[s], stored)
            ve.tensor_tensor(yrec[:, s, :], lru_h[:, :], sgr[:, s, :], ALU.mult).then_inc(yrec_ready, 1)
            ve.wait_ge(yrec_ready, j + 1)

        convolve(0, 0, 16)
        convolve(1, 1, 16)
        recur(0, 0)
        with ve.Fori(0, N_RG // 2 - 1) as i:
            turns.enter(i, 24)
            step.enter(i, 2 * (3 + CONVW - 1 + 1 + 8))
            convolve(i * 2 + 2, 0, i * 16 + 32, i * 2)
            recur(i * 2 + 1, 1, None)
            convolve(i * 2 + 3, 1, i * 16 + 32, i * 2 + 1)
            recur(i * 2 + 2, 0, i * 16 + 16)
            turns.leave(N_RG // 2 - 1)
            step.leave(N_RG // 2 - 1)

        rots = []
        turned_groups = {}

        def turned(u):
            if TUNITS[u][0] != "v":
                turned_groups[u] = turns.take()

        for u, (kind, c, i) in enumerate(TUNITS):
            b, value = turns.take()
            if u == 0:
                recur(N_RG - 1, 1, None)
                ve.wait_ge(rope_in, 48)
            if kind != "v":
                rows, r = ROWS[i], len(rots) % 2
                ve.wait_ge(filled[b], value)
                src = bank(b, CHUNK, rows).rearrange("p (h s n) -> p h s n", s=2, n=32)
                r1 = rot1[0:rows, :].rearrange("p (h s n) -> p h s n", s=2, n=32)
                r2 = rot2[0:rows, :].rearrange("p (h s n) -> p h s n", s=2, n=32)
                heads = [rows, CHUNK // DK, 32]
                if rots:
                    ve.wait_ge(rot_ready, len(rots))
                ve.tensor_tensor(rot1[0:rows, :].rearrange("p (h n) -> p h n", n=32),
                                 bank(b, CHUNK, rows).rearrange("p (h n) -> p h n", n=32),
                                 ropec[0:rows, i:i + 1, :].broadcast_to([rows, CHUNK // 32, 32]), ALU.mult)
                ve.tensor_tensor(r2[:, :, 0, :], src[:, :, 1, :], ropen[0:rows, i:i + 1, :].broadcast_to(heads), ALU.mult)
                ve.tensor_tensor(r2[:, :, 1, :], src[:, :, 0, :], ropes[0:rows, i:i + 1, :].broadcast_to(heads), ALU.mult)\
                  .then_inc(emptied[b], 1)
                ve.wait_ge(emptied[b], value + 1)
                if len(rots) >= 2:
                    before = rots[-2]
                    tb, tv = turned_groups[before]
                    ve.wait_ge(filled[tb], tv)
                    if TUNITS[before][0] == "k":
                        ve.wait_ge(k_store[r], 16 * ((len(rots) - 2) // 2 + 1))
                ve.tensor_tensor(rot[0:rows, r, :], rot1[0:rows, :], rot2[0:rows, :], ALU.add).then_inc(rot_ready, 1)
                rots.append(u)
            if u >= 1:
                turned(u - 1)
        turned(len(TUNITS) - 1)

        def maxima(u):
            i, h = UNITS[u]
            rows = ROWS[i]
            ve.wait_ge(sc_ready, u + 1)
            if u >= 2:
                ve.wait_ge(p_ready, u - 1)
            if i < TILES - 1:
                n = P * (i + 1)
                src = ps[:, 2 * (u % 2) * BANK:(2 * (u % 2) + 2) * BANK].rearrange("p (s n) -> p s n", s=2)[:, :, 0:n]
            else:
                src = ps[0:rows, 0:4 * BANK].rearrange("p (s n) -> p s n", s=2)[:, :, 0:NT]
            ve.tensor_reduce(sm["nmax"][0:rows, 2 * (u % 2):2 * (u % 2) + 2], src, AX, ALU.max, negate=True)\
              .then_inc(nm_ready, 1)

        def combine(u):
            i, h = UNITS[u]
            rows = ROWS[i]
            if i < TILES - 1:
                p1, p2 = (prob[:, u % 2, s, 0:P * (i + 1)] for s in range(2))
            else:
                p1, p2 = (probs[0:rows, s, :] for s in range(2))
            rz = sm["pk"][0:rows, 0:2]
            ve.wait_ge(p_ready, u + 1)
            if u >= 1:
                ve.wait_ge(a_ready, u)
            step.done(ve.reciprocal(rz, sm["z"][0:rows, 2 * (u % 2):2 * (u % 2) + 2]))
            step.done(ve.tensor_tensor(rz, rz, lamv[0:rows, :], ALU.mult))
            step.done(ve.tensor_scalar(p2, p2, rz[:, 1:2], None, ALU.mult))
            ve.scalar_tensor_tensor(p1, p1, rz[:, 0:1], p2, ALU.mult, ALU.add).then_inc(a_ready, 1)

        for i in range(TILES):
            rows = ROWS[i]
            for h in range(HEADS):
                u = i * HEADS + h
                maxima(u)
                if i == TILES - 1:
                    combine(u)
                elif h > 0:
                    combine(u - 1)
            if i < TILES - 1:
                combine(i * HEADS + HEADS - 1)
            ve.wait_ge(osb_ready, i + 1)
            step.done(ve.tensor_tensor(osq[0:rows, :], osb[0:rows, :], osb[0:rows, :], ALU.mult))
            step.done(ve.tensor_reduce(sm["oss"][0:rows, :], osq[0:rows, :].rearrange("p (h d) -> p h d", h=HEADS),
                                       AX, ALU.add))
            ve.tensor_scalar(sm["orstd"][0:rows, :], sm["oss"][0:rows, :], 1.0 / DV, SUBLN_EPS, ALU.mult, ALU.add)\
              .then_inc(ovar_ready, 1)
            ve.wait_ge(ostd_ready, i + 1)
            step.done(ve.reciprocal(sm["orstd"][0:rows, :], sm["orstd"][0:rows, :]))
            heads = osb[0:rows, :].rearrange("p (h d) -> p h d", h=HEADS)
            ve.tensor_tensor(heads, heads, sm["orstd"][0:rows, :].unsqueeze(2).broadcast_to([rows, HEADS, DV]),
                             ALU.mult).then_inc(on_ready, 1)
            ve.wait_ge(yt_ready, i + 1)
            ve.wait_ge(sat_in, 32 * (i + 1))
            for m in range(2):
                part = sat[:, 4 * m:4 * m + 4, 0:rows]
                step.done(ve.scalar_tensor_tensor(part, bank(4 + m, 4 * rows).rearrange("p (k t) -> p k t", k=4),
                                                  sm["gsub"], part, ALU.mult, ALU.mult))
            ve.tensor_tensor(sat[:, :, 0:rows], sat[:, :, 0:rows], rt[:, :, 0:rows], ALU.add).then_inc(merged, 1)
            ve.wait_ge(mh_done, i + 1)
            t = slice(T0[i], T0[i] + rows)
            ve.tensor_tensor(actL[:, :, t], sat[:, :, 0:rows], actH[:, :, t].bitcast(F32), ALU.subtract)\
              .then_inc(ml_done, 1)

        def add_products():
            for c in range(2):
                for i in range(TILES):
                    b, _ = wait_filled()
                    part = xres[0:ROWS[i], i, c * CHUNK:(c + 1) * CHUNK]
                    ve.tensor_tensor(part, part, bank(b, CHUNK, ROWS[i]), ALU.add).then_inc(emptied[b], 1)

        ve.wait_ge(x_in, 64)
        add_products()
        normalise(TILES, xres, 2)
        skip(N_CQ * 8)

        def cross_maxima(i):
            ve.wait_ge(cs_ready, i + 1)
            if i >= 2:
                ve.wait_ge(ce_ready, i - 1)
            rows, at = ROWS[i], 2 * (i % 2) * BANK
            ve.tensor_reduce(sm["nmax"][0:rows, 4 * (i % 2):4 * (i % 2) + 4],
                             ps[0:rows, at:at + 2 * BANK].rearrange("p (h n) -> p h n", h=CA_HEADS), AX, ALU.max,
                             negate=True).then_inc(cm_ready, 1)

        cross_maxima(0)
        for i in range(TILES):
            rows = ROWS[i]
            if i + 1 < TILES:
                cross_maxima(i + 1)
            ve.wait_ge(ce_ready, i + 1)
            if i >= 1:
                ve.wait_ge(cn_ready, i)
            rz = sm["pk"][0:rows, 0:4]
            step.done(ve.reciprocal(rz, sm["mz"][0:rows, 4 * (i % 2):4 * (i % 2) + 4]))
            heads = cp[0:rows, i % 2, :].rearrange("p (h n) -> p h n", h=CA_HEADS)
            ve.tensor_tensor(heads, heads, rz.unsqueeze(2).broadcast_to([rows, CA_HEADS, MEM]), ALU.mult)\
              .then_inc(cn_ready, 1)
            for m in range(2):
                ve.wait_ge(ch_done, 2 * i + m + 1)
                cut = (slice(None), slice(4 * m, 4 * m + 4), slice(T0[i], T0[i] + rows))
                ve.tensor_tensor(actL[cut], bank(6 + m, 4 * rows).rearrange("p (k t) -> p k t", k=4),
                                 actH[cut].bitcast(F32), ALU.subtract).then_inc(cl_done, 1)
        add_products()
        normalise(TILES, xres, 3)
        skip(N_PQ * 8)

        S2 = 2 * PK_HEADS
        halves_of = work[:, :].rearrange("p (s n) -> p s n", s=S2)
        sums_of = cand[:, :].rearrange("p (h n) -> p h n", h=PK_HEADS)
        rest_of = work[:, :].rearrange("p (h n) -> p h n", h=PK_HEADS)

        def best_of(n, values, rest, best_values, best_places, rows, used=None):
            for s in range(n):
                ins = ve.max(best_values[0:rows, s, 0:8], values[0:rows, s, :])
            step.done(ins)
            for s in range(n):
                ve.match_replace(rest[0:rows, s, :], best_values[0:rows, s, 0:8], values[0:rows, s, :], NEG)
                ins = ve.max_index(best_places[0:rows, s, 0:8], best_values[0:rows, s, 0:8], values[0:rows, s, :])
            step.done(ins)
            for s in range(n):
                ins = ve.max(best_values[0:rows, s, 8:16], rest[0:rows, s, :])
            step.done(ins)
            for s in range(n):
                ins = ve.max_index(best_places[0:rows, s, 8:16], best_values[0:rows, s, 8:16], rest[0:rows, s, :])
            step.done(ins)

        ve.wait_ge(iota16_in, 16)
        ve.wait_ge(ssb_ready, TILES)
        for i in range(TILES):
            rows = ROWS[i]
            best_of(S2, ssb[:, i], halves_of, top, topi, rows)
            step.done(ve.tensor_copy(topf[0:rows, :, :], topi[0:rows, :, :]))
            square = [rows, TOPK, TOPK]
            for h in range(PK_HEADS):
                ins = ve.tensor_tensor(sums_of[0:rows, h, :].rearrange("p (x y) -> p x y", y=TOPK),
                                       top[0:rows, 2 * h, :].unsqueeze(2).broadcast_to(square),
                                       top[0:rows, 2 * h + 1, :].unsqueeze(1).broadcast_to(square), ALU.add)
            step.done(ins)
            best_of(PK_HEADS, sums_of, rest_of, best, besti, rows)
            step.done(ve.tensor_scalar(bestr[0:rows, 0], besti[0:rows], 4, None, ALU.logical_shift_right))
            step.done(ve.tensor_scalar(bestr[0:rows, 1], besti[0:rows], TOPK - 1, None, ALU.bitwise_and))
            step.done(ve.tensor_copy(bestf[0:rows].rearrange("p r h t -> p (r h t)"),
                                     bestr[0:rows].rearrange("p r h t -> p (r h t)")))
            g = chosen[0:rows, i, 2, :].rearrange("p (h t) -> p h t", t=TOPK)
            ve.tensor_tensor(g, best[0:rows], best[0:rows, :, 0:1].broadcast_to([rows, PK_HEADS, TOPK]), ALU.subtract)\
              .then_inc(gexp_in, 1)
            for half in range(2):
                for h in range(PK_HEADS):
                    k = h % 4
                    hit = pick[0:rows, k * TOPK * TOPK:(k + 1) * TOPK * TOPK].rearrange("p (t j) -> p t j", j=TOPK)
                    step.done(ve.tensor_tensor(hit, bestf[0:rows, half, h, :].unsqueeze(2).broadcast_to(square),
                                               iota16[0:rows, :].unsqueeze(1).broadcast_to(square), ALU.is_equal))
                    step.done(ve.tensor_tensor(hit, hit, topf[0:rows, 2 * h + half, :].unsqueeze(1)
                                               .broadcast_to(square), ALU.mult))
                    step.done(ve.tensor_reduce(chosen[0:rows, i, half, h * TOPK:(h + 1) * TOPK], hit, AX, ALU.add))
        for i in range(TILES):
            rows = ROWS[i]
            ve.wait_ge(gexp_out, 1 + i // (TILES - 1))
            g = chosen[0:rows, i, 2, :].rearrange("p (h t) -> p h t", t=TOPK)
            total = sm["pk"][0:rows, 8:16]
            step.done(ve.tensor_reduce(total, g, AX, ALU.add))
            step.done(ve.reciprocal(total, total))
            step.done(ve.tensor_tensor(g, g, total.unsqueeze(2).broadcast_to([rows, PK_HEADS, TOPK]), ALU.mult))
        ve.sem_inc(chosen_ready, 1)

        ve.wait_ge(chT_copied, TILES)
        step.done(ve.tensor_copy(iota[:, 0:TOPK], iota16[:, :]))
        for k in range(1, NKEYS // TOPK):
            ins = ve.tensor_scalar(iota[:, k * TOPK:(k + 1) * TOPK], iota16[:, :], float(k * TOPK), None, ALU.add)
        step.done(ins)
        with ve.Fori(0, NT // 16) as i:
            for s in range(2):
                ve.wait_ge(c_filled, i * 4 + (2 * s + 2))
                shape = [P, 8, NKEYS]
                ve.tensor_tensor(hot1[:, s], iota[:, :].unsqueeze(1).broadcast_to(shape),
                                 chosenT[:, 0, bass.ds(i * 16 + 8 * s, 8)].unsqueeze(2).broadcast_to(shape), ALU.is_equal)
                for t in range(8):
                    tok = bass.ds(i * 16 + (8 * s + t), 1)
                    ins = ve.tensor_scalar(hot2[:, s, t, :], iota[:, :], chosenT[:, 1, tok], chosenT[:, 2, tok],
                                           ALU.is_equal, ALU.mult)
                ins.then_inc(hot_ready, 1)

        for s in range(2):
            ve.wait_ge(c_store[s], 16 * TBN // 2)
        step.done(ve.memset(acc[:, :, :], 0.0))
        ve.sem_inc(gf_ready, 2)
        ve.sem_inc(acc_added, 2)

        def weigh(e, s, n, c_arrived, ge_arrived=None):
            if ge_arrived is not None:
                ve.wait_ge(ge_in[e], ge_arrived)
            else:
                ve.wait_ge(ge_ready, n + 3)
            ve.wait_ge(gh_done, n + 1)
            if e == 0:
                ve.wait_ge(c_in[s], c_arrived)
            ve.tensor_tensor(gf[:, e % 2, :].rearrange("p (b t) -> p b t", t=TB),
                             ge[:, e, :].rearrange("p (b t) -> p b t", t=TB), cg[:, s, :, e, :], ALU.mult)\
              .then_inc(gf_ready, 1)
            ve.wait_ge(gh_done, n + 3)
            ve.tensor_tensor(gL[:, s, e, :], gf[:, e % 2, :], gH[:, s, e, :].bitcast(F32), ALU.subtract)\
              .then_inc(gl_done, 1)
            ve.wait_ge(gl_done, n + 1)

        def add_down(d, m):
            ve.wait_ge(v_done, m + 1)
            part = acc[:, d, :].rearrange("p (c n) -> p c n", c=2)
            ve.tensor_tensor(part, part, halves(4 + 2 * (d % 2)), ALU.add).then_inc(acc_added, 1)

        for e in range(EG):
            weigh(e, 0, e, 16, 16)
        for e in range(EG):
            weigh(e, 1, EG + e, 16, 32)
            for d in (2 * e, 2 * e + 1):
                add_down(d, d)
        with ve.Fori(0, EARLY // 2 - 1) as i:
            for s in range(2):
                for e in range(EG):
                    weigh(e, s, i * (2 * EG) + (EG * (s + 2) + e), i * 16 + 32, i * 32 + 16 * (s + 3))
                    for d in (2 * e, 2 * e + 1):
                        add_down(d, i * (2 * KT) + (KT * (s + 1) + d))
        for d in range(KT):
            add_down(d, KT * (EARLY - 1) + d)
        for e in range(EG):
            weigh(e, 0, EG * EARLY + e, 16 * (EARLY // 2 + 1))
        with ve.Fori(0, LATE_PAIRS) as i:
            for s in range(2):
                for e in range(EG):
                    weigh(e, 1 - s, i * (2 * EG) + (EG * (EARLY + s + 1) + e), i * 16 + 16 * (EARLY // 2 + 1 + s))
                for d in range(KT):
                    add_down(d, i * (2 * KT) + (KT * (EARLY + s) + d))
        for e in range(EG):
            weigh(e, 1, EG * (GROUPS - 1) + e, 16 * (GROUPS // 2))
        for m in range(KT * (GROUPS - 2), KT * GROUPS):
            add_down(m % KT, m)

        ve.wait_ge(gain_in, 16 * 5)
        ve.wait_ge(x2_in, 32)
        for i in range(TILES):
            rows = ROWS[i]
            at = 2 * (i % 2) * BANK
            ve.wait_ge(yt2_ready, i + 1)
            ve.tensor_tensor(x2b[0:rows, i, :], x2b[0:rows, i, :], ps[0:rows, at:at + 2 * BANK], ALU.add)\
              .then_inc(res_ready, 1)
            ve.wait_ge(ssq_ready, sums[0] + i + 1)
            rstd = sm["rstd"][0:rows, i:i + 1]
            ve.tensor_scalar(rstd, sm["ssq"][0:rows, i:i + 1], 1.0 / D, RMS_EPS, ALU.mult, ALU.add)\
              .then_inc(var_ready, 1)
            ve.wait_ge(std_ready, 4 + i + 1)
            step.done(ve.reciprocal(rstd, rstd))
            ve.scalar_tensor_tensor(yout[0:rows, i % 2, :], x2b[0:rows, i, :], rstd, gain[0:rows, :],
                                    ALU.mult, ALU.mult).then_inc(y_ready, 1)


INPUTS = ["wts", "ident", "x", "mem", "gains", "par", "lamp", "gsub", "ropec", "ropes", "ropen", "mask", "ckT", "cv",
          "cmkT", "cmv", "keysT", "iota"]
OUTPUTS = {"y": (NT, D), "k": (NT, D), "v": (NT, D), "mkT": (D, MEM), "mv": (MEM, D), "cstate": (P, KT, 6),
           "hstate": (P, KT, 2)}


def layout(p):
    p = {name: np.asarray(value) for name, value in p.items()}
    f32 = np.float32

    def pieces(w):
        n = w.shape[1] // CHUNK
        return w.reshape(2, 4, P, n, CHUNK).transpose(3, 0, 2, 1, 4).reshape(2 * n, P, PIECE)

    w_in = p["w_in"][0]
    q, k, v, rx, rg, ga, gr = (w_in[:, c * D:(c + 1) * D] for c in range(7))
    recurrent = np.concatenate([w[:, j * P:(j + 1) * P] for j in range(N_RG) for w in (rx, rg, gr, ga)], axis=1)
    u = p["peer_u"][0].reshape(NKEYS, NKEYS, D)
    u = u.reshape(NKEYS, GROUPS, EG, 2, 4, P).transpose(1, 3, 5, 4, 2, 0).reshape(GROUPS, 2, P, PIECE)
    vt = p["peer_v"][0].reshape(NKEYS, GROUPS, 2, 2, D).transpose(1, 2, 0, 3, 4).reshape(GROUPS, 2, P, PIECE)
    experts = [*u[:EARLY], *vt[:EARLY], u[EARLY]]
    for g in range(EARLY + 1, GROUPS):
        experts += [u[g], vt[g - 1]]
    experts.append(vt[GROUPS - 1])
    wts = np.concatenate([pieces(p["w_ck"][0]), pieces(p["w_cv"][0]), pieces(recurrent), pieces(k), pieces(v),
                          pieces(q), pieces(p["w_out"][0]), pieces(p["w_cq"][0]), pieces(p["w_co"][0]),
                          pieces(p["w_pq"][0])] + experts)

    def columns(x):
        return np.moveaxis(x.reshape(x.shape[:-1] + (KT, P)), (-2, -1), (0, 1))

    par = np.zeros((KT, P, PAR_N), f32)
    for at, w in ((0, p["rg_wa"][0]), (P, p["rg_wx"][0])):
        for b in range(2):
            par[:, b * 64:b * 64 + 64, at + b * 64:at + b * 64 + 64] = w[b::2]
    par[:, :, PAR_CW:PAR_CW + CONVW] = columns(p["conv_w"][0])
    for at, name in ((PAR_CB, "conv_b"), (PAR_BA, "rg_ba"), (PAR_BX, "rg_bx")):
        par[:, :, at] = columns(p[name][0])
    par[:, :, PAR_SC:PAR_SC + 3] = columns(p["state_conv"][0, 0])
    par[:, :, PAR_H0] = columns(p["state_rglru"][0, 0])

    lams = np.concatenate([p[n][0] for n in ("lam_q1", "lam_k1", "lam_q2", "lam_k2")])
    lamp = np.concatenate([np.broadcast_to(lams, (P, 4 * DK)), p["rg_lambda"][0].reshape(KT, P).T], axis=1)
    gains = np.stack([p["g_mem"][0], p["g_mix"][0], p["g_cross"][0], p["g_ffn"][0], p["g_final"]])

    inv = np.exp(f32(-math.log(10000.0)) * np.arange(32, dtype=f32) * f32(2.0 / DK)).astype(f32)
    pos = np.arange(TILES * P, dtype=f32)
    ang = (pos[:, None] * inv[None, :]).astype(f32).astype(np.float64)
    rope = {n: np.ascontiguousarray(t.astype(f32).reshape(TILES, P, 32).transpose(1, 0, 2))
            for n, t in (("ropec", np.cos(ang)), ("ropes", np.sin(ang)), ("ropen", -np.sin(ang)))}
    mask = np.zeros((1, P + DK), f32)
    mask[0, 0:DK] = 1.0
    mask[0, P:] = -1e30
    keys = np.stack([p["pk_keys1"][0], p["pk_keys2"][0]], axis=1).reshape(2 * PK_HEADS, NKEYS, P)
    arrays = {
        "wts": wts, "ident": np.eye(P, dtype=f32),
        "x": np.concatenate([p["x_prompt"][0], p["x_sample"][0]]), "mem": p["mem_prompt"][0],
        "gains": np.broadcast_to(gains[:, None, :], (5, P, D)), "par": par, "lamp": lamp,
        "gsub": p["g_subln"][0][:, None], **rope, "mask": mask,
        "ckT": p["cache_attn_k"][0, 0].reshape(PAST, HEADS, P).transpose(1, 2, 0),
        "cv": p["cache_attn_v"][0, 0].reshape(PAST // P, P, D).transpose(1, 0, 2),
        "cmkT": p["cache_mem_k"][0, 0].reshape(MEM, D).T, "cmv": p["cache_mem_v"][0, 0].reshape(MEM, D),
        "keysT": keys.transpose(2, 0, 1), "iota": np.broadcast_to(np.arange(P, dtype=f32), (P, P)),
    }
    return {name: np.ascontiguousarray(arrays[name]) for name in INPUTS}


def kernel(**inputs):
    import concourse.bacc as _bacc
    from concourse.bass_utils import run_bass_kernel_spmd as _run

    arrays = layout(inputs)
    nc = _bacc.Bacc("TRN2", target_bir_lowering=False, num_devices=1)
    a = {name: nc.dram_tensor(name, x.shape, F32, kind="ExternalInput").ap() for name, x in arrays.items()}
    o = {name: nc.dram_tensor(f"out_{name}", shape, F32, kind="ExternalOutput").ap() for name, shape in OUTPUTS.items()}
    with nc.Block() as block:
        encoder_layer(nc, block, a, o)
    r = _run(nc, [arrays], core_ids=[0]).results[0]
    y, k, v, mkT, mv, cs, hs = (np.asarray(r[f"out_{name}"]) for name in OUTPUTS)
    cs = cs.transpose(2, 1, 0).reshape(6, D)
    hs = hs.transpose(2, 1, 0).reshape(2, D)
    n = NP_TOK
    return (y[None, :n], y[None, n:],
            k[:n].reshape(1, 1, n, 2 * HEADS, DK), v[:n].reshape(1, 1, n, HEADS, DV),
            mkT.T.reshape(1, 1, MEM, CA_HEADS, CA_DH), mv.reshape(1, 1, MEM, CA_HEADS, CA_DH),
            cs[None, None, 0:3], hs[None, 0:1],
            k[n:].reshape(1, 1, NS_TOK, 2 * HEADS, DK), v[n:].reshape(1, 1, NS_TOK, HEADS, DV),
            cs[None, None, 3:6], hs[None, 1:2])
```

```python
import math

import concourse.bass as bass
import numpy as np
from concourse import mybir

F32 = mybir.dt.float32
F32R = mybir.dt.float32r
U32 = mybir.dt.uint32
ALU = mybir.AluOpType
ACT = mybir.ActivationFunctionType
AX = mybir.AxisListType.X

P = 128
D = 1024
KT = D // P
NP_TOK, NS_TOK = 512, 64
NT = NP_TOK + NS_TOK
HALF = NT // 2
ROWS = [128, 128, 128, 128, 64]
T0 = [0, 128, 256, 384, 512]
TILES = len(ROWS)
HEADS, DK, DV = 8, 64, 128
LAM_INIT = 0.8 - 0.6 * math.exp(-0.3 * 0)
PAST = 512
MEM = 256
MT = MEM // P
CA_HEADS, CA_DH = 4, 256
PK_HEADS, NKEYS, TOPK = 8, 128, 16
RG_C = 8.0
CONVW = 4
RMS_EPS, SUBLN_EPS = 1e-6, 1e-5
BANK = 512
BANKS = 8
CHUNK = 512
PIECE = 4 * CHUNK
SEG = NP_TOK + CONVW - 1
XPW = SEG + CONVW - 1 + NS_TOK
CW = XPW - (CONVW - 1)
CA_ = 290
PAR_CW, PAR_CB, PAR_BA, PAR_BX, PAR_SC, PAR_H0, PAR_N = 256, 260, 261, 262, 264, 267, 272
N_CK, N_CV, N_RG, N_K, N_V, N_Q, N_OUT, N_CQ, N_CO, N_PQ = 2, 2, 8, 2, 2, 2, 2, 2, 2, 4
PRE_CHUNKS = N_CK + N_CV + N_RG + N_K + N_V + N_Q + N_OUT + N_CQ + N_CO + N_PQ
EG = 4
GROUPS = NKEYS // EG
CHUNKS = PRE_CHUNKS + 2 * GROUPS
TB = 32
TBN = NT // TB
RANK_GROUPS = 12
C_GROUPS = TBN // 2
EARLY = RANK_GROUPS + C_GROUPS + 1
LATE_PAIRS = (GROUPS - EARLY) // 2 - 1
assert EARLY % 2 == 0 and RANK_GROUPS % 2 == 0 and C_GROUPS % 2 == 1
NEG = -3.0e38
ROUND = 1.5 * 2.0 ** 23


class Steps:

    def __init__(self, eng, sem):
        self.eng, self.sem, self.n, self.i, self.per = eng, sem, 0, None, 0

    def done(self, ins):
        self.n += 1
        ins.then_inc(self.sem, 1)
        self.eng.wait_ge(self.sem, self.n if self.i is None else self.i * self.per + self.n)

    def enter(self, i, per):
        self.i, self.per, self.start = i, per, self.n

    def leave(self, times):
        assert self.n - self.start == self.per, (self.n - self.start, self.per)
        self.n, self.i = self.start + times * self.per, None


class Turns:

    def __init__(self):
        self.n, self.i, self.per = 0, None, 0

    def take(self):
        bank, value = self.n % BANKS, self.n // BANKS + 1
        self.n += 1
        return bank, value if self.i is None else self.i * (self.per // BANKS) + value

    def enter(self, i, per):
        self.i, self.per, self.start = i, per, self.n

    def leave(self, times):
        assert self.n - self.start == self.per and self.per % BANKS == 0
        self.n, self.i = self.start + times * self.per, None


def projection_turns(turns):
    first = [turns.take() for _ in range(TILES)]
    second, turning = [], []
    for i in range(TILES):
        second.append(turns.take())
        if i >= 2:
            turning.append([turns.take(), turns.take()])
    while len(turning) < TILES:
        turning.append([turns.take(), turns.take()])
    return first, second, turning


class Count:

    def __init__(self, n=0):
        self.n, self.i, self.per = n, None, 0

    def up(self, k=1):
        self.n += k
        return self.value()

    def value(self, more=0):
        v = self.n + more
        return v if self.i is None else self.i * self.per + v

    def enter(self, i, per):
        self.i, self.per, self.start = i, per, self.n

    def leave(self, times):
        assert self.n - self.start == self.per, (self.n - self.start, self.per)
        self.n, self.i = self.start + times * self.per, None


def encoder_layer(nc: bass.Bass, block, a: dict, o: dict):
    base = (nc.sbuf_base + 31) // 32 * 32
    cursor = [base]

    def put(name, shape, dt=F32, at=None):
        size = int(np.prod(shape[1:])) * 4
        where = cursor[0] if at is None else at
        t = nc.alloc_sbuf_tensor_at(name, shape, dt, offset=where)
        if at is None:
            cursor[0] += (size + 31) // 32 * 32
        return t

    actH = put("actH", [P, KT, NT], F32R)
    actL = put("actL", [P, KT, NT], F32R)
    wH = put("wH", [P, 4, 4, CHUNK], F32R)
    wL = put("wL", [P, 4, 4, CHUNK], F32R)
    raw = put("raw", [P, 2, PIECE])
    ident = put("ident", [P, P])
    gain = put("gain", [P, D])
    small = put("small", [P, 256])
    mask = put("mask", [1, P + DK])
    arena = cursor[0]

    class Region:
        def __init__(self, start=arena):
            self.at = start

        def put(self, name, shape, dt=F32):
            size = (int(np.prod(shape[1:])) * 4 + 31) // 32 * 32
            t = nc.alloc_sbuf_tensor_at(name, shape, dt, offset=self.at)
            self.at += size
            return t

    sm = {}
    at = 0
    for name, n in (("ssq", 8), ("rstd", 8), ("nmax", 8), ("z", 8), ("lamv", 2), ("lamt", 8), ("gsub", 1),
                    ("ncall", 8), ("pcall", 8), ("sp", 40), ("oss", 8), ("orstd", 8), ("mz", 8), ("pk", 24)):
        sm[name] = small[:, at:at + n]
        at += n
    assert at <= 256

    r = Region()
    xres = r.put("xres", [P, TILES, D])
    after_xres = r.at
    xn = r.put("xn", [P, 2, D])
    sq = r.put("sq", [P, D])
    memx = r.put("memx", [P, MT, D])
    mk_sb = r.put("mk_sb", [P, KT, MEM])
    mv_sb = r.put("mv_sb", [P, MT, D])
    r = Region()
    rxp = r.put("rxp", [P, 2, XPW + 2])
    par = r.put("par", [P, 2, PAR_N])
    conv = r.put("conv", [P, 2, CW + 1])
    gel = r.put("gel", [P, 2, NT])
    sgr = r.put("sgr", [P, 2, NT])
    sga = r.put("sga", [P, 2, NT])
    gate_r = r.put("gate_r", [P, CW + 1])
    gate_i = r.put("gate_i", [P, CW + 1])
    lru_a = r.put("lru_a", [P, CW + 1])
    lru_t = r.put("lru_t", [P, CW + 1])
    assert r.at <= arena + 2 * HEADS * NT * 4
    r = Region()
    kT = r.put("kT", [P, HEADS, NT])
    qT = r.put("qT", [P, HEADS, NT])
    vtok_at = r.at
    vtok = r.put("vtok", [P, TILES, D])
    att = r.at
    ropec = r.put("ropec", [P, TILES, 32])
    ropes = r.put("ropes", [P, TILES, 32])
    ropen = r.put("ropen", [P, TILES, 32])
    rot1 = r.put("rot1", [P, CHUNK])
    rot2 = r.put("rot2", [P, CHUNK])
    rot = r.put("rot", [P, 2, CHUNK])
    lru_m = r.put("lru_m", [P, CW + 1])
    lru_h = r.put("lru_h", [P, NT])
    yrec = r.put("yrec", [P, 2, NT])
    cstate = r.put("cstate", [P, KT, 6])
    hstate = r.put("hstate", [P, KT, 2])
    lamp = r.put("lamp", [P, 4 * DK + KT])
    r = Region(att)
    sat = r.put("sat", [P, KT, P])
    rt = r.put("rt", [P, KT, P])
    osb = r.put("osb", [P, D])
    prob_at = r.at
    prob = r.put("prob", [P, 2, 2, NP_TOK])
    aT = r.put("aT", [P, 2, CHUNK])
    ckv = r.put("ckv", [P, 2, PAST])
    r = Region(vtok_at)
    cvv = r.put("cvv", [P, 2, PAST])
    probs = [nc.alloc_sbuf_tensor_at("probs0", [P, 2, NT], F32, offset=prob_at), r.put("probs1", [P, 2, NT])]
    assert r.at <= vtok_at + (TILES - 1) * D * 4
    r = Region(after_xres)
    qcT = r.put("qcT", [P, KT, NT])
    mkT = r.put("mkT", [P, 2, KT, MEM])
    mvt = r.put("mvt", [P, 2, MT, D])
    cp = r.put("cp", [P, 2, D])
    cpT = r.put("cpT", [P, D])
    r = Region()
    pqT = r.put("pqT", [P, 2 * PK_HEADS, NT])
    keys = r.put("keys", [P, 2 * PK_HEADS, NKEYS])
    after_keys = r.at
    ssb = r.put("ssb", [P, TILES, 2 * PK_HEADS, NKEYS])
    iota16 = r.put("iota16", [P, TOPK])
    assert r.at <= nc.sbuf_usable_end, r.at
    r = Region()
    ge = r.put("ge", [P, EG, NT])
    after_ge = r.at
    work = r.put("work", [P, 2048])
    after_work = r.at
    cand = r.put("cand", [P, 2048])
    pick = cand
    top = r.put("top", [P, 2 * PK_HEADS, TOPK])
    topi = r.put("topi", [P, 2 * PK_HEADS, TOPK], U32)
    topf = r.put("topf", [P, 2 * PK_HEADS, TOPK])
    best = r.put("best", [P, PK_HEADS, TOPK])
    besti = r.put("besti", [P, PK_HEADS, TOPK], U32)
    bestf = r.put("bestf", [P, 2, PK_HEADS, TOPK])
    chosen = r.put("chosen", [P, TILES, 3, PK_HEADS * TOPK])
    assert r.at <= after_keys
    chosenT = nc.alloc_sbuf_tensor_at("chosenT", [P, 3, NT], F32, offset=after_ge)
    assert after_ge + 3 * NT * 4 <= after_work
    r = Region(after_work)
    iota = r.put("iota", [P, NKEYS])
    hot1 = r.put("hot1", [P, 2, 8, NKEYS])
    hot2 = r.put("hot2", [P, 2, 8, NKEYS])
    cst = r.put("cst", [P, 2, NKEYS, TB])
    assert r.at <= nc.sbuf_usable_end, r.at
    r = Region(after_ge)
    acc = r.put("acc", [P, KT, NT])
    cg = r.put("cg", [P, 2, TBN, EG, TB])
    gf = r.put("gf", [P, 2, NT])
    after_gf = r.at
    gH = r.put("gH", [P, 2, EG, NT], F32R)
    gL = r.put("gL", [P, 2, EG, NT], F32R)
    assert r.at <= nc.sbuf_usable_end, r.at
    r = Region(after_ge + KT * NT * 4)
    x2b = r.put("x2b", [P, TILES, D])
    assert r.at <= after_gf
    yout = nc.alloc_sbuf_tensor_at("yout", [P, 2, D], F32, offset=arena)

    ps = nc.alloc_psum_tensor("ps", [P, BANKS * BANK], F32)

    def bank(b, n=BANK, rows=P):
        return ps[0:rows, b * BANK:b * BANK + n]

    sa_d = nc.dram_tensor("sa_scratch", (KT, P, NT), F32).ap()
    r_d = nc.dram_tensor("r_scratch", (KT, P, NT), F32).ap()
    x2_d = nc.dram_tensor("x2_scratch", (NT, D), F32).ap()
    ge_d = nc.dram_tensor("ge_scratch", ((EARLY - 1) * EG, P, NT), F32).ap()
    c_d = nc.dram_tensor("c_scratch", (TBN, P, NKEYS, TB), F32).ap()

    S = nc.alloc_semaphore
    raw_in = [S(f"raw_in{j}") for j in range(2)]
    high_done = S("high_done")
    w_ready = S("w_ready")
    w_free = S("w_free")
    filled = [S(f"filled{b}") for b in range(BANKS)]
    emptied = [S(f"emptied{b}") for b in range(BANKS)]
    ve_step = S("ve_step")
    names = """const_in gain_in gain_used memx_in x_in ssq_clear ssq_ready var_ready std_ready xn_ready acth_done
        out_done lamp_in sp_neg sp_exp sp_one sp_ln lam_sums lam_exp lam_ready conv_done gate_ready m_ready
        root_ready yrec_ready rot_ready rope_in sc_ready nm_ready p_ready a_ready t_ready aT_ready pv_done
        osb_ready ovar_ready ostd_ready on_ready yt_ready merged mh_done ml_done sat_in turned_used mask_in mem_in
        cs_ready cm_ready ce_ready cn_ready ct_ready cpT_ready co_ready ch_done cl_done res_ready x2_store
        keys_in iota16_in score_ready ssb_ready  gexp_in gexp_out chosen_ready chT_ready chT_copied
        hot_ready c_filled c_copied u_done ge_ready gf_ready gh_done gl_done v_done acc_added
        x2_in yt2_ready y_ready taken_up""".split()
    (const_in, gain_in, gain_used, memx_in, x_in, ssq_clear, ssq_ready, var_ready, std_ready, xn_ready, acth_done,
     out_done, lamp_in, sp_neg, sp_exp, sp_one, sp_ln, lam_sums, lam_exp, lam_ready, conv_done, gate_ready, m_ready,
     root_ready, yrec_ready, rot_ready, rope_in, sc_ready, nm_ready, p_ready, a_ready, t_ready, aT_ready, pv_done,
     osb_ready, ovar_ready, ostd_ready, on_ready, yt_ready, merged, mh_done, ml_done, sat_in, turned_used, mask_in, mem_in,
     cs_ready, cm_ready, ce_ready, cn_ready, ct_ready, cpT_ready, co_ready, ch_done, cl_done, res_ready, x2_store,
     keys_in, iota16_in, score_ready, ssb_ready, gexp_in, gexp_out, chosen_ready, chT_ready, chT_copied,
     hot_ready, c_filled, c_copied, u_done, ge_ready, gf_ready, gh_done, gl_done, v_done, acc_added,
     x2_in, yt2_ready, y_ready, taken_up) = [S(name) for name in names]
    ck_in = [S(f"ck_in{j}") for j in range(2)]
    cv_in = [S(f"cv_in{j}") for j in range(2)]
    par_in = [S(f"par_in{j}") for j in range(2)]
    sa_store = [S(f"sa_store{j}") for j in range(2)]
    r_store = [S(f"r_store{j}") for j in range(2)]
    k_store = [S(f"k_store{j}") for j in range(2)]
    c_store = [S(f"c_store{j}") for j in range(2)]
    c_in = [S(f"c_in{j}") for j in range(2)]
    ge_store = [S(f"ge_store{j}") for j in range(EG)]
    ge_in = [S(f"ge_in{j}") for j in range(EG)]
    y_store = [S(f"y_store{j}") for j in range(2)]

    UNITS = [(i, h) for i in range(TILES) for h in range(HEADS)]
    VKQ = [("v", 0), ("v", 1), ("k", 0), ("k", 1), ("q", 0), ("q", 1)]
    TUNITS = [(kind, c, i) for kind, c in VKQ for i in range(TILES)]

    def halves(b):
        return ps[:, b * BANK:(b + 2) * BANK].rearrange("p (c n) -> p c n", n=BANK)[:, :, 0:HALF]

    @block.sync
    def _(sp):
        for j in range(2):
            sp.dma_start(raw[:, j, :], a["wts"][j]).then_inc(raw_in[j], 16)
        with sp.Fori(0, CHUNKS - 1) as i:
            for j in range(2):
                sp.wait_ge(w_ready, i * 4 + (2 * j + 2))
                sp.dma_start(raw[:, j, :], a["wts"][i * 2 + (2 + j)]).then_inc(raw_in[j], 16)

    @block.gpsimd
    def _(pool):
        with pool.Fori(0, CHUNKS // 2) as i:
            for s in range(4):
                w = raw[:, s % 2, :]
                hi = wH[:, s].rearrange("p k n -> p (k n)")
                lo = wL[:, s].rearrange("p k n -> p (k n)")
                pool.wait_ge(raw_in[s % 2], i * 32 + 16 * (s // 2 + 1))
                pool.wait_ge(w_free, i * 4 + (s // 2 * 2 + 2))
                pool.sem_inc(taken_up, 1)
                cuts = (slice(0, PIECE // 2), slice(PIECE // 2, PIECE))
                for cut in cuts:
                    pool.tensor_scalar(hi[:, cut], w[:, cut], 1.0, 1.0, ALU.mult, ALU.mult).then_inc(high_done, 1)
                for c, cut in enumerate(cuts):
                    pool.wait_ge(high_done, i * 8 + (2 * s + c + 1))
                    pool.tensor_tensor(lo[:, cut], w[:, cut], hi[:, cut].bitcast(F32), ALU.subtract)\
                        .then_inc(w_ready, 1)

    @block.tensor
    def _(pe):
        turns = Turns()
        pieces = Count()
        release = [0]

        def begin(ins):
            if release[0]:
                ins.then_inc(w_free, 2)
                release[0] = 0

        pe.sem_inc(w_free, 4)
        for b in range(BANKS):
            pe.sem_inc(emptied[b], 1)
        pe.wait_ge(const_in, 16)

        def fill(out, terms, sem=None):
            for t, (lhs, rhs) in enumerate(terms):
                mm = pe.matmul(out, lhs, rhs, start=t == 0, stop=t == len(terms) - 1)
                if t == 0 and len(terms) > 1:
                    begin(mm)
            if sem is not None:
                mm.then_inc(sem, 1)
            return mm

        def weight(slot, k, cut):
            return wH[:, slot + k // 4, k % 4, cut], wL[:, slot + k // 4, k % 4, cut]

        def chunk(slot, groups, after=None):
            for g, (cols, terms) in enumerate(groups):
                b, value = turns.take()
                pe.wait_ge(emptied[b], value)
                for k in range(KT):
                    if g == 0 and k % 4 == 0:
                        pieces.up(2)
                        pe.wait_ge(w_ready, pieces.value())
                    for t, (lhs, rhs) in enumerate(terms(k)):
                        mm = pe.matmul(cols(b), lhs, rhs, start=k == 0 and t == 0, stop=k == KT - 1 and t == 2)
                        if k == 0 and t == 0:
                            begin(mm)
                mm.then_inc(filled[b], 1)
                if after is not None:
                    after(g)
            release[0] = 1

        def feature_chunk(slot, n_tok, n_parts):
            def make(blk, part):
                w = slice(blk * P, blk * P + P)
                t = slice(part * n_tok, (part + 1) * n_tok)

                def terms(k):
                    h, l = weight(slot, k, w)
                    return (h, actH[:, k, t]), (h, actL[:, k, t]), (l, actH[:, k, t])
                return (lambda b: bank(b, n_tok)), terms
            chunk(slot, [make(blk, part) for blk in range(4) for part in range(n_parts)])

        def token_group(slot, i, rows, t0):
            t = slice(t0, t0 + rows)

            def terms(k):
                h, l = weight(slot, k, slice(0, CHUNK))
                return (actH[:, k, t], h), (actH[:, k, t], l), (actL[:, k, t], h)
            return (lambda b: bank(b, CHUNK, rows)), terms

        def norm(n_tiles, first, rows):
            for i in range(n_tiles):
                turn_tile(i, first, rows)

        def turn_tile(i, first, rows):
            pe.wait_ge(xn_ready, first + i + 1)
            for half in range(2):
                b, value = turns.take()
                pe.wait_ge(emptied[b], value)
                for k in range(4):
                    src = xn[0:rows[i], (first + i) % 2, (half * 4 + k) * P:(half * 4 + k + 1) * P]
                    mm = pe.transpose(ps[:, b * BANK + k * rows[i]:b * BANK + (k + 1) * rows[i]], src,
                                      ident[0:rows[i], 0:rows[i]])
                    if half == 0 and k == 0:
                        begin(mm)
                mm.then_inc(filled[b], 1)
            last[0] = (b, value)

        last = [None]

        def evacuated():
            b, value = last[0]
            pe.wait_ge(emptied[b], value + 1)

        norm(MT, 0, ROWS)
        evacuated()
        for c in range(N_CK):
            feature_chunk(2 * c, MEM, 1)
        for c in range(N_CV):
            chunk(2 * c, [token_group(2 * c, i, P, i * P) for i in range(MT)])
        norm(TILES, MT, ROWS)
        evacuated()

        def gates(s, value):
            pe.wait_ge(conv_done, value)
            for w in range(2):
                for cut in (slice(0, CA_), slice(CA_, CW)):
                    b, turn = turns.take()
                    pe.wait_ge(emptied[b], turn)
                    fill(ps[:, b * BANK:b * BANK + cut.stop - cut.start],
                         [(par[:, s, w * P:(w + 1) * P], conv[:, s, cut])], filled[b])

        feature_chunk(0, HALF, 2)
        feature_chunk(2, HALF, 2)
        gates(0, 1)
        with pe.Fori(0, N_RG // 2 - 1) as i:
            turns.enter(i, 24)
            pieces.enter(i, 8)
            feature_chunk(0, HALF, 2)
            gates(1, i * 2 + 2)
            feature_chunk(2, HALF, 2)
            gates(0, i * 2 + 3)
            turns.leave(N_RG // 2 - 1)
            pieces.leave(N_RG // 2 - 1)
        def turn_rotated(u):
            kind, c, i = TUNITS[u]
            if kind == "v":
                return
            n = sum(1 for k, _, _ in TUNITS[:u + 1] if k != "v")
            pe.wait_ge(rot_ready, n)
            b, value = turns.take()
            pe.wait_ge(emptied[b], value)
            for k in range(4):
                mm = pe.transpose(ps[:, b * BANK + k * ROWS[i]:b * BANK + (k + 1) * ROWS[i]],
                                  rot[0:ROWS[i], (n - 1) % 2, k * P:(k + 1) * P], ident[0:ROWS[i], 0:ROWS[i]])
                if k == 0:
                    begin(mm)
            mm.then_inc(filled[b], 1)

        u = 0
        for n, (kind, c) in enumerate(VKQ):
            slot = 2 * (n % 2)
            for i in range(TILES):
                cols, terms = token_group(slot, i, ROWS[i], T0[i])
                b, value = turns.take()
                pe.wait_ge(emptied[b], value)
                for k in range(KT):
                    if i == 0 and k % 4 == 0:
                        pieces.up(2)
                        pe.wait_ge(w_ready, pieces.value())
                    for t, (lhs, rhs) in enumerate(terms(k)):
                        mm = pe.matmul(cols(b), lhs, rhs, start=k == 0 and t == 0, stop=k == KT - 1 and t == 2)
                        if k == 0 and t == 0:
                            begin(mm)
                mm.then_inc(filled[b], 1)
                if i == TILES - 1:
                    release[0] = 1
                if n == 0 and i == 0:
                    gates(1, N_RG)
                if u >= 2:
                    turn_rotated(u - 2)
                u += 1
        turn_rotated(u - 2)
        turn_rotated(u - 1)
        for b in range(BANKS):
            pe.wait_ge(emptied[b], (turns.n - 1 - b) // BANKS + 2)

        pe.wait_ge(mask_in, 16)

        def scores(u):
            i, h = UNITS[u]
            rows = ROWS[i]
            t = slice(T0[i], T0[i] + rows)
            if u >= 1 and (i == TILES - 1 or u >= 2):
                pe.wait_ge(p_ready, u if i == TILES - 1 else u - 1)
            if i == TILES - 1:
                pe.wait_ge(ck_in[h % 2], 16 * (h // 2 + 1))
            for s in range(2):
                half = slice(s * DK, (s + 1) * DK)
                if i < TILES - 1:
                    b, n = 2 * (u % 2) + s, P * (i + 1)
                    mm = pe.matmul(bank(b, n), qT[half, h, t], kT[half, h, 0:n], start=True, stop=False)
                    if s == 0:
                        begin(mm)
                    mm = pe.matmul(ps[:, b * BANK + n - DK:b * BANK + n], mask[0:1, 0:P], mask[0:1, P:P + DK],
                                   start=False, stop=True)
                else:
                    b = 2 * s
                    pe.matmul(bank(b, PAST, rows), qT[half, h, t], ckv[half, h % 2, :], start=True, stop=True)
                    mm = pe.matmul(bank(b + 1, rows, rows), qT[half, h, t], kT[half, h, t], start=True, stop=True)
            mm.then_inc(sc_ready, 1)

        def turn_probs(u):
            i, h = UNITS[u]
            rows = ROWS[i]
            pe.wait_ge(a_ready, u + 1)
            if u >= 2:
                pe.wait_ge(aT_ready, u - 1)
            b = 4 + u % 2
            if i < TILES - 1:
                for k in range(i + 1):
                    mm = pe.transpose(ps[:, b * BANK + k * P:b * BANK + (k + 1) * P],
                                      prob[:, u % 2, 0, k * P:(k + 1) * P], ident[:, :])
            else:
                for k in range(PAST // P):
                    pe.transpose(ps[:, b * BANK + k * rows:b * BANK + (k + 1) * rows],
                                 probs[u % 2][0:rows, 0, k * P:(k + 1) * P], ident[0:rows, 0:rows])
                k = PAST // P
                mm = pe.transpose(ps[0:rows, b * BANK + k * rows:b * BANK + (k + 1) * rows],
                                  probs[u % 2][0:rows, 0, PAST:NT], ident[0:rows, 0:rows])
            mm.then_inc(t_ready, 1)

        def weighted(u):
            i, h = UNITS[u]
            rows = ROWS[i]
            pe.wait_ge(aT_ready, u + 1)
            if h == 0 and i > 0:
                pe.wait_ge(turned_used, i)
            if i == TILES - 1:
                pe.wait_ge(cv_in[h % 2], 16 * (h // 2 + 1))
            out = ps[0:rows, 6 * BANK + h * DV:6 * BANK + (h + 1) * DV]
            cols = slice(h * DV, (h + 1) * DV)
            if i < TILES - 1:
                terms = [(aT[:, u % 2, k * P:(k + 1) * P], vtok[:, k, cols]) for k in range(i + 1)]
            else:
                terms = [(aT[:, u % 2, k * rows:(k + 1) * rows], cvv[:, h % 2, k * P:(k + 1) * P]) for k in range(PAST // P)]
                k = PAST // P
                terms.append((aT[0:rows, u % 2, k * rows:(k + 1) * rows], vtok[0:rows, TILES - 1, cols]))
            for t, (lhs, rhs) in enumerate(terms):
                mm = pe.matmul(out, lhs, rhs, start=t == 0, stop=t == len(terms) - 1)
            mm.then_inc(pv_done, 1)

        def turn_outputs(i):
            rows = ROWS[i]
            pe.wait_ge(on_ready, i + 1)
            for h in range(HEADS):
                b = 6 + h // 4
                mm = pe.transpose(ps[:, b * BANK + (h % 4) * rows:b * BANK + (h % 4 + 1) * rows],
                                  osb[0:rows, h * DV:(h + 1) * DV], ident[0:rows, 0:rows])
            mm.then_inc(yt_ready, 1)

        scores(0)
        for u, (i, h) in enumerate(UNITS):
            if u + 1 < len(UNITS):
                scores(u + 1)
            turn_probs(u)
            if h == 1 and i > 0:
                turn_outputs(i - 1)
            if u > 0:
                weighted(u - 1)
        weighted(len(UNITS) - 1)

        def before_last_tile(g):
            if g == 1:
                turn_outputs(TILES - 1)
                pe.wait_ge(turned_used, TILES)
            if g == TILES - 2:
                pe.wait_ge(ml_done, TILES)

        def project_and_norm(first, between=None):
            chunk(0, [token_group(0, i, ROWS[i], T0[i]) for i in range(TILES)], between)
            chunk(2, [token_group(2, i, ROWS[i], T0[i]) for i in range(TILES)],
                  lambda g: turn_tile(g - 2, first, ROWS) if g >= 2 else None)
            for i in range(TILES - 2, TILES):
                turn_tile(i, first, ROWS)
            evacuated()

        assert turns.n % BANKS == 4
        pe.wait_ge(ml_done, TILES - 1)
        project_and_norm(MT + TILES, before_last_tile)
        for c in range(N_CQ):
            feature_chunk(2 * c, HALF, 2)
        for b in range(BANKS):
            pe.wait_ge(emptied[b], (turns.n - 1 - b) // BANKS + 2)
        pe.wait_ge(mem_in, 64)

        def cross_scores(i):
            rows, src = ROWS[i], i // (TILES - 1)
            if i >= 2:
                pe.wait_ge(ce_ready, i - 1)
            for h in range(CA_HEADS):
                out = ps[0:rows, 2 * (i % 2) * BANK + h * MEM:2 * (i % 2) * BANK + (h + 1) * MEM]
                mm = fill(out, [(qcT[:, 2 * h + k, T0[i]:T0[i] + rows], mkT[:, src, 2 * h + k, :]) for k in range(2)])
            mm.then_inc(cs_ready, 1)

        def cross_rest(i):
            rows, src = ROWS[i], i // (TILES - 1)
            pe.wait_ge(cn_ready, i + 1)
            if i >= 1:
                pe.wait_ge(cpT_ready, i)
            for m in range(2 * CA_HEADS):
                b = 4 + m // 4
                mm = pe.transpose(ps[:, b * BANK + (m % 4) * rows:b * BANK + (m % 4 + 1) * rows],
                                  cp[0:rows, i % 2, m * P:(m + 1) * P], ident[0:rows, 0:rows])
            mm.then_inc(ct_ready, 1)
            if i + 2 < TILES:
                cross_scores(i + 2)
            pe.wait_ge(cpT_ready, i + 1)
            if i >= 1:
                pe.wait_ge(cl_done, 2 * i)
            for blk in range(KT):
                h = blk // 2
                out = ps[:, (6 + blk // 4) * BANK + (blk % 4) * rows:(6 + blk // 4) * BANK + (blk % 4 + 1) * rows]
                mm = fill(out, [(mvt[:, src, m, blk * P:(blk + 1) * P], cpT[:, (2 * h + m) * rows:(2 * h + m + 1) * rows])
                                for m in range(MT)])
            mm.then_inc(co_ready, 1)

        for i in range(2):
            cross_scores(i)
        for i in range(TILES):
            cross_rest(i)
        pe.wait_ge(cl_done, 2 * (TILES - 1))
        assert turns.n % BANKS == 0
        project_and_norm(MT + 2 * TILES,
                         lambda g: pe.wait_ge(cl_done, 2 * TILES) if g == TILES - 2 else None)
        for c in range(N_PQ):
            feature_chunk(2 * (c % 2), HALF, 2)
        for b in range(BANKS):
            pe.wait_ge(emptied[b], (turns.n - 1 - b) // BANKS + 2)

        pe.wait_ge(keys_in, 16)
        for i in range(TILES):
            rows = ROWS[i]
            if i >= 2:
                pe.wait_ge(ssb_ready, i - 1)
            for s in range(2 * PK_HEADS):
                at = 4 * (i % 2) * BANK + s * P
                mm = fill(ps[0:rows, at:at + P], [(pqT[:, s, T0[i]:T0[i] + rows], keys[:, s, :])])
            mm.then_inc(score_ready, 1)
        pe.wait_ge(ssb_ready, TILES)

        def up(slot, gelus, between=None):
            for e in range(EG):
                b = 2 * (e % 2)
                pe.wait_ge(ge_ready, gelus(e))
                for part in range(2):
                    t = slice(part * HALF, (part + 1) * HALF)
                    for k in range(KT):
                        if e == 0 and part == 0 and k % 4 == 0:
                            pieces.up(2)
                            pe.wait_ge(w_ready, pieces.value())
                        h, l = weight(slot, k, slice(e * P, (e + 1) * P))
                        for w, (lhs, rhs) in enumerate(((h, actH[:, k, t]), (h, actL[:, k, t]), (l, actH[:, k, t]))):
                            mm = pe.matmul(bank(b + part, HALF), lhs, rhs, start=k == 0 and w == 0,
                                           stop=k == KT - 1 and w == 2)
                            if k == 0 and w == 0 and part == 0 and e == 0:
                                begin(mm)
                    if part == 1:
                        mm.then_inc(u_done, 1)
                    if between is not None:
                        between(2 * e + part)
            release[0] = 1

        with pe.Fori(0, RANK_GROUPS // 2 - 1) as i:
            pieces.enter(i, 8)
            for s in range(2):
                up(2 * s, lambda e: i * (2 * EG) + (EG * s + e + 1))
            pieces.leave(RANK_GROUPS // 2 - 1)
        up(0, lambda e: EG * (RANK_GROUPS - 2) + e + 1)

        def turn_choices(n):
            if n != 3:
                return
            pe.wait_ge(chosen_ready, 1)
            for i in range(TILES):
                if i >= 4:
                    pe.wait_ge(chT_copied, i - 3)
                for s in range(3):
                    at = (4 + i % 4) * BANK + s * P
                    mm = pe.transpose(ps[:, at:at + ROWS[i]], chosen[0:ROWS[i], i, s, :], ident[0:ROWS[i], 0:ROWS[i]])
                mm.then_inc(chT_ready, 1)

        up(2, lambda e: EG * (RANK_GROUPS - 1) + e + 1, turn_choices)

        pe.wait_ge(chT_copied, TILES)
        pe.sem_inc(c_filled, 4)

        def c_tokens(i, n):
            pe.wait_ge(hot_ready, i * 8 + (n + 1))
            for half in range(2):
                q = 2 * n + half
                pe.wait_ge(c_copied, i * 16 + (q + 1))
                for t in range(4):
                    at = (4 + q % 4) * BANK + t * P
                    mm = pe.matmul(ps[:, at:at + P], hot1[:, n % 2, 4 * half + t, :], hot2[:, n % 2, 4 * half + t, :],
                                   start=True, stop=True)
                mm.then_inc(c_filled, 1)

        with pe.Fori(0, C_GROUPS // 2) as i:
            pieces.enter(i, 8)
            for s in range(2):
                up(2 * s, lambda e: i * (2 * EG) + (EG * (RANK_GROUPS + s) + e + 1),
                   lambda n: c_tokens(i * 2, 8 * s + n))
            pieces.leave(C_GROUPS // 2)
        up(0, lambda e: EG * (EARLY - 2) + e + 1, lambda n: c_tokens(0, 8 * (C_GROUPS - 1) + n))
        up(2, lambda e: EG * (EARLY - 1) + e + 1)
        pe.wait_ge(c_copied, NT // 4 + 4)

        def down(slot, s, split, added):
            pe.wait_ge(gl_done, split)
            for d in range(KT):
                b = 4 + 2 * (d % 2)
                pe.wait_ge(acc_added, added(d))
                for part in range(2):
                    t = slice(part * HALF, (part + 1) * HALF)
                    for e in range(EG):
                        if d == 0 and part == 0 and e % 2 == 0:
                            pieces.up(2)
                            pe.wait_ge(w_ready, pieces.value())
                        at = (e % 2) * D + d * P
                        h = wH[:, slot + e // 2].rearrange("p k n -> p (k n)")[:, at:at + P]
                        l = wL[:, slot + e // 2].rearrange("p k n -> p (k n)")[:, at:at + P]
                        for w, (lhs, rhs) in enumerate(((h, gH[:, s, e, t]), (h, gL[:, s, e, t]), (l, gH[:, s, e, t]))):
                            mm = pe.matmul(bank(b + part, HALF), lhs, rhs, start=e == 0 and w == 0,
                                           stop=e == EG - 1 and w == 2)
                            if d == 0 and part == 0 and e == 0 and w == 0:
                                begin(mm)
                mm.then_inc(v_done, 1)
            release[0] = 1

        with pe.Fori(0, EARLY // 2) as i:
            pieces.enter(i, 8)
            for s in range(2):
                down(2 * s, s, i * (2 * EG) + EG * (s + 1), lambda d: i * (2 * KT) + (KT * s + d + 1))
            pieces.leave(EARLY // 2)
        up(0, lambda e: EG * EARLY + e + 1)
        with pe.Fori(0, LATE_PAIRS) as i:
            pieces.enter(i, 16)
            for s in range(2):
                up(2, lambda e: i * (2 * EG) + (EG * (EARLY + s + 1) + e + 1))
                down(0, s, i * (2 * EG) + EG * (EARLY + s + 1), lambda d: i * (2 * KT) + (KT * (EARLY + s) + d + 1))
            pieces.leave(LATE_PAIRS)
        up(2, lambda e: EG * (GROUPS - 1) + e + 1)
        down(0, 0, EG * (GROUPS - 1), lambda d: KT * (GROUPS - 2) + d + 1)
        down(2, 1, EG * GROUPS, lambda d: KT * (GROUPS - 1) + d + 1)

        pe.wait_ge(acc_added, KT * GROUPS + 2)
        for i in range(TILES):
            if i >= 2:
                pe.wait_ge(res_ready, i - 1)
            for k in range(KT):
                b = 2 * (i % 2) + k // 4
                mm = pe.transpose(ps[0:ROWS[i], b * BANK + (k % 4) * P:b * BANK + (k % 4 + 1) * P],
                                  acc[:, k, T0[i]:T0[i] + ROWS[i]], ident[:, :])
            mm.then_inc(yt2_ready, 1)


    @block.scalar
    def _(act):
        turns = Turns()

        def wait_filled():
            b, value = turns.take()
            act.wait_ge(filled[b], value)
            return b, value

        def skip(n):
            for _ in range(n):
                turns.take()

        def load_x():
            act.dma_start(xres[:, 0:4, :], a["x"][0:NP_TOK].rearrange("(i p) d -> p i d", p=P)).then_inc(x_in, 16)
            act.dma_start(xres[0:NS_TOK, 4, :], a["x"][NP_TOK:NT]).then_inc(x_in, 16)

        act.dma_start(memx[:, :, :], a["mem"].rearrange("(i p) d -> p i d", p=P)).then_inc(memx_in, 16)
        act.dma_start(ident[:, :], a["ident"]).then_inc(const_in, 16)
        act.dma_start(gain[:, :], a["gains"][0]).then_inc(gain_in, 16)
        load_x()

        for name, t in (("ropec", ropec), ("ropes", ropes), ("ropen", ropen)):
            act.dma_start(t[:, :, :], a[name]).then_inc(rope_in, 16)
        act.dma_start(mask[0:1, :], a["mask"]).then_inc(mask_in, 16)

        sums = [0]

        def squares(n_tiles, src, n):
            act.wait_ge(ssq_clear, n + 1)
            for i in range(n_tiles):
                if sums[0]:
                    act.wait_ge(ssq_ready, sums[0])
                rows = ROWS[i]
                act.activation(sq[0:rows, :], src[0:rows, i, :], ACT.Square, accum_out=sm["ssq"][0:rows, i:i + 1])\
                   .then_inc(ssq_ready, 1)
                sums[0] += 1
            act.wait_ge(var_ready, n + 1)
            act.activation(sm["rstd"][:, 0:n_tiles], sm["rstd"][:, 0:n_tiles], ACT.Sqrt).then_inc(std_ready, 1)

        def high_parts(n_tiles, turning=None):
            for i in range(n_tiles):
                high_tile(i, turning[i] if turning else [turns.take(), turns.take()])

        def high_tile(i, pair):
                for half, (b, value) in enumerate(pair):
                    act.wait_ge(filled[b], value)
                    act.activation(actH[:, half * 4:half * 4 + 4, T0[i]:T0[i] + ROWS[i]],
                                   bank(b, 4 * ROWS[i]).rearrange("p (k t) -> p k t", k=4), ACT.Copy)\
                       .then_inc(acth_done, 1)

        def next_gain(n, tiles):
            act.wait_ge(xn_ready, tiles)
            act.dma_start(gain[:, :], a["gains"][n]).then_inc(gain_in, 16)

        act.wait_ge(memx_in, 16)
        squares(MT, memx, 0)
        high_parts(MT)
        next_gain(1, MT)
        act.wait_ge(x_in, 32)
        squares(TILES, xres, 1)
        for q in range(N_CK * 4):
            b, value = wait_filled()
            act.activation(mk_sb[:, q, :], bank(b, MEM), ACT.Copy).then_inc(emptied[b], 1)
            act.wait_ge(emptied[b], value + 1)
        act.dma_start(o["mkT"].rearrange("(k p) m -> p k m", p=P), mk_sb[:, :, :]).then_inc(out_done, 16)
        for c in range(N_CV):
            for i in range(MT):
                b, value = wait_filled()
                act.activation(mv_sb[:, i, c * CHUNK:(c + 1) * CHUNK], bank(b), ACT.Copy).then_inc(emptied[b], 1)
                act.wait_ge(emptied[b], value + 1)
        act.dma_start(o["mv"].rearrange("(i p) d -> p i d", p=P), mv_sb[:, :, :]).then_inc(out_done, 16)
        high_parts(TILES)
        act.wait_ge(out_done, 32)
        act.wait_ge(xn_ready, MT + TILES)

        for s in range(2):
            act.dma_start(par[:, s, :], a["par"][s]).then_inc(par_in[s], 16)
        act.dma_start(lamp[:, :], a["lamp"]).then_inc(lamp_in, 16)
        act.dma_start(sm["gsub"], a["gsub"]).then_inc(lamp_in, 16)

        def projections(j, s, first=False, j_old=None, stored=None):
            if not first:
                act.wait_ge(conv_done, j_old + 1)
            for part in range(2):
                b, _ = wait_filled()
                if part == 0:
                    act.activation(rxp[:, s, 3:3 + HALF], bank(b, HALF), ACT.Copy).then_inc(emptied[b], 1)
                else:
                    act.activation(rxp[:, s, 3 + HALF:3 + NP_TOK], bank(b, NP_TOK - HALF), ACT.Copy)
                    act.activation(rxp[:, s, SEG + 3:XPW], ps[:, b * BANK + NP_TOK - HALF:b * BANK + HALF],
                                   ACT.Copy).then_inc(emptied[b], 1)
            if not first:
                act.wait_ge(yrec_ready, j_old + 1)
                act.dma_start(par[:, s, :], a["par"][j]).then_inc(par_in[s], 16)
            for dst, func in ((gel, ACT.Gelu), (sgr, ACT.Sigmoid), (sga, ACT.Sigmoid)):
                if dst is sga and not first:
                    act.wait_ge(sa_store[s], stored)
                for part in range(2):
                    b, value = wait_filled()
                    act.activation(dst[:, s, part * HALF:(part + 1) * HALF], bank(b, HALF), func).then_inc(emptied[b], 1)
                    if dst is sga:
                        act.wait_ge(emptied[b], value + 1)
            act.dma_start(sa_d[j], sga[:, s, :]).then_inc(sa_store[s], 16)

        def gate_block(j, s, first=False):
            for w, (dst, col) in enumerate(((gate_r, PAR_BA), (gate_i, PAR_BX))):
                for cut in (slice(0, CA_), slice(CA_, CW)):
                    b, value = wait_filled()
                    if w == 0 and cut.start == 0 and not first:
                        act.wait_ge(yrec_ready, j)
                    act.activation(dst[:, cut], ps[:, b * BANK:b * BANK + cut.stop - cut.start], ACT.Sigmoid,
                                   bias=par[:, s, col:col + 1]).then_inc(emptied[b], 1)
                    act.wait_ge(emptied[b], value + 1)
            if first:
                act.wait_ge(lam_ready, 1)
            act.activation(lru_a[:, 0:CW], gate_r[:, 0:CW], ACT.Exp, scale=sm["ncall"][:, bass.ds(j, 1)])\
               .then_inc(gate_ready, 1)
            act.activation(lru_t[:, 0:CW], gate_r[:, 0:CW], ACT.Tanh, scale=sm["pcall"][:, bass.ds(j, 1)])\
               .then_inc(gate_ready, 1)
            act.wait_ge(m_ready, j + 1)
            act.activation(lru_m[:, 0:CW], lru_m[:, 0:CW], ACT.Sqrt).then_inc(root_ready, 1)
            act.wait_ge(yrec_ready, j + 1)
            act.dma_start(r_d[j], yrec[:, s, :]).then_inc(r_store[s], 16)

        projections(0, 0, first=True)
        sp = sm["sp"]
        act.wait_ge(sp_neg, 1)
        act.activation(sp[:, 16:24], sp[:, 8:16], ACT.Exp, scale=-1.0).then_inc(sp_exp, 1)
        act.wait_ge(sp_one, 1)
        act.activation(sp[:, 32:40], sp[:, 24:32], ACT.Ln).then_inc(sp_ln, 1)
        act.wait_ge(lam_sums, 1)
        act.activation(sm["lamt"][:, 2:4], sm["lamt"][:, 0:2], ACT.Exp).then_inc(lam_exp, 1)
        projections(1, 1, first=True)
        gate_block(0, 0, first=True)
        with act.Fori(0, N_RG // 2 - 1) as i:
            turns.enter(i, 24)
            projections(i * 2 + 2, 0, j_old=i * 2, stored=i * 16 + 16)
            gate_block(i * 2 + 1, 1)
            projections(i * 2 + 3, 1, j_old=i * 2 + 1, stored=i * 16 + 16)
            gate_block(i * 2 + 2, 0)
            turns.leave(N_RG // 2 - 1)

        def turned(u):
            kind, c, i = TUNITS[u]
            if kind == "v":
                return
            n = sum(1 for k, _, _ in TUNITS[:u + 1] if k != "v")
            if kind == "k":
                act.wait_ge(rot_ready, n)
                act.dma_start(o["k"][T0[i]:T0[i] + ROWS[i], c * CHUNK:(c + 1) * CHUNK],
                              rot[0:ROWS[i], (n - 1) % 2, :]).then_inc(k_store[(n - 1) % 2], 16)
            b, _ = wait_filled()
            dst = kT if kind == "k" else qT
            act.activation(dst[:, 4 * c:4 * c + 4, T0[i]:T0[i] + ROWS[i]],
                           bank(b, 4 * ROWS[i]).rearrange("p (h t) -> p h t", h=4), ACT.Copy,
                           scale=1.0 if kind == "k" else DK ** -0.5).then_inc(emptied[b], 1)

        for u, (kind, c, i) in enumerate(TUNITS):
            b, value = turns.take()
            if kind == "v":
                act.wait_ge(filled[b], value)
                act.activation(vtok[0:ROWS[i], i, c * CHUNK:(c + 1) * CHUNK], bank(b, CHUNK, ROWS[i]),
                               ACT.Copy).then_inc(emptied[b], 1)
                if (c, i) == (1, TILES - 1):
                    act.wait_ge(emptied[b], value + 1)
                    act.dma_start(o["v"][0:NP_TOK].rearrange("(i p) d -> p i d", p=P), vtok[:, 0:4, :])\
                       .then_inc(out_done, 16)
                    act.dma_start(o["v"][NP_TOK:NT], vtok[0:NS_TOK, 4, :]).then_inc(out_done, 16)
            if u == 0:
                gate_block(N_RG - 1, 1)
                act.dma_start(o["cstate"], cstate[:, :, :]).then_inc(out_done, 16)
                act.dma_start(o["hstate"], hstate[:, :, :]).then_inc(out_done, 16)
                for s in range(2):
                    act.wait_ge(sa_store[s], 16 * N_RG // 2)
                    act.wait_ge(r_store[s], 16 * N_RG // 2)
                act.wait_ge(out_done, 64)
            if u >= 2:
                turned(u - 2)
        turned(len(TUNITS) - 2)
        turned(len(TUNITS) - 1)
        for s in range(2):
            act.wait_ge(k_store[s], 16 * TILES)

        def load_merge(i):
            t = slice(T0[i], T0[i] + ROWS[i])
            act.dma_start(sat[:, :, 0:ROWS[i]], sa_d[:, :, t].rearrange("k p t -> p k t")).then_inc(sat_in, 16)
            act.dma_start(rt[:, :, 0:ROWS[i]], r_d[:, :, t].rearrange("k p t -> p k t")).then_inc(sat_in, 16)

        def load_keys(h):
            act.dma_start(ckv[:, h % 2, :], a["ckT"][h]).then_inc(ck_in[h % 2], 16)

        def load_values(h):
            act.dma_start(cvv[:, h % 2, :].rearrange("p (k d) -> p k d", k=4),
                          a["cv"][:, :, h * DV:(h + 1) * DV]).then_inc(cv_in[h % 2], 16)

        def exps(u):
            i, h = UNITS[u]
            rows = ROWS[i]
            act.wait_ge(nm_ready, u + 1)
            if u >= 2:
                act.wait_ge(t_ready, u if (i, h) == (TILES - 1, 0) else u - 1)
            for s in range(2):
                if i < TILES - 1:
                    n = P * (i + 1)
                    dst, src = prob[:, u % 2, s, 0:n], bank(2 * (u % 2) + s, n)
                else:
                    dst, src = probs[u % 2][0:rows, s, :], ps[0:rows, 2 * s * BANK:2 * s * BANK + NT]
                col = 2 * (u % 2) + s
                ins = act.activation(dst, src, ACT.Exp, bias=sm["nmax"][0:rows, col:col + 1],
                                     accum_out=sm["z"][0:rows, col:col + 1])
            ins.then_inc(p_ready, 1)

        def copy_turned(u):
            i, h = UNITS[u]
            rows = ROWS[i]
            b = 4 + u % 2
            act.wait_ge(t_ready, u + 1)
            if u >= 2:
                act.wait_ge(pv_done, u - 1)
            if i < TILES - 1:
                n = P * (i + 1)
                act.activation(aT[:, u % 2, 0:n], bank(b, n), ACT.Copy).then_inc(aT_ready, 1)
            else:
                n = (PAST // P) * rows
                act.activation(aT[:, u % 2, 0:n], bank(b, n), ACT.Copy)
                act.activation(aT[0:rows, u % 2, n:n + rows], ps[0:rows, b * BANK + n:b * BANK + n + rows],
                               ACT.Copy).then_inc(aT_ready, 1)

        def copy_outputs(i):
            rows = ROWS[i]
            act.wait_ge(pv_done, HEADS * (i + 1))
            act.activation(osb[0:rows, :], ps[0:rows, 6 * BANK:8 * BANK], ACT.Copy).then_inc(osb_ready, 1)

        def root(i):
            act.wait_ge(ovar_ready, i + 1)
            std = sm["orstd"][0:ROWS[i], :]
            act.activation(std, std, ACT.Sqrt).then_inc(ostd_ready, 1)

        def merged_high(i):
            act.wait_ge(merged, i + 1)
            act.activation(actH[:, :, T0[i]:T0[i] + ROWS[i]], sat[:, :, 0:ROWS[i]], ACT.Copy).then_inc(mh_done, 1)

        load_merge(0)
        for h in range(2):
            load_keys(h)
        for u, (i, h) in enumerate(UNITS):
            exps(u)
            if i == TILES - 1 and h + 2 < HEADS:
                load_keys(h + 2)
            if u > 0:
                copy_turned(u - 1)
            if i > 0 and h == 0:
                copy_outputs(i - 1)
            if i > 0 and h == 1:
                root(i - 1)
            if i > 0 and h == 2:
                merged_high(i - 1)
            if i > 0 and h == 3:
                act.wait_ge(ml_done, i)
                load_merge(i)
            if (i, h) == (TILES - 1, 0):
                act.wait_ge(out_done, 96)
                load_values(0)
                load_values(1)
            elif i == TILES - 1 and h >= 2:
                act.wait_ge(pv_done, u - 1)
                load_values(h)
        last = TILES - 1
        copy_turned(len(UNITS) - 1)
        load_x()
        copy_outputs(last)
        root(last)
        next_gain(2, MT + TILES)
        merged_high(last)
        act.wait_ge(ml_done, TILES)


        def norm_behind(variances):
            _, second, turning = projection_turns(turns)
            for i in range(TILES):
                rows = ROWS[i]
                b, value = second[i]
                act.wait_ge(emptied[b], value + 1)
                act.wait_ge(ssq_ready, sums[0])
                act.activation(sq[0:rows, :], xres[0:rows, i, :], ACT.Square, accum_out=sm["ssq"][0:rows, i:i + 1])\
                   .then_inc(ssq_ready, 1)
                sums[0] += 1
                act.wait_ge(var_ready, variances + i + 1)
                std = sm["rstd"][0:rows, i:i + 1]
                act.activation(std, std, ACT.Sqrt).then_inc(std_ready, 1)
                if i >= 2:
                    high_tile(i - 2, turning[i - 2])
            return turning

        turning = norm_behind(2)
        for i in range(TILES - 2, TILES):
            high_tile(i, turning[i])
        next_gain(3, MT + 2 * TILES)
        act.dma_start(mkT[:, 0, :, :], o["mkT"].rearrange("(k p) m -> p k m", p=P)).then_inc(mem_in, 16)
        act.dma_start(mkT[:, 1, :, :], a["cmkT"].rearrange("(k p) m -> p k m", p=P)).then_inc(mem_in, 16)
        act.dma_start(mvt[:, 0, :, :], o["mv"].rearrange("(i p) d -> p i d", p=P)).then_inc(mem_in, 16)
        act.dma_start(mvt[:, 1, :, :], a["cmv"].rearrange("(i p) d -> p i d", p=P)).then_inc(mem_in, 16)
        for q in range(N_CQ * 4):
            for part in range(2):
                b, _ = wait_filled()
                act.activation(qcT[:, q, part * HALF:(part + 1) * HALF], bank(b, HALF), ACT.Copy,
                               scale=CA_DH ** -0.5).then_inc(emptied[b], 1)

        def cross_exps(i):
            rows = ROWS[i]
            act.wait_ge(cm_ready, i + 1)
            if i >= 2:
                act.wait_ge(ct_ready, i - 1)
            for h in range(CA_HEADS):
                c = 4 * (i % 2) + h
                at = 2 * (i % 2) * BANK + h * MEM
                ins = act.activation(cp[0:rows, i % 2, h * MEM:(h + 1) * MEM], ps[0:rows, at:at + MEM],
                                     ACT.Exp, bias=sm["nmax"][0:rows, c:c + 1], accum_out=sm["mz"][0:rows, c:c + 1])
            ins.then_inc(ce_ready, 1)

        cross_exps(0)
        for i in range(TILES):
            rows = ROWS[i]
            act.wait_ge(ct_ready, i + 1)
            if i >= 1:
                act.wait_ge(co_ready, i)
            for m in range(2):
                ins = act.activation(cpT[:, m * 4 * rows:(m + 1) * 4 * rows], bank(4 + m, 4 * rows), ACT.Copy)
            ins.then_inc(cpT_ready, 1)
            if i + 1 < TILES:
                cross_exps(i + 1)
            act.wait_ge(co_ready, i + 1)
            for m in range(2):
                act.activation(actH[:, 4 * m:4 * m + 4, T0[i]:T0[i] + rows],
                               bank(6 + m, 4 * rows).rearrange("p (k t) -> p k t", k=4), ACT.Copy).then_inc(ch_done, 1)

        turning = norm_behind(2 + TILES)
        act.dma_start(x2_d[0:NP_TOK].rearrange("(i p) d -> p i d", p=P), xres[:, 0:4, :]).then_inc(x2_store, 16)
        act.dma_start(x2_d[NP_TOK:NT], xres[0:NS_TOK, 4, :]).then_inc(x2_store, 16)
        for i in range(TILES - 2, TILES):
            high_tile(i, turning[i])
        next_gain(4, MT + 3 * TILES)
        act.dma_start(keys[:, :, :], a["keysT"]).then_inc(keys_in, 16)
        act.dma_start(iota16[:, :], a["iota"][:, 0:TOPK]).then_inc(iota16_in, 16)
        act.wait_ge(x2_store, 32)
        for q in range(N_PQ * 4):
            for part in range(2):
                b, _ = wait_filled()
                act.activation(pqT[:, q, part * HALF:(part + 1) * HALF], bank(b, HALF), ACT.Copy)\
                   .then_inc(emptied[b], 1)
        for i in range(TILES):
            rows = ROWS[i]
            act.wait_ge(score_ready, i + 1)
            act.activation(ssb[0:rows, i, :, :].rearrange("p h n -> p (h n)"),
                           ps[0:rows, 4 * (i % 2) * BANK:4 * (i % 2 + 1) * BANK], ACT.Copy).then_inc(ssb_ready, 1)

        act.sem_inc(ge_ready, 2)

        def gelu(e, n):
            act.wait_ge(u_done, n + 1)
            act.activation(ge[:, e, :].rearrange("p (c n) -> p c n", c=2), halves(2 * (e % 2)), ACT.Gelu)\
               .then_inc(ge_ready, 1)

        def gelu_early(e, n, stored):
            if stored is not None:
                act.wait_ge(ge_store[e], stored)
            gelu(e, n)
            act.wait_ge(ge_ready, n + 3)
            act.dma_start(ge_d[n], ge[:, e, :]).then_inc(ge_store[e], 16)

        for g in range(2):
            for e in range(EG):
                gelu_early(e, EG * g + e, 16 * g if g else None)
        with act.Fori(0, RANK_GROUPS - 3) as i:
            for e in range(EG):
                gelu_early(e, i * EG + (2 * EG + e), i * 16 + 32)
        act.wait_ge(gexp_in, TILES)
        for rows, tiles in ((P, slice(0, TILES - 1)), (NS_TOK, slice(TILES - 1, TILES))):
            g = chosen[0:rows, tiles, 2, :]
            act.activation(g, g, ACT.Exp).then_inc(gexp_out, 1)

        def early(e):
            gelu_early(e, EG * (RANK_GROUPS - 1) + e, 16 * (RANK_GROUPS - 1))

        early(0)
        early(1)
        for i in range(TILES):
            rows, at = ROWS[i], (4 + i % 4) * BANK
            act.wait_ge(chT_ready, i + 1)
            act.activation(chosenT[:, :, T0[i]:T0[i] + rows],
                           ps[:, at:at + 3 * P].rearrange("p (s t) -> p s t", s=3)[:, :, 0:rows],
                           ACT.Copy).then_inc(chT_copied, 1)
        early(2)
        early(3)

        act.sem_inc(c_copied, 4)

        def c_group(i, n, stored):
            for k in range(8):
                s, at = k // 4, 8 * (k % 4)
                if k % 4 == 0 and stored is not None:
                    act.wait_ge(c_store[s], stored)
                for half in range(2):
                    q = 16 * n + 2 * k + half
                    act.wait_ge(c_filled, i * 16 + (q + 5))
                    act.activation(cst[:, s, :, at + 4 * half:at + 4 * half + 4],
                                   bank(4 + q % 4).rearrange("p (t e) -> p e t", t=4), ACT.Copy).then_inc(c_copied, 1)
                if k % 2 == 0:
                    gelu_early(k // 2, i * EG + (EG * (RANK_GROUPS + n) + k // 2), i * 16 + 16 * (RANK_GROUPS + n))
                if k % 4 == 3:
                    act.wait_ge(c_copied, i * 16 + (16 * n + 2 * k + 2 + 4))
                    act.dma_start(c_d[i * 2 + (2 * n + s)], cst[:, s, :, :]).then_inc(c_store[s], 16)

        c_group(0, 0, None)
        with act.Fori(0, C_GROUPS - 1) as i:
            c_group(i, 1, i * 16 + 16)
        act.sem_inc(gh_done, 2)

        def load_c(g, s):
            act.dma_start(cg[:, s], c_d[:, :, bass.ts(g, EG), :].rearrange("b p e t -> p b e t")).then_inc(c_in[s], 16)

        def load_ge(e, n):
            act.dma_start(ge[:, e, :], ge_d[n]).then_inc(ge_in[e], 16)

        def high(e, s, n, used):
            act.wait_ge(gf_ready, n + 3)
            if used is not None:
                act.wait_ge(v_done, used)
            act.activation(gH[:, s, e, :], gf[:, e % 2, :], ACT.Copy).then_inc(gh_done, 1)

        for s in range(2):
            act.wait_ge(c_store[s], 16 * C_GROUPS)
        load_c(EARLY - 1, 0)
        load_c(0, 1)
        for e in range(EG):
            act.wait_ge(ge_store[e], 16 * (EARLY - 1))
            gelu(e, EG * (EARLY - 1) + e)
            if e >= 1:
                high(e - 1, 0, e - 1, None)
                load_ge(e - 1, e - 1)
        high(EG - 1, 0, EG - 1, None)
        load_ge(EG - 1, EG - 1)
        load_c(1, 0)
        for e in range(EG):
            high(e, 1, EG + e, None)
            load_ge(e, EG + e)
        load_c(2, 1)
        with act.Fori(0, EARLY // 2 - 2) as i:
            for s in range(2):
                for e in range(EG):
                    high(e, s, i * (2 * EG) + (EG * (s + 2) + e), i * (2 * KT) + KT * (s + 1))
                    load_ge(e, i * (2 * EG) + (EG * (s + 2) + e))
                load_c(i * 2 + (3 + s), s)
        for g in (EARLY - 2, EARLY - 1):
            for e in range(EG):
                high(e, g % 2, EG * g + e, KT * (g - 1))
                if g == EARLY - 2:
                    load_ge(e, EG * g + e)
            load_c(g + 2 if g == EARLY - 1 else EARLY, g % 2)

        def gelu_and_high(e, s, n, used):
            act.wait_ge(gf_ready, n - 1)
            gelu(e, n)
            high(e, s, n, used)

        for e in range(EG):
            gelu_and_high(e, 0, EG * EARLY + e, KT * (EARLY - 1))
        with act.Fori(0, LATE_PAIRS) as i:
            for s in range(2):
                load_c(i * 2 + (EARLY + 2 + s), s)
                for e in range(EG):
                    n = EG * (EARLY + 1 + s) + e
                    gelu_and_high(e, 1 - s, i * (2 * EG) + n, i * (2 * KT) + KT * (EARLY + s))
        for e in range(EG):
            gelu_and_high(e, 1, EG * (GROUPS - 1) + e, KT * (GROUPS - 2))

        act.wait_ge(gl_done, EG * GROUPS)
        act.dma_start(x2b[:, 0:4, :], x2_d[0:NP_TOK].rearrange("(i p) d -> p i d", p=P)).then_inc(x2_in, 16)
        act.dma_start(x2b[0:NS_TOK, 4, :], x2_d[NP_TOK:NT]).then_inc(x2_in, 16)
        for i in range(TILES):
            rows = ROWS[i]
            act.wait_ge(res_ready, i + 1)
            if i >= 2:
                act.wait_ge(y_store[i % 2], 16 * (i // 2))
            act.activation(yout[0:rows, i % 2, :], x2b[0:rows, i, :], ACT.Square,
                           accum_out=sm["ssq"][0:rows, i:i + 1]).then_inc(ssq_ready, 1)
            act.wait_ge(var_ready, 2 + 2 * TILES + i + 1)
            act.activation(sm["rstd"][0:rows, i:i + 1], sm["rstd"][0:rows, i:i + 1], ACT.Sqrt).then_inc(std_ready, 1)
            act.wait_ge(y_ready, i + 1)
            act.dma_start(o["y"][T0[i]:T0[i] + rows, :], yout[0:rows, i % 2, :]).then_inc(y_store[i % 2], 16)
        for s in range(2):
            act.wait_ge(y_store[s], 16 * ((TILES + 1 - s) // 2))

    @block.vector
    def _(ve):
        turns = Turns()
        step = Steps(ve, ve_step)

        def wait_filled():
            b, value = turns.take()
            ve.wait_ge(filled[b], value)
            return b, value

        def skip(n):
            for _ in range(n):
                turns.take()

        xn_groups = []
        sums = [0]

        def normalise(n_tiles, src, n):
            first = len(xn_groups)
            rstd = sm["rstd"][:, 0:n_tiles]
            step.done(ve.memset(sm["ssq"], 0.0))
            ve.sem_inc(ssq_clear, 1)
            sums[0] += n_tiles
            ve.wait_ge(ssq_ready, sums[0])
            ve.tensor_scalar(rstd, sm["ssq"][:, 0:n_tiles], 1.0 / D, RMS_EPS, ALU.mult, ALU.add).then_inc(var_ready, 1)
            ve.wait_ge(std_ready, n + 1)
            step.done(ve.reciprocal(rstd, rstd))
            ve.wait_ge(gain_in, 16 * (n + 1))
            for i in range(n_tiles):
                if first + i >= 2:
                    b, value = xn_groups[first + i - 2]
                    ve.wait_ge(filled[b], value)
                rows = ROWS[i]
                ve.scalar_tensor_tensor(xn[0:rows, (first + i) % 2, :], src[0:rows, i, :], sm["rstd"][0:rows, i:i + 1],
                                        gain[0:rows, :], ALU.mult, ALU.mult).then_inc(xn_ready, 1)
                if n == 1 and i == 0:
                    skip(N_CK * 4 + N_CV * MT)
                take = [turns.take(), turns.take()]
                xn_groups.append(take[1])
                todo.append((first + i, i, take))
                if i >= 1:
                    low_parts(*todo.pop(0))
            low_parts(*todo.pop(0))

        todo = []

        def low_parts(tile, i, take):
            for half, (b, value) in enumerate(take):
                ve.wait_ge(acth_done, 2 * tile + half + 1)
                cut = (slice(None), slice(half * 4, half * 4 + 4), slice(T0[i], T0[i] + ROWS[i]))
                ve.tensor_tensor(actL[cut], bank(b, 4 * ROWS[i]).rearrange("p (k t) -> p k t", k=4),
                                 actH[cut].bitcast(F32), ALU.subtract).then_inc(emptied[b], 1)

        normalise(MT, memx, 0)
        normalise(TILES, xres, 1)

        sp, lamt, lamv = sm["sp"], sm["lamt"], sm["lamv"]
        neg, mag, exp_, one, log = (sp[:, 8 * k:8 * k + 8] for k in range(5))
        ve.wait_ge(lamp_in, 32)
        step.done(ve.tensor_scalar(neg, lamp[:, 4 * DK:4 * DK + KT], -1.0, None, ALU.mult))
        ve.tensor_tensor(mag, neg, lamp[:, 4 * DK:4 * DK + KT], ALU.max).then_inc(sp_neg, 1)
        ve.wait_ge(sp_exp, 1)
        ve.tensor_scalar(one, exp_, 1.0, None, ALU.add).then_inc(sp_one, 1)
        for k in range(2):
            step.done(ve.tensor_tensor(lamp[:, 2 * k * DK:(2 * k + 1) * DK], lamp[:, 2 * k * DK:(2 * k + 1) * DK],
                                       lamp[:, (2 * k + 1) * DK:(2 * k + 2) * DK], ALU.mult))
        step.done(ve.tensor_reduce(lamt[:, 0:1], lamp[:, 0:DK], AX, ALU.add))
        ve.tensor_reduce(lamt[:, 1:2], lamp[:, 2 * DK:3 * DK], AX, ALU.add).then_inc(lam_sums, 1)
        ve.wait_ge(sp_ln, 1)
        step.done(ve.tensor_scalar(mag, one, -1.0, None, ALU.add))
        step.done(ve.tensor_scalar(one, mag, 0.0, None, ALU.is_equal))
        step.done(ve.tensor_scalar(mag, mag, 1e-30, None, ALU.max))
        step.done(ve.reciprocal(mag, mag))
        step.done(ve.tensor_tensor(mag, mag, log, ALU.mult))
        step.done(ve.tensor_tensor(mag, mag, exp_, ALU.mult))
        step.done(ve.tensor_tensor(exp_, exp_, one, ALU.mult))
        step.done(ve.tensor_tensor(mag, mag, exp_, ALU.add))
        step.done(ve.tensor_scalar(neg, neg, 0.0, None, ALU.max))
        step.done(ve.tensor_tensor(neg, neg, mag, ALU.add))
        step.done(ve.tensor_scalar(sm["pcall"], neg, RG_C, None, ALU.mult))
        ve.wait_ge(lam_exp, 1)
        step.done(ve.tensor_tensor(lamt[:, 4:5], lamt[:, 2:3], lamt[:, 3:4], ALU.subtract))
        step.done(ve.tensor_scalar(lamv[:, 1:2], lamt[:, 4:5], LAM_INIT, -1.0, ALU.add, ALU.mult))
        step.done(ve.memset(lamv[:, 0:1], 1.0))
        step.done(ve.tensor_scalar(sm["gsub"], sm["gsub"], 1.0 - LAM_INIT, None, ALU.mult))
        for s in range(2):
            step.done(ve.memset(rxp[:, s, 0:CONVW - 1], 0.0))
        ve.tensor_scalar(sm["ncall"], neg, -RG_C, None, ALU.mult).then_inc(lam_ready, 1)

        def convolve(j, s, arrived, j_old=None):
            groups = [turns.take(), turns.take()]
            ve.wait_ge(par_in[s], arrived)
            if j_old is not None:
                ve.wait_ge(yrec_ready, j_old + 1)
            step.done(ve.tensor_copy(rxp[:, s, SEG:SEG + 3], par[:, s, PAR_SC:PAR_SC + 3]))
            for b, value in groups:
                ve.wait_ge(emptied[b], value + 1)
            step.done(ve.tensor_copy(cstate[:, bass.ds(j, 1), 0:3], rxp[:, s:s + 1, NP_TOK:NP_TOK + 3]))
            step.done(ve.tensor_copy(cstate[:, bass.ds(j, 1), 3:6], rxp[:, s:s + 1, SEG + NS_TOK:SEG + NS_TOK + 3]))
            step.done(ve.tensor_scalar(conv[:, s, 0:CW], rxp[:, s, 0:CW], par[:, s, PAR_CW:PAR_CW + 1],
                                       par[:, s, PAR_CB:PAR_CB + 1], ALU.mult, ALU.add))
            for w in range(1, CONVW):
                ins = ve.scalar_tensor_tensor(conv[:, s, 0:CW], rxp[:, s, w:w + CW], par[:, s, PAR_CW + w:PAR_CW + w + 1],
                                              conv[:, s, 0:CW], ALU.mult, ALU.add)
                if w < CONVW - 1:
                    step.done(ins)
            ins.then_inc(conv_done, 1)
            skip(6)

        def recur(j, s, stored=None):
            skip(4)
            ve.wait_ge(gate_ready, j * 2 + 2)
            step.done(ve.tensor_scalar(lru_m[:, 0:CW], lru_t[:, 0:CW], 1.0, None, ALU.add))
            step.done(ve.reciprocal(lru_m[:, 0:CW], lru_m[:, 0:CW]))
            ve.scalar_tensor_tensor(lru_m[:, 0:CW], lru_t[:, 0:CW], 2.0, lru_m[:, 0:CW], ALU.mult, ALU.mult)\
              .then_inc(m_ready, 1)
            step.done(ve.tensor_tensor(gate_i[:, 0:CW], gate_i[:, 0:CW], conv[:, s, 0:CW], ALU.mult))
            ve.wait_ge(root_ready, j + 1)
            step.done(ve.tensor_tensor(gate_i[:, 0:CW], gate_i[:, 0:CW], lru_m[:, 0:CW], ALU.mult))
            step.done(ve.tensor_tensor_scan(lru_h[:, 0:NP_TOK], lru_a[:, 0:NP_TOK], gate_i[:, 0:NP_TOK], 0.0,
                                            ALU.mult, ALU.add))
            step.done(ve.tensor_tensor_scan(lru_h[:, NP_TOK:NT], lru_a[:, SEG:CW], gate_i[:, SEG:CW],
                                            par[:, s, PAR_H0:PAR_H0 + 1], ALU.mult, ALU.add))
            step.done(ve.tensor_copy(hstate[:, bass.ds(j, 1), 0:1], lru_h[:, NP_TOK - 1:NP_TOK].unsqueeze(1)))
            step.done(ve.tensor_copy(hstate[:, bass.ds(j, 1), 1:2], lru_h[:, NT - 1:NT].unsqueeze(1)))
            step.done(ve.tensor_tensor(lru_h[:, :], lru_h[:, :], gel[:, s, :], ALU.mult))
            if stored is not None:
                ve.wait_ge(r_store[s], stored)
            ve.tensor_tensor(yrec[:, s, :], lru_h[:, :], sgr[:, s, :], ALU.mult).then_inc(yrec_ready, 1)
            ve.wait_ge(yrec_ready, j + 1)

        convolve(0, 0, 16)
        convolve(1, 1, 16)
        recur(0, 0)
        with ve.Fori(0, N_RG // 2 - 1) as i:
            turns.enter(i, 24)
            step.enter(i, 2 * (3 + CONVW - 1 + 1 + 8))
            convolve(i * 2 + 2, 0, i * 16 + 32, i * 2)
            recur(i * 2 + 1, 1, None)
            convolve(i * 2 + 3, 1, i * 16 + 32, i * 2 + 1)
            recur(i * 2 + 2, 0, i * 16 + 16)
            turns.leave(N_RG // 2 - 1)
            step.leave(N_RG // 2 - 1)

        rots = []
        turned_groups = {}

        def turned(u):
            if TUNITS[u][0] != "v":
                turned_groups[u] = turns.take()

        for u, (kind, c, i) in enumerate(TUNITS):
            b, value = turns.take()
            if u >= 2:
                turned(u - 2)
            if u == 0:
                recur(N_RG - 1, 1, None)
                ve.wait_ge(rope_in, 48)
            if kind != "v":
                rows, r = ROWS[i], len(rots) % 2
                ve.wait_ge(filled[b], value)
                src = bank(b, CHUNK, rows).rearrange("p (h s n) -> p h s n", s=2, n=32)
                r1 = rot1[0:rows, :].rearrange("p (h s n) -> p h s n", s=2, n=32)
                r2 = rot2[0:rows, :].rearrange("p (h s n) -> p h s n", s=2, n=32)
                heads = [rows, CHUNK // DK, 32]
                if rots:
                    ve.wait_ge(rot_ready, len(rots))
                ve.tensor_tensor(rot1[0:rows, :].rearrange("p (h n) -> p h n", n=32),
                                 bank(b, CHUNK, rows).rearrange("p (h n) -> p h n", n=32),
                                 ropec[0:rows, i:i + 1, :].broadcast_to([rows, CHUNK // 32, 32]), ALU.mult)
                ve.tensor_tensor(r2[:, :, 0, :], src[:, :, 1, :], ropen[0:rows, i:i + 1, :].broadcast_to(heads), ALU.mult)
                ve.tensor_tensor(r2[:, :, 1, :], src[:, :, 0, :], ropes[0:rows, i:i + 1, :].broadcast_to(heads), ALU.mult)\
                  .then_inc(emptied[b], 1)
                ve.wait_ge(emptied[b], value + 1)
                if len(rots) >= 2:
                    before = rots[-2]
                    tb, tv = turned_groups[before]
                    ve.wait_ge(filled[tb], tv)
                    if TUNITS[before][0] == "k":
                        ve.wait_ge(k_store[r], 16 * ((len(rots) - 2) // 2 + 1))
                ve.tensor_tensor(rot[0:rows, r, :], rot1[0:rows, :], rot2[0:rows, :], ALU.add).then_inc(rot_ready, 1)
                rots.append(u)
        turned(len(TUNITS) - 2)
        turned(len(TUNITS) - 1)

        def maxima(u):
            i, h = UNITS[u]
            rows = ROWS[i]
            ve.wait_ge(sc_ready, u + 1)
            if u >= 2:
                ve.wait_ge(p_ready, u - 1)
            if i < TILES - 1:
                n = P * (i + 1)
                src = ps[:, 2 * (u % 2) * BANK:(2 * (u % 2) + 2) * BANK].rearrange("p (s n) -> p s n", s=2)[:, :, 0:n]
            else:
                src = ps[0:rows, 0:4 * BANK].rearrange("p (s n) -> p s n", s=2)[:, :, 0:NT]
            ve.tensor_reduce(sm["nmax"][0:rows, 2 * (u % 2):2 * (u % 2) + 2], src, AX, ALU.max, negate=True)\
              .then_inc(nm_ready, 1)

        def combine(u):
            i, h = UNITS[u]
            rows = ROWS[i]
            if i < TILES - 1:
                p1, p2 = (prob[:, u % 2, s, 0:P * (i + 1)] for s in range(2))
            else:
                p1, p2 = (probs[u % 2][0:rows, s, :] for s in range(2))
            rz = sm["pk"][0:rows, 0:2]
            ve.wait_ge(p_ready, u + 1)
            if u >= 1:
                ve.wait_ge(a_ready, u)
            step.done(ve.reciprocal(rz, sm["z"][0:rows, 2 * (u % 2):2 * (u % 2) + 2]))
            step.done(ve.tensor_tensor(rz, rz, lamv[0:rows, :], ALU.mult))
            step.done(ve.tensor_scalar(p2, p2, rz[:, 1:2], None, ALU.mult))
            ve.scalar_tensor_tensor(p1, p1, rz[:, 0:1], p2, ALU.mult, ALU.add).then_inc(a_ready, 1)

        osq = gain

        def variance(i):
            rows = ROWS[i]
            ve.wait_ge(osb_ready, i + 1)
            step.done(ve.tensor_tensor(osq[0:rows, :], osb[0:rows, :], osb[0:rows, :], ALU.mult))
            step.done(ve.tensor_reduce(sm["oss"][0:rows, :], osq[0:rows, :].rearrange("p (h d) -> p h d", h=HEADS),
                                       AX, ALU.add))
            ve.tensor_scalar(sm["orstd"][0:rows, :], sm["oss"][0:rows, :], 1.0 / DV, SUBLN_EPS, ALU.mult, ALU.add)\
              .then_inc(ovar_ready, 1)

        def merge(i):
            rows = ROWS[i]
            ve.wait_ge(ostd_ready, i + 1)
            step.done(ve.reciprocal(sm["orstd"][0:rows, :], sm["orstd"][0:rows, :]))
            heads = osb[0:rows, :].rearrange("p (h d) -> p h d", h=HEADS)
            ve.tensor_tensor(heads, heads, sm["orstd"][0:rows, :].unsqueeze(2).broadcast_to([rows, HEADS, DV]),
                             ALU.mult).then_inc(on_ready, 1)
            ve.wait_ge(yt_ready, i + 1)
            ve.wait_ge(sat_in, 32 * (i + 1))
            for m in range(2):
                part = sat[:, 4 * m:4 * m + 4, 0:rows]
                ins = ve.scalar_tensor_tensor(part, bank(6 + m, 4 * rows).rearrange("p (k t) -> p k t", k=4),
                                              sm["gsub"], part, ALU.mult, ALU.mult)
            ins.then_inc(turned_used, 1)
            ve.wait_ge(turned_used, i + 1)
            ve.tensor_tensor(sat[:, :, 0:rows], sat[:, :, 0:rows], rt[:, :, 0:rows], ALU.add).then_inc(merged, 1)

        def merged_low(i):
            t = slice(T0[i], T0[i] + ROWS[i])
            ve.wait_ge(mh_done, i + 1)
            ve.tensor_tensor(actL[:, :, t], sat[:, :, 0:ROWS[i]], actH[:, :, t].bitcast(F32), ALU.subtract)\
              .then_inc(ml_done, 1)

        for u, (i, h) in enumerate(UNITS):
            if u > 0:
                combine(u - 1)
            maxima(u)
            if i > 0 and h == 1:
                variance(i - 1)
            if i > 0 and h == 2:
                merge(i - 1)
            if i > 0 and h == 3:
                merged_low(i - 1)
        combine(len(UNITS) - 1)
        variance(TILES - 1)
        merge(TILES - 1)
        merged_low(TILES - 1)

        def project_and_norm(n, variances):
            first, second, turning = projection_turns(turns)
            tile0 = len(xn_groups)
            xn_groups.extend(pair[1] for pair in turning)
            ve.wait_ge(gain_in, 16 * (n + 1))
            for c, groups in enumerate((first, second)):
                for i, (b, value) in enumerate(groups):
                    rows = ROWS[i]
                    ve.wait_ge(filled[b], value)
                    part = xres[0:rows, i, c * CHUNK:(c + 1) * CHUNK]
                    ve.tensor_tensor(part, part, bank(b, CHUNK, rows), ALU.add).then_inc(emptied[b], 1)
                    if c == 0:
                        continue
                    sums[0] += 1
                    ve.wait_ge(ssq_ready, sums[0])
                    rstd = sm["rstd"][0:rows, i:i + 1]
                    ve.tensor_scalar(rstd, sm["ssq"][0:rows, i:i + 1], 1.0 / D, RMS_EPS, ALU.mult, ALU.add)\
                      .then_inc(var_ready, 1)
                    ve.wait_ge(std_ready, variances + i + 1)
                    step.done(ve.reciprocal(rstd, rstd))
                    tb, tv = xn_groups[tile0 + i - 2]
                    ve.wait_ge(filled[tb], tv)
                    ve.scalar_tensor_tensor(xn[0:rows, (tile0 + i) % 2, :], xres[0:rows, i, :], rstd, gain[0:rows, :],
                                            ALU.mult, ALU.mult).then_inc(xn_ready, 1)
                    if i >= 2:
                        low_parts(tile0 + i - 2, i - 2, turning[i - 2])
            for i in range(TILES - 2, TILES):
                low_parts(tile0 + i, i, turning[i])

        ve.wait_ge(x_in, 64)
        project_and_norm(2, 2)
        skip(N_CQ * 8)

        def cross_maxima(i):
            ve.wait_ge(cs_ready, i + 1)
            if i >= 2:
                ve.wait_ge(ce_ready, i - 1)
            rows, at = ROWS[i], 2 * (i % 2) * BANK
            ve.tensor_reduce(sm["nmax"][0:rows, 4 * (i % 2):4 * (i % 2) + 4],
                             ps[0:rows, at:at + 2 * BANK].rearrange("p (h n) -> p h n", h=CA_HEADS), AX, ALU.max,
                             negate=True).then_inc(cm_ready, 1)

        def cross_low(i):
            rows = ROWS[i]
            for m in range(2):
                ve.wait_ge(ch_done, 2 * i + m + 1)
                cut = (slice(None), slice(4 * m, 4 * m + 4), slice(T0[i], T0[i] + rows))
                ve.tensor_tensor(actL[cut], bank(6 + m, 4 * rows).rearrange("p (k t) -> p k t", k=4),
                                 actH[cut].bitcast(F32), ALU.subtract).then_inc(cl_done, 1)

        cross_maxima(0)
        for i in range(TILES):
            rows = ROWS[i]
            ve.wait_ge(ce_ready, i + 1)
            if i >= 1:
                ve.wait_ge(cn_ready, i)
            rz = sm["pk"][0:rows, 0:4]
            step.done(ve.reciprocal(rz, sm["mz"][0:rows, 4 * (i % 2):4 * (i % 2) + 4]))
            heads = cp[0:rows, i % 2, :].rearrange("p (h n) -> p h n", h=CA_HEADS)
            ve.tensor_tensor(heads, heads, rz.unsqueeze(2).broadcast_to([rows, CA_HEADS, MEM]), ALU.mult)\
              .then_inc(cn_ready, 1)
            if i + 1 < TILES:
                cross_maxima(i + 1)
            if i >= 1:
                cross_low(i - 1)
        cross_low(TILES - 1)
        project_and_norm(3, 2 + TILES)
        skip(N_PQ * 8)

        S2 = 2 * PK_HEADS
        halves_of = work[:, :].rearrange("p (s n) -> p s n", s=S2)
        sums_of = cand[:, :].rearrange("p (h n) -> p h n", h=PK_HEADS)
        rest_of = work[:, :].rearrange("p (h n) -> p h n", h=PK_HEADS)

        def best_of(n, values, rest, best_values, best_places, rows, used=None):
            for s in range(n):
                ins = ve.max(best_values[0:rows, s, 0:8], values[0:rows, s, :])
            step.done(ins)
            for s in range(n):
                ve.match_replace(rest[0:rows, s, :], best_values[0:rows, s, 0:8], values[0:rows, s, :], NEG)
                ins = ve.max_index(best_places[0:rows, s, 0:8], best_values[0:rows, s, 0:8], values[0:rows, s, :])
            step.done(ins)
            for s in range(n):
                ins = ve.max(best_values[0:rows, s, 8:16], rest[0:rows, s, :])
            step.done(ins)
            for s in range(n):
                ins = ve.max_index(best_places[0:rows, s, 8:16], best_values[0:rows, s, 8:16], rest[0:rows, s, :])
            step.done(ins)

        ve.wait_ge(iota16_in, 16)
        ve.wait_ge(ssb_ready, TILES)
        for i in range(TILES):
            rows = ROWS[i]
            best_of(S2, ssb[:, i], halves_of, top, topi, rows)
            step.done(ve.tensor_copy(topf[0:rows, :, :], topi[0:rows, :, :]))
            pairs = top[0:rows].rearrange("p (h r) t -> p h r t", r=2)
            cube = [rows, PK_HEADS, TOPK, TOPK]
            step.done(ve.tensor_tensor(cand[0:rows].rearrange("p (h x y) -> p h x y", x=TOPK, y=TOPK),
                                       pairs[:, :, 0].unsqueeze(3).broadcast_to(cube),
                                       pairs[:, :, 1].unsqueeze(2).broadcast_to(cube), ALU.add))
            best_of(PK_HEADS, sums_of, rest_of, best, besti, rows)
            place = bestf[0:rows, 1]
            whole = bestf[0:rows, 0]
            step.done(ve.tensor_copy(place, besti[0:rows]))
            step.done(ve.tensor_scalar(whole, place, 1.0 / TOPK, -0.5 * (TOPK - 1) / TOPK, ALU.mult, ALU.add))
            step.done(ve.tensor_scalar(whole, whole, ROUND, None, ALU.add))
            step.done(ve.tensor_scalar(whole, whole, -ROUND, None, ALU.add))
            step.done(ve.scalar_tensor_tensor(place, whole, -float(TOPK), place, ALU.mult, ALU.add))
            g = chosen[0:rows, i, 2, :].rearrange("p (h t) -> p h t", t=TOPK)
            ve.tensor_tensor(g, best[0:rows], best[0:rows, :, 0:1].broadcast_to([rows, PK_HEADS, TOPK]), ALU.subtract)\
              .then_inc(gexp_in, 1)
            hit = pick[0:rows].rearrange("p (h t j) -> p h t j", h=PK_HEADS, j=TOPK)
            flat = pick[0:rows].rearrange("p (x j) -> p x j", j=TOPK)
            indices = topf[0:rows].rearrange("p (h r) j -> p h r j", r=2)
            long = [rows, PK_HEADS * TOPK, TOPK]
            for half in range(2):
                step.done(ve.tensor_tensor(flat, bestf[0:rows, half].rearrange("p h t -> p (h t)").unsqueeze(2)
                                           .broadcast_to(long), iota16[0:rows, :].unsqueeze(1).broadcast_to(long),
                                           ALU.is_equal))
                step.done(ve.tensor_tensor(hit, hit, indices[:, :, half].unsqueeze(2).broadcast_to(cube), ALU.mult))
                step.done(ve.tensor_reduce(chosen[0:rows, i, half, :], flat, AX, ALU.add))
        for i in range(TILES):
            rows = ROWS[i]
            ve.wait_ge(gexp_out, 1 + i // (TILES - 1))
            g = chosen[0:rows, i, 2, :].rearrange("p (h t) -> p h t", t=TOPK)
            total = sm["pk"][0:rows, 8:16]
            step.done(ve.tensor_reduce(total, g, AX, ALU.add))
            step.done(ve.reciprocal(total, total))
            step.done(ve.tensor_tensor(g, g, total.unsqueeze(2).broadcast_to([rows, PK_HEADS, TOPK]), ALU.mult))
        ve.sem_inc(chosen_ready, 1)

        ve.wait_ge(chT_copied, TILES)
        step.done(ve.tensor_copy(iota[:, 0:TOPK], iota16[:, :]))
        for k in range(1, NKEYS // TOPK):
            ins = ve.tensor_scalar(iota[:, k * TOPK:(k + 1) * TOPK], iota16[:, :], float(k * TOPK), None, ALU.add)
        step.done(ins)
        with ve.Fori(0, NT // 16) as i:
            for s in range(2):
                ve.wait_ge(c_filled, i * 4 + (2 * s + 2))
                shape = [P, 8, NKEYS]
                ve.tensor_tensor(hot1[:, s], iota[:, :].unsqueeze(1).broadcast_to(shape),
                                 chosenT[:, 0, bass.ds(i * 16 + 8 * s, 8)].unsqueeze(2).broadcast_to(shape), ALU.is_equal)
                for t in range(8):
                    tok = bass.ds(i * 16 + (8 * s + t), 1)
                    ins = ve.tensor_scalar(hot2[:, s, t, :], iota[:, :], chosenT[:, 1, tok], chosenT[:, 2, tok],
                                           ALU.is_equal, ALU.mult)
                ins.then_inc(hot_ready, 1)

        for s in range(2):
            ve.wait_ge(c_store[s], 16 * TBN // 2)
        step.done(ve.memset(acc[:, :, :], 0.0))
        ve.sem_inc(gf_ready, 2)
        ve.sem_inc(acc_added, 2)

        def weigh(e, s, n, c_arrived, ge_arrived=None, gelus=None):
            if ge_arrived is not None:
                ve.wait_ge(ge_in[e], ge_arrived)
            else:
                ve.wait_ge(ge_ready, n + 3 if gelus is None else gelus)
            ve.wait_ge(gh_done, n + 1)
            if e == 0:
                ve.wait_ge(c_in[s], c_arrived)
            ve.tensor_tensor(gf[:, e % 2, :].rearrange("p (b t) -> p b t", t=TB),
                             ge[:, e, :].rearrange("p (b t) -> p b t", t=TB), cg[:, s, :, e, :], ALU.mult)\
              .then_inc(gf_ready, 1)
            ve.wait_ge(gh_done, n + 3)
            ve.tensor_tensor(gL[:, s, e, :], gf[:, e % 2, :], gH[:, s, e, :].bitcast(F32), ALU.subtract)\
              .then_inc(gl_done, 1)
            ve.wait_ge(gl_done, n + 1)

        def add_down(d, m):
            ve.wait_ge(v_done, m + 1)
            part = acc[:, d, :].rearrange("p (c n) -> p c n", c=2)
            ve.tensor_tensor(part, part, halves(4 + 2 * (d % 2)), ALU.add).then_inc(acc_added, 1)

        for e in range(EG):
            weigh(e, 0, e, 16, None, EG * (EARLY - 1) + e + 3)
        for e in range(EG):
            weigh(e, 1, EG + e, 16, 16)
            for d in (2 * e, 2 * e + 1):
                add_down(d, d)
        with ve.Fori(0, EARLY // 2 - 1) as i:
            for s in range(2):
                for e in range(EG):
                    weigh(e, s, i * (2 * EG) + (EG * (s + 2) + e), i * 16 + 32, i * 32 + 16 * (s + 2))
                    for d in (2 * e, 2 * e + 1):
                        add_down(d, i * (2 * KT) + (KT * (s + 1) + d))
        for d in range(KT):
            add_down(d, KT * (EARLY - 1) + d)
        for e in range(EG):
            weigh(e, 0, EG * EARLY + e, 16 * (EARLY // 2 + 1))
        with ve.Fori(0, LATE_PAIRS) as i:
            for s in range(2):
                for e in range(EG):
                    weigh(e, 1 - s, i * (2 * EG) + (EG * (EARLY + s + 1) + e), i * 16 + 16 * (EARLY // 2 + 1 + s))
                for d in range(KT):
                    add_down(d, i * (2 * KT) + (KT * (EARLY + s) + d))
        for e in range(EG):
            weigh(e, 1, EG * (GROUPS - 1) + e, 16 * (GROUPS // 2))
        for m in range(KT * (GROUPS - 2), KT * GROUPS):
            add_down(m % KT, m)

        ve.wait_ge(gain_in, 16 * 5)
        ve.wait_ge(x2_in, 32)
        def add_residual(i):
            rows, at = ROWS[i], 2 * (i % 2) * BANK
            ve.wait_ge(yt2_ready, i + 1)
            ve.tensor_tensor(x2b[0:rows, i, :], x2b[0:rows, i, :], ps[0:rows, at:at + 2 * BANK], ALU.add)\
              .then_inc(res_ready, 1)

        add_residual(0)
        for i in range(TILES):
            rows = ROWS[i]
            if i + 1 < TILES:
                add_residual(i + 1)
            ve.wait_ge(ssq_ready, sums[0] + i + 1)
            rstd = sm["rstd"][0:rows, i:i + 1]
            ve.tensor_scalar(rstd, sm["ssq"][0:rows, i:i + 1], 1.0 / D, RMS_EPS, ALU.mult, ALU.add)\
              .then_inc(var_ready, 1)
            ve.wait_ge(std_ready, 2 + 2 * TILES + i + 1)
            step.done(ve.reciprocal(rstd, rstd))
            ve.scalar_tensor_tensor(yout[0:rows, i % 2, :], x2b[0:rows, i, :], rstd, gain[0:rows, :],
                                    ALU.mult, ALU.mult).then_inc(y_ready, 1)


INPUTS = ["wts", "ident", "x", "mem", "gains", "par", "lamp", "gsub", "ropec", "ropes", "ropen", "mask", "ckT", "cv",
          "cmkT", "cmv", "keysT", "iota"]
OUTPUTS = {"y": (NT, D), "k": (NT, D), "v": (NT, D), "mkT": (D, MEM), "mv": (MEM, D), "cstate": (P, KT, 6),
           "hstate": (P, KT, 2)}


def layout(p):
    p = {name: np.asarray(value) for name, value in p.items()}
    f32 = np.float32

    def pieces(w):
        n = w.shape[1] // CHUNK
        return w.reshape(2, 4, P, n, CHUNK).transpose(3, 0, 2, 1, 4).reshape(2 * n, P, PIECE)

    w_in = p["w_in"][0]
    q, k, v, rx, rg, ga, gr = (w_in[:, c * D:(c + 1) * D] for c in range(7))
    recurrent = np.concatenate([w[:, j * P:(j + 1) * P] for j in range(N_RG) for w in (rx, rg, gr, ga)], axis=1)
    u = p["peer_u"][0].reshape(NKEYS, NKEYS, D)
    u = u.reshape(NKEYS, GROUPS, EG, 2, 4, P).transpose(1, 3, 5, 4, 2, 0).reshape(GROUPS, 2, P, PIECE)
    vt = p["peer_v"][0].reshape(NKEYS, GROUPS, 2, 2, D).transpose(1, 2, 0, 3, 4).reshape(GROUPS, 2, P, PIECE)
    experts = [*u[:EARLY], vt[EARLY - 1], *vt[:EARLY - 1], u[EARLY]]
    for g in range(EARLY + 1, GROUPS):
        experts += [u[g], vt[g - 1]]
    experts.append(vt[GROUPS - 1])
    wts = np.concatenate([pieces(p["w_ck"][0]), pieces(p["w_cv"][0]), pieces(recurrent), pieces(v), pieces(k),
                          pieces(q), pieces(p["w_out"][0]), pieces(p["w_cq"][0]), pieces(p["w_co"][0]),
                          pieces(p["w_pq"][0])] + experts)

    def columns(x):
        return np.moveaxis(x.reshape(x.shape[:-1] + (KT, P)), (-2, -1), (0, 1))

    par = np.zeros((KT, P, PAR_N), f32)
    for at, w in ((0, p["rg_wa"][0]), (P, p["rg_wx"][0])):
        for b in range(2):
            par[:, b * 64:b * 64 + 64, at + b * 64:at + b * 64 + 64] = w[b::2]
    par[:, :, PAR_CW:PAR_CW + CONVW] = columns(p["conv_w"][0])
    for at, name in ((PAR_CB, "conv_b"), (PAR_BA, "rg_ba"), (PAR_BX, "rg_bx")):
        par[:, :, at] = columns(p[name][0])
    par[:, :, PAR_SC:PAR_SC + 3] = columns(p["state_conv"][0, 0])
    par[:, :, PAR_H0] = columns(p["state_rglru"][0, 0])

    lams = np.concatenate([p[n][0] for n in ("lam_q1", "lam_k1", "lam_q2", "lam_k2")])
    lamp = np.concatenate([np.broadcast_to(lams, (P, 4 * DK)), p["rg_lambda"][0].reshape(KT, P).T], axis=1)
    gains = np.stack([p["g_mem"][0], p["g_mix"][0], p["g_cross"][0], p["g_ffn"][0], p["g_final"]])

    inv = np.exp(f32(-math.log(10000.0)) * np.arange(32, dtype=f32) * f32(2.0 / DK)).astype(f32)
    pos = np.arange(TILES * P, dtype=f32)
    ang = (pos[:, None] * inv[None, :]).astype(f32).astype(np.float64)
    rope = {n: np.ascontiguousarray(t.astype(f32).reshape(TILES, P, 32).transpose(1, 0, 2))
            for n, t in (("ropec", np.cos(ang)), ("ropes", np.sin(ang)), ("ropen", -np.sin(ang)))}
    mask = np.zeros((1, P + DK), f32)
    mask[0, 0:DK] = 1.0
    mask[0, P:] = -1e30
    keys = np.stack([p["pk_keys1"][0], p["pk_keys2"][0]], axis=1).reshape(2 * PK_HEADS, NKEYS, P)
    arrays = {
        "wts": wts, "ident": np.eye(P, dtype=f32),
        "x": np.concatenate([p["x_prompt"][0], p["x_sample"][0]]), "mem": p["mem_prompt"][0],
        "gains": np.broadcast_to(gains[:, None, :], (5, P, D)), "par": par, "lamp": lamp,
        "gsub": p["g_subln"][0][:, None], **rope, "mask": mask,
        "ckT": p["cache_attn_k"][0, 0].reshape(PAST, HEADS, P).transpose(1, 2, 0),
        "cv": p["cache_attn_v"][0, 0].reshape(PAST // P, P, D).transpose(1, 0, 2),
        "cmkT": p["cache_mem_k"][0, 0].reshape(MEM, D).T, "cmv": p["cache_mem_v"][0, 0].reshape(MEM, D),
        "keysT": keys.transpose(2, 0, 1), "iota": np.broadcast_to(np.arange(P, dtype=f32), (P, P)),
    }
    return {name: np.ascontiguousarray(arrays[name]) for name in INPUTS}


def kernel(**inputs):
    import concourse.bacc as _bacc
    from concourse.bass_utils import run_bass_kernel_spmd as _run

    arrays = layout(inputs)
    nc = _bacc.Bacc("TRN2", target_bir_lowering=False, num_devices=1)
    a = {name: nc.dram_tensor(name, x.shape, F32, kind="ExternalInput").ap() for name, x in arrays.items()}
    o = {name: nc.dram_tensor(f"out_{name}", shape, F32, kind="ExternalOutput").ap() for name, shape in OUTPUTS.items()}
    with nc.Block() as block:
        encoder_layer(nc, block, a, o)
    r = _run(nc, [arrays], core_ids=[0]).results[0]
    y, k, v, mkT, mv, cs, hs = (np.asarray(r[f"out_{name}"]) for name in OUTPUTS)
    cs = cs.transpose(2, 1, 0).reshape(6, D)
    hs = hs.transpose(2, 1, 0).reshape(2, D)
    n = NP_TOK
    return (y[None, :n], y[None, n:],
            k[:n].reshape(1, 1, n, 2 * HEADS, DK), v[:n].reshape(1, 1, n, HEADS, DV),
            mkT.T.reshape(1, 1, MEM, CA_HEADS, CA_DH), mv.reshape(1, 1, MEM, CA_HEADS, CA_DH),
            cs[None, None, 0:3], hs[None, 0:1],
            k[n:].reshape(1, 1, NS_TOK, 2 * HEADS, DK), v[n:].reshape(1, 1, NS_TOK, HEADS, DV),
            cs[None, None, 3:6], hs[None, 1:2])
```
